# Optimizing a Trainium2 kernel written in Bass

```python
import jax, jax.numpy as jnp
from jax import lax
import numpy as np

D_MODEL = 1024
BATCH = 1
SEQ = 512
DEPTH = 1
DEC_BATCH = 8
DEC_SEQ = 4
PAST_LEN = 1024
PAGE_SIZE = 128

NSA_HEADS = 8
NSA_KV = 2
HEAD_DIM = 64
NSA_GROUP = NSA_HEADS // NSA_KV
NSA_W = NSA_HEADS * HEAD_DIM
CMP_STRIDE = 16
CMP_LEN = 2 * CMP_STRIDE
CMP_HID = 128
SEL_BLK = 64
SEL_TOPK = 16
WINDOW = 512
Q_BLOCK = 64
ROPE_THETA = 500000.0
ROPE_DIM = HEAD_DIM // 4
HG_HEADS = 4
HG_DK = 128
HG_DV = 128
HG_W = HG_HEADS * HG_DV
HG_CHUNK = 32
MIX_W = NSA_W + HG_W
MEM_LEN = 256
CA_HEADS = 4
CA_HD = D_MODEL // CA_HEADS
FFN_HID = -(-8 * D_MODEL // (3 * 256)) * 256
IN_SIZES = [NSA_W, 3 * NSA_HEADS] + [NSA_KV * HEAD_DIM] * 6 + [HG_W] * 4
N_IN = sum(IN_SIZES)
EPS = 1e-6
FORCE_SCORE = 1e4
NEG = -1e30

kernel_name = "hymba_nsa_hgrn2_decoder_step"

def rmsnorm(x, g):
    xf = x.astype(jnp.float32)
    y = xf * lax.rsqrt(jnp.mean(xf * xf, axis=-1, keepdims=True) + EPS)
    return (y * g.astype(jnp.float32)).astype(x.dtype)

def rope(x, pos):
    half = ROPE_DIM // 2
    inv = ROPE_THETA ** (-jnp.arange(half, dtype=jnp.float32) / half)
    ang = pos.astype(jnp.float32)[:, None] * inv[None, :]
    cos = jnp.cos(ang)[:, None, :]
    sin = jnp.sin(ang)[:, None, :]
    xf = x.astype(jnp.float32)
    x1 = xf[..., :half]
    x2 = xf[..., half:ROPE_DIM]
    out = jnp.concatenate([x1 * cos - x2 * sin, x1 * sin + x2 * cos, xf[..., ROPE_DIM:]], axis=-1)
    return out.astype(x.dtype)

def masked_softmax(s, mask, axis=-1):
    s = jnp.where(mask, s.astype(jnp.float32), NEG)
    m = jnp.max(s, axis=axis, keepdims=True)
    e = jnp.where(mask, jnp.exp(s - m), 0.0)
    return e / jnp.maximum(jnp.sum(e, axis=axis, keepdims=True), 1e-20)

def compress(k, pe, w1, w2):
    B, T = k.shape[:2]
    nseg = T // CMP_STRIDE
    seg = k[:, :nseg * CMP_STRIDE].reshape(B, nseg, CMP_STRIDE, NSA_KV, HEAD_DIM)
    seg = seg.transpose(0, 1, 3, 2, 4).reshape(B, nseg, NSA_KV, CMP_STRIDE * HEAD_DIM)
    pe = pe.reshape(2, CMP_STRIDE * HEAD_DIM)
    w1 = w1.reshape(2, CMP_STRIDE * HEAD_DIM, CMP_HID)
    ha = (seg + pe[0]) @ w1[0]
    hb = (seg + pe[1]) @ w1[1]
    h = jax.nn.gelu(ha[:, :-1] + hb[:, 1:])
    kc = h @ w2
    cend = jnp.arange(nseg - 1) * CMP_STRIDE + CMP_LEN - 1
    return kc, cend

def nsa_attend(q, gates, qpos, kc, vc, cend, fetch, nsel, kw, vw, kwpos):
    B, Tq = q.shape[:2]
    scale = HEAD_DIM ** -0.5
    qg = q.reshape(B, Tq, NSA_KV, NSA_GROUP, HEAD_DIM)
    qr = rope(q, qpos).reshape(B, Tq, NSA_KV, NSA_GROUP, HEAD_DIM)
    s = jnp.einsum('btgrd,bngd->bgrtn', qg, kc).astype(jnp.float32) * scale
    p_c = masked_softmax(s, cend[None, :] <= qpos[:, None])
    o_c = jnp.einsum('bgrtn,bngd->btgrd', p_c.astype(vc.dtype), vc)
    nc = kc.shape[1]
    cps = SEL_BLK // CMP_STRIDE
    imp = jnp.sum(p_c, axis=2)
    imp = jnp.pad(imp, ((0, 0), (0, 0), (0, 0), (0, nsel * cps - nc)))
    imp = imp.reshape(B, NSA_KV, Tq, nsel, cps).sum(-1)
    cur = qpos // SEL_BLK
    j = jnp.arange(nsel)
    avail = j[None, :] <= cur[:, None]
    forced = (j[None, :] == 0) | (j[None, :] == cur[:, None]) | (j[None, :] == cur[:, None] - 1)
    score = jnp.where(avail, jnp.where(forced, FORCE_SCORE, imp), -FORCE_SCORE)
    _, idx = lax.top_k(score, min(SEL_TOPK, nsel))
    ks, vs = fetch(idx)
    kpos = idx[..., None] * SEL_BLK + jnp.arange(SEL_BLK)
    smask = (idx <= cur[None, None, :, None])[..., None] & (kpos <= qpos[None, None, :, None, None])
    s = jnp.einsum('btgrd,bgtksd->bgrtks', qr, ks).astype(jnp.float32) * scale
    p_s = masked_softmax(s, smask[:, :, None], axis=(-2, -1))
    o_s = jnp.einsum('bgrtks,bgtksd->btgrd', p_s.astype(vs.dtype), vs)
    wmask = ((kwpos[None, :] <= qpos[:, None]) & (kwpos[None, :] > qpos[:, None] - WINDOW)
             & (kwpos[None, :] >= 0))
    s = jnp.einsum('btgrd,bkgd->bgrtk', qr, kw).astype(jnp.float32) * scale
    p_w = masked_softmax(s, wmask)
    o_w = jnp.einsum('bgrtk,bkgd->btgrd', p_w.astype(vw.dtype), vw)
    g = jax.nn.sigmoid(gates.astype(jnp.float32)).reshape(B, Tq, NSA_KV, NSA_GROUP, 3, 1)
    o = g[..., 0, :] * o_c + g[..., 1, :] * o_s + g[..., 2, :] * o_w
    return o.reshape(B, Tq, NSA_W).astype(q.dtype)

def nsa_prompt(q, gates, kcn, vcn, ksn, vsn, kwn, vwn, pe_k, w1_k, w2_k, pe_v, w1_v, w2_v):
    B, T = q.shape[:2]
    kc, cend = compress(kcn, pe_k, w1_k, w2_k)
    vc, _ = compress(vcn, pe_v, w1_v, w2_v)
    nsel = -(-T // SEL_BLK)
    padn = nsel * SEL_BLK - T
    ksr = jnp.pad(ksn, ((0, 0), (0, padn), (0, 0), (0, 0))).reshape(B, nsel, SEL_BLK, NSA_KV, HEAD_DIM)
    vsr = jnp.pad(vsn, ((0, 0), (0, padn), (0, 0), (0, 0))).reshape(B, nsel, SEL_BLK, NSA_KV, HEAD_DIM)
    bi = jnp.arange(B)[:, None, None, None]
    gi = jnp.arange(NSA_KV)[None, :, None, None]

    def fetch(idx):
        return ksr[bi, idx, :, gi], vsr[bi, idx, :, gi]

    kw_pad = jnp.pad(kwn, ((0, 0), (WINDOW, 0), (0, 0), (0, 0)))
    vw_pad = jnp.pad(vwn, ((0, 0), (WINDOW, 0), (0, 0), (0, 0)))

    def block(i):
        s0 = i * Q_BLOCK
        qpos = s0 + jnp.arange(Q_BLOCK)
        qb = lax.dynamic_slice_in_dim(q, s0, Q_BLOCK, 1)
        gb = lax.dynamic_slice_in_dim(gates, s0, Q_BLOCK, 1)
        kwb = lax.dynamic_slice_in_dim(kw_pad, s0, WINDOW + Q_BLOCK, 1)
        vwb = lax.dynamic_slice_in_dim(vw_pad, s0, WINDOW + Q_BLOCK, 1)
        kwpos = s0 - WINDOW + jnp.arange(WINDOW + Q_BLOCK)
        return nsa_attend(qb, gb, qpos, kc, vc, cend, fetch, nsel, kwb, vwb, kwpos)

    o = lax.map(block, jnp.arange(T // Q_BLOCK))
    return o.transpose(1, 0, 2, 3).reshape(B, T, NSA_W)

def nsa_sample(q, gates, kcn, vcn, ksn, vsn, kwn, vwn, pos, pool_ck, pool_cv, pool_sk, pool_sv,
               win_k, win_v, page_table, pe_k, w1_k, w2_k, pe_v, w1_v, w2_v):
    DB, TS = q.shape[:2]
    n_pages = page_table.shape[1]
    past = n_pages * PAGE_SIZE
    kc_all = jnp.concatenate([pool_ck[page_table].reshape(DB, past, NSA_KV, HEAD_DIM), kcn], axis=1)
    vc_all = jnp.concatenate([pool_cv[page_table].reshape(DB, past, NSA_KV, HEAD_DIM), vcn], axis=1)
    kc, cend = compress(kc_all, pe_k, w1_k, w2_k)
    vc, _ = compress(vc_all, pe_v, w1_v, w2_v)
    nsel = -(-(past + TS) // SEL_BLK)
    bpp = PAGE_SIZE // SEL_BLK
    npb = past // SEL_BLK
    n_new = -(-TS // SEL_BLK)
    padn = n_new * SEL_BLK - TS
    new_k = jnp.pad(ksn, ((0, 0), (0, padn), (0, 0), (0, 0))).reshape(DB, n_new, SEL_BLK, NSA_KV, HEAD_DIM)
    new_v = jnp.pad(vsn, ((0, 0), (0, padn), (0, 0), (0, 0))).reshape(DB, n_new, SEL_BLK, NSA_KV, HEAD_DIM)
    pool_kb = pool_sk.reshape(-1, SEL_BLK, NSA_KV, HEAD_DIM)
    pool_vb = pool_sv.reshape(-1, SEL_BLK, NSA_KV, HEAD_DIM)
    bi = jnp.arange(DB)[:, None, None, None]
    gi = jnp.arange(NSA_KV)[None, :, None, None]

    def fetch(idx):
        jp = jnp.minimum(idx, npb - 1)
        phys = page_table[bi, jp // bpp] * bpp + jp % bpp
        jn = jnp.clip(idx - npb, 0, n_new - 1)
        is_past = (idx < npb)[..., None, None]
        k = jnp.where(is_past, pool_kb[phys, :, gi], new_k[bi, jn, :, gi])
        v = jnp.where(is_past, pool_vb[phys, :, gi], new_v[bi, jn, :, gi])
        return k, v

    wb = win_k.shape[1]
    kw = jnp.concatenate([win_k, kwn], axis=1)
    vw = jnp.concatenate([win_v, vwn], axis=1)
    kwpos = past - wb + jnp.arange(wb + TS)
    o = nsa_attend(q, gates, pos, kc, vc, cend, fetch, nsel, kw, vw, kwpos)
    return o, kw[:, -wb:], vw[:, -wb:]

def hgrn2_scan(q, log_f, k, v, S0):
    B, T = q.shape[:2]
    Tp = -(-T // HG_CHUNK) * HG_CHUNK
    padn = Tp - T

    def to_chunks(a):
        a = jnp.pad(a, ((0, 0), (0, padn), (0, 0), (0, 0)))
        return a.reshape(B, Tp // HG_CHUNK, HG_CHUNK, HG_HEADS, -1).transpose(1, 0, 3, 2, 4)

    mask = jnp.tril(jnp.ones((HG_CHUNK, HG_CHUNK), dtype=bool))[:, :, None]

    def step(S, inp):
        qc, lfc, kc, vc = inp
        b = jnp.cumsum(lfc, axis=2)
        o_inter = jnp.einsum('bhtd,bhde->bhte', qc * jnp.exp(b), S)
        diff = b[:, :, :, None, :] - b[:, :, None, :, :]
        decay = jnp.exp(jnp.where(mask, diff, -jnp.inf))
        A = jnp.einsum('bhtd,bhsd,bhtsd->bhts', qc, kc, decay)
        o = o_inter + jnp.einsum('bhts,bhse->bhte', A, vc)
        bl = b[:, :, -1:, :]
        S = jnp.exp(bl[:, :, 0, :])[..., None] * S + jnp.einsum('bhsd,bhse->bhde', kc * jnp.exp(bl - b), vc)
        return S, o

    S, o = lax.scan(step, S0, (to_chunks(q), to_chunks(log_f), to_chunks(k), to_chunks(v)))
    o = o.transpose(1, 0, 3, 2, 4).reshape(B, Tp, HG_HEADS, HG_DV)[:, :T]
    return o, S

def hgrn2_mix(hq, hf, hi, hg, lb, out_g, S0):
    B, T = hq.shape[:2]
    q = hq.reshape(B, T, HG_HEADS, HG_DK).astype(jnp.float32)
    z = hf.reshape(B, T, HG_HEADS, HG_DK).astype(jnp.float32)
    log_f = jnp.log(lb + (1.0 - lb) * jax.nn.sigmoid(z))
    k = (1.0 - lb) * jax.nn.sigmoid(-z)
    v = hi.reshape(B, T, HG_HEADS, HG_DV).astype(jnp.float32)
    o, S = hgrn2_scan(q, log_f, k, v, S0)
    o = rmsnorm(o, out_g.reshape(HG_HEADS, HG_DV))
    o = o * jax.nn.silu(hg.astype(jnp.float32).reshape(B, T, HG_HEADS, HG_DV))
    return o.reshape(B, T, HG_W).astype(hq.dtype), S

def cross_attn(h, mk, mv, wq, wo):
    B, T = h.shape[:2]
    q = (h @ wq).reshape(B, T, CA_HEADS, CA_HD)
    s = jnp.einsum('bthd,bmhd->bhtm', q, mk).astype(jnp.float32) * CA_HD ** -0.5
    p = jax.nn.softmax(s, axis=-1)
    o = jnp.einsum('bhtm,bmhd->bthd', p.astype(mv.dtype), mv).reshape(B, T, CA_HEADS * CA_HD)
    return o @ wo

def swiglu(h, wg, wu, wd):
    return (jax.nn.silu(h @ wg) * (h @ wu)) @ wd

def split_proj(h, w_in):
    offs = [int(o) for o in np.cumsum(IN_SIZES)[:-1]]
    return jnp.split(h @ w_in, offs, axis=-1)

def setup_inputs(seed: int = 0) -> dict:
    key = jax.random.key(seed)
    ks = iter(jax.random.split(key, 48))
    nrm = lambda shape, s=1.0: jax.random.normal(next(ks), shape, jnp.float32) * s
    w = lambda shape, fan_in: nrm(shape, fan_in ** -0.5)
    gain = lambda shape: 1.0 + nrm(shape, 0.05)
    n_pages = PAST_LEN // PAGE_SIZE
    n_pool = (DEC_BATCH * n_pages * 5) // 4
    wb = min(WINDOW, PAST_LEN)
    pool = (DEPTH, n_pool, PAGE_SIZE, NSA_KV, HEAD_DIM)
    page_table = jax.random.permutation(next(ks), n_pool)[:DEC_BATCH * n_pages]
    page_table = page_table.reshape(DEC_BATCH, n_pages).astype(jnp.int32)
    return {
        "x_prompt": nrm((BATCH, SEQ, D_MODEL)),
        "x_sample": nrm((DEC_BATCH, DEC_SEQ, D_MODEL)),
        "cache_cmp_k": nrm(pool),
        "cache_cmp_v": nrm(pool),
        "cache_sel_k": nrm(pool),
        "cache_sel_v": nrm(pool),
        "cache_win_k": nrm((DEPTH, DEC_BATCH, wb, NSA_KV, HEAD_DIM)),
        "cache_win_v": nrm((DEPTH, DEC_BATCH, wb, NSA_KV, HEAD_DIM)),
        "state_hgrn": nrm((DEPTH, DEC_BATCH, HG_HEADS, HG_DK, HG_DV), 0.5),
        "cache_mem_k": nrm((DEPTH, DEC_BATCH, MEM_LEN, CA_HEADS, CA_HD)),
        "cache_mem_v": nrm((DEPTH, DEC_BATCH, MEM_LEN, CA_HEADS, CA_HD)),
        "page_table": page_table,
        "mem_prompt": nrm((BATCH, MEM_LEN, D_MODEL)),
        "norm_mix": gain((DEPTH, D_MODEL)),
        "w_in": w((DEPTH, D_MODEL, N_IN), D_MODEL),
        "cmp_pe_k": nrm((DEPTH, CMP_LEN, HEAD_DIM), 0.1),
        "cmp_w1_k": w((DEPTH, CMP_LEN * HEAD_DIM, CMP_HID), CMP_LEN * HEAD_DIM),
        "cmp_w2_k": w((DEPTH, CMP_HID, HEAD_DIM), CMP_HID),
        "cmp_pe_v": nrm((DEPTH, CMP_LEN, HEAD_DIM), 0.1),
        "cmp_w1_v": w((DEPTH, CMP_LEN * HEAD_DIM, CMP_HID), CMP_LEN * HEAD_DIM),
        "cmp_w2_v": w((DEPTH, CMP_HID, HEAD_DIM), CMP_HID),
        "nsa_out_norm": gain((DEPTH, NSA_W)),
        "hg_lb_logits": nrm((DEPTH + 1, HG_HEADS * HG_DK), 0.5),
        "hg_out_norm": gain((DEPTH, HG_W)),
        "w_out": w((DEPTH, MIX_W, D_MODEL), MIX_W),
        "norm_ca": gain((DEPTH, D_MODEL)),
        "norm_mem": gain((DEPTH, D_MODEL)),
        "ca_wq": w((DEPTH, D_MODEL, CA_HEADS * CA_HD), D_MODEL),
        "ca_wk": w((DEPTH, D_MODEL, CA_HEADS * CA_HD), D_MODEL),
        "ca_wv": w((DEPTH, D_MODEL, CA_HEADS * CA_HD), D_MODEL),
        "ca_wo": w((DEPTH, CA_HEADS * CA_HD, D_MODEL), CA_HEADS * CA_HD),
        "norm_ffn": gain((DEPTH, D_MODEL)),
        "ffn_w_gate": w((DEPTH, D_MODEL, FFN_HID), D_MODEL),
        "ffn_w_up": w((DEPTH, D_MODEL, FFN_HID), D_MODEL),
        "ffn_w_down": w((DEPTH, FFN_HID, D_MODEL), FFN_HID),
        "final_norm": gain((D_MODEL,)),
    }

def reference(x_prompt, x_sample, cache_cmp_k, cache_cmp_v, cache_sel_k, cache_sel_v, cache_win_k, cache_win_v,
              state_hgrn, cache_mem_k, cache_mem_v, page_table, mem_prompt, norm_mix, w_in, cmp_pe_k, cmp_w1_k,
              cmp_w2_k, cmp_pe_v, cmp_w1_v, cmp_w2_v, nsa_out_norm, hg_lb_logits, hg_out_norm, w_out, norm_ca,
              norm_mem, ca_wq, ca_wk, ca_wv, ca_wo, norm_ffn, ffn_w_gate, ffn_w_up, ffn_w_down, final_norm):
    B, T = x_prompt.shape[:2]
    DB, TS = x_sample.shape[:2]
    past = page_table.shape[1] * PAGE_SIZE
    pos_p = jnp.arange(T)
    pos_s = past + jnp.arange(TS)
    lb_all = jnp.cumsum(jax.nn.softmax(hg_lb_logits.astype(jnp.float32), axis=0), axis=0)
    kvs = lambda a, n: a.reshape(a.shape[0], n, NSA_KV, HEAD_DIM)
    xp, xs = x_prompt, x_sample
    P = {n: [] for n in ['ck', 'cv', 'sk', 'sv', 'wk', 'wv', 'hg', 'mk', 'mv']}
    S = {n: [] for n in ['ck', 'cv', 'sk', 'sv', 'wk', 'wv', 'hg']}
    for l in range(DEPTH):
        lb = lb_all[l].reshape(HG_HEADS, HG_DK)
        cmpw = (cmp_pe_k[l], cmp_w1_k[l], cmp_w2_k[l], cmp_pe_v[l], cmp_w1_v[l], cmp_w2_v[l])
        qp, gp, kcp, vcp, ksp, vsp, kwp, vwp, hqp, hfp, hip, hgp = split_proj(rmsnorm(xp, norm_mix[l]), w_in[l])
        kcp, vcp, vsp, vwp = kvs(kcp, T), kvs(vcp, T), kvs(vsp, T), kvs(vwp, T)
        ksp = rope(kvs(ksp, T), pos_p)
        kwp = rope(kvs(kwp, T), pos_p)
        o_nsa = nsa_prompt(qp.reshape(B, T, NSA_HEADS, HEAD_DIM), gp.reshape(B, T, NSA_HEADS, 3),
                           kcp, vcp, ksp, vsp, kwp, vwp, *cmpw)
        o_hg, S_p = hgrn2_mix(hqp, hfp, hip, hgp, lb, hg_out_norm[l],
                              jnp.zeros((B, HG_HEADS, HG_DK, HG_DV), jnp.float32))
        xp = xp + jnp.concatenate([rmsnorm(o_nsa, nsa_out_norm[l]), o_hg], axis=-1) @ w_out[l]
        mn = rmsnorm(mem_prompt, norm_mem[l])
        mk = (mn @ ca_wk[l]).reshape(B, MEM_LEN, CA_HEADS, CA_HD)
        mv = (mn @ ca_wv[l]).reshape(B, MEM_LEN, CA_HEADS, CA_HD)
        xp = xp + cross_attn(rmsnorm(xp, norm_ca[l]), mk, mv, ca_wq[l], ca_wo[l])
        xp = xp + swiglu(rmsnorm(xp, norm_ffn[l]), ffn_w_gate[l], ffn_w_up[l], ffn_w_down[l])
        wbp = min(WINDOW, T)
        for n, a in zip(['ck', 'cv', 'sk', 'sv', 'wk', 'wv', 'hg', 'mk', 'mv'],
                        [kcp, vcp, ksp, vsp, kwp[:, -wbp:], vwp[:, -wbp:], S_p.astype(state_hgrn.dtype), mk, mv]):
            P[n].append(a)
        qs, gs, kcs, vcs, kss, vss, kws, vws, hqs, hfs, his, hgs = split_proj(rmsnorm(xs, norm_mix[l]), w_in[l])
        kcs, vcs, vss, vws = kvs(kcs, TS), kvs(vcs, TS), kvs(vss, TS), kvs(vws, TS)
        kss = rope(kvs(kss, TS), pos_s)
        kws = rope(kvs(kws, TS), pos_s)
        o_nsa_s, nwk, nwv = nsa_sample(qs.reshape(DB, TS, NSA_HEADS, HEAD_DIM), gs.reshape(DB, TS, NSA_HEADS, 3),
                                       kcs, vcs, kss, vss, kws, vws, pos_s, cache_cmp_k[l], cache_cmp_v[l],
                                       cache_sel_k[l], cache_sel_v[l], cache_win_k[l], cache_win_v[l],
                                       page_table, *cmpw)
        o_hg_s, S_s = hgrn2_mix(hqs, hfs, his, hgs, lb, hg_out_norm[l], state_hgrn[l].astype(jnp.float32))
        xs = xs + jnp.concatenate([rmsnorm(o_nsa_s, nsa_out_norm[l]), o_hg_s], axis=-1) @ w_out[l]
        xs = xs + cross_attn(rmsnorm(xs, norm_ca[l]), cache_mem_k[l], cache_mem_v[l], ca_wq[l], ca_wo[l])
        xs = xs + swiglu(rmsnorm(xs, norm_ffn[l]), ffn_w_gate[l], ffn_w_up[l], ffn_w_down[l])
        for n, a in zip(['ck', 'cv', 'sk', 'sv', 'wk', 'wv', 'hg'],
                        [kcs, vcs, kss, vss, nwk, nwv, S_s.astype(state_hgrn.dtype)]):
            S[n].append(a)
    y_prompt = rmsnorm(xp, final_norm)
    y_sample = rmsnorm(xs, final_norm)
    st = lambda lst: jnp.stack(lst, axis=0)
    return (y_prompt, y_sample,
            st(P['ck']), st(P['cv']), st(P['sk']), st(P['sv']), st(P['wk']), st(P['wv']), st(P['hg']),
            st(P['mk']), st(P['mv']),
            st(S['ck']), st(S['cv']), st(S['sk']), st(S['sv']), st(S['wk']), st(S['wv']), st(S['hg']))


_drawn_inputs = setup_inputs


def setup_inputs(seed=0):
    import zlib

    import numpy as np

    out = dict(_drawn_inputs(seed))
    spreads = {}
    factors = {'cmp_pe_k': 4.995, 'hg_out_norm': 3.064, 'norm_ca': 8.0, 'norm_ffn': 2.751}
    for name, (base, spread) in spreads.items():
        noise = np.random.default_rng([zlib.crc32(name.encode()), seed]).standard_normal(out[name].shape)
        drawn = base * np.exp(spread * noise) if base else spread * noise
        out[name] = __import__('jax').numpy.asarray(drawn.astype(out[name].dtype))
    for name, factor in factors.items():
        out[name] = (out[name] * factor).astype(out[name].dtype)
    return out
```

```python
from contextlib import ExitStack

import numpy as np
import concourse.bass as bass
from concourse import mybir

F32 = mybir.dt.float32
I32 = mybir.dt.int32
ALU = mybir.AluOpType
ACT = mybir.ActivationFunctionType
AX = mybir.AxisListType.X

P = 128
DM = 1024
KT = DM // P
SEQ = 512
DB, DS = 8, 4
NSMP = DB * DS
TOK = SEQ + NSMP
HALF = TOK // 2
QT = SEQ // P
PAST, PAGE = 1024, 128
NPAGE = PAST // PAGE
PROWS = P // NPAGE
NH, NG, HD = 8, 2, 64
NR = NH // NG
GW = NG * HD
NSAW = NH * HD
STR = 16
SELB = 64
WIN = 512
CHID = 128
HH, HK = 4, 128
MEM = 256
CH, CD = 4, 256
FFN = 2816
FT = FFN // P
EPS = 1e-6
NEG = -1e30
SCALE = HD ** -0.5
CSCALE = CD ** -0.5
CSEG = PAST // STR
NCB = CSEG - 1
PSEG = SEQ // STR
NPB = PSEG - 1
C_Q, C_G, C_CK, C_SK, C_WK, C_HQ, C_HF, C_HI, C_HG = 0, 512, 536, 792, 1048, 1304, 1816, 2328, 2840
LEVELS = [0, 1, 2, 4, 8, 16, 32, 64]
WRING, WSLOT = 4, KT * 256
ARENA = 27700
RAWS, XKS = 4, 2
ROWV = 88
V_MIX, V_CA, V_MEM, V_FFN, V_FIN, V_NSA, V_HG, V_LB, V_PEK, V_PEV = 0, 8, 16, 24, 32, 40, 44, 48, 56, 72


def constants():
    f = np.float32
    rows = np.arange(P)
    parts = {}
    parts["ident"] = np.eye(P)
    parts["causal"] = np.where(rows[None, :] <= rows[:, None], 0.0, NEG)
    t = np.arange(QT)[None, :, None] * P + rows[:, None, None]
    ok = (np.arange(NPB) * STR + 2 * STR - 1)[None, None, :] <= t
    parts["cadd"] = np.where(ok, 0.0, NEG).reshape(P, -1)
    parts["cmul"] = ok.astype(f).reshape(P, -1)
    s, u = rows[:, None], rows[None, :]

    def level(s, u, L):
        if L == 0:
            return s == u
        return (s // (2 * L) == u // (2 * L)) & (s % (2 * L) < L) & (u % (2 * L) >= L)
    parts["hmask"] = np.concatenate([level(s, u[:, rows % (2 * L) >= L] if L else u, L) for L in LEVELS], 1)
    reset = np.ones(TOK)
    reset[0:SEQ:P] = 0
    reset[SEQ::DS] = 0
    parts["reset"] = np.tile(reset, (P, 1))
    pos = np.concatenate([np.arange(SEQ), PAST + np.tile(np.arange(DS), 32)]).reshape(QT + 1, P).T
    inv = f(500000.0) ** (-np.arange(8, dtype=f) / f(8))
    ang = pos.astype(f)[:, :, None] * inv
    parts["rope"] = np.concatenate([np.cos(ang), np.sin(ang)], -1).reshape(P, -1)
    b4, t4 = rows // 32, rows % 4
    kb, kt = np.arange(NSMP) // DS, np.arange(NSMP) % DS
    for r in range(2):
        new = (kb[None, :] == 4 * r + b4[:, None]) & (kt[None, :] <= t4[:, None])
        parts[f"snew{r}"] = np.where(new, 0.0, NEG)
    parts["swin"] = np.where(np.arange(4)[None, :] > t4[:, None], 0.0, NEG)
    grp = b4 * 8 + (rows % 32 // 16) * 4 + t4
    parts["gsum"] = grp[:, None] == grp[None, :]
    parts["jidx"] = np.tile(np.arange(16), (P, 1))
    parts["isg"] = np.stack([rows % 32 // 16 == 0, rows % 32 // 16 == 1], 1)
    parts["page_row"] = rows[:, None] % PROWS
    parts["bsel"] = (rows[:, None] // DS == np.arange(DB)[None, :])
    at, cols = {}, []
    n = 0
    for k, v in parts.items():
        at[k] = (n, v.shape[1])
        n += v.shape[1]
        cols.append(v.astype(f))
    return at, np.ascontiguousarray(np.concatenate(cols, 1), dtype=f)


def plan():
    ring, last, chunks = [], {}, []

    def item(*n):
        ring.append(n)

    def chunk(*n):
        chunks.append(n)

    def used(*n):
        last[n] = len(ring) - 1
    item("vec")
    for k in range(KT):
        item("xT", k)
    item("sum", 0)
    for c in ("cmp", "sel", "win", "gate", "q0", "q1"):
        chunk(c)
        item(c, "p")
        if c != "gate":
            item(c, "s")
        used(c)
    for s in range(2):
        item("kT", s)
    for rot in range(2):
        for r in range(NR):
            item("qT", rot, r)
    seqs = [(g, j) for g in range(2) for j in range(4)] + [(2, 0)]
    for kv in range(2):
        chunk("w1", kv)
        item("pe", kv)
        for n in range(len(seqs)):
            item("xk", kv, n)
            if n in (6, 8):
                item("kvc", kv, 0 if n == 6 else 1)
        item("kvc", kv, 2)
        used("w1", kv)
    item("pcs")
    heads = [(i, g, r) for i in range(QT) for g in range(NG) for r in range(NR)]
    item("S", 0)
    item("S", 1)
    for n in range(len(heads)):
        if n % 8 == 0:
            item("PTc", n // 8)
        item("PT", n)
        if n + 2 < len(heads):
            item("S", n + 2)
    for rd in range(2):
        item("sms", rd)
        item("imp", rd)
        for b in range(4):
            item("skT", rd, b)
        for b in range(4):
            item("wkT", rd, b)
        item("sPT", rd, 0)
        item("sPT", rd, 1)
    for f in range(4):
        item("nT", f)
    for c in ("hi0", "hi1"):
        chunk(c)
        item(c, "p")
        item(c, "s")
        used(c)
    for c in ("hf", "hq", "hg"):
        for n in range(2):
            chunk(c, n)
            item(c, 2 * n)
            item(c, 2 * n + 1)
            used(c, n)
    for h in range(HH):
        for n in ("klT", "dS", "dSs"):
            item(n, h)
        for L in range(len(LEVELS)):
            item("A", h, L)
        item("o", h)
        item("osum", h)
    for n in range(4):
        chunk("wout", n)
        item("wout", 2 * n)
        item("wout", 2 * n + 1)
        used("wout", n)
    for n in range(2):
        item("mT", n)
    item("msum")
    for c in ("wk", "wv"):
        for n in range(4):
            chunk(c, n)
            item(c, n)
            used(c, n)
    for n in range(2):
        item("mkT", n)
    item("sum", 1)
    for n in range(4):
        chunk("wq", n)
        item("wq", 2 * n)
        item("wq", 2 * n + 1)
        used("wq", n)
    for i in range(QT):
        item("cS", i)
        item("cPT", i)
        item("cO", i)
    for b in range(DB):
        for n in range(2):
            item("cx", b, n)
    item("csPT")
    for n in range(4):
        chunk("wo", n)
        item("wo", 2 * n)
        item("wo", 2 * n + 1)
        used("wo", n)
    item("sum", 2)
    for n in range(FT // 2):
        chunk("ffg", n)
        chunk("ffu", n)
        for m in range(2):
            item("ffg", 2 * n + m)
            if m == 1:
                used("ffg", n)
            item("ffu", 2 * n + m)
        used("ffu", n)
    for n in range(4):
        item("ffd", 2 * n)
        item("ffd", 2 * n + 1)
        for k in range(3):
            chunk("ffd", n, k)
            used("ffd", n, k)
    item("sum", 3)
    for tt in range(QT + 1):
        item("y", tt)
    hold = [("h", kv, g) for kv in range(2) for g in range(3)] + [("o", i, g) for i in range(QT) for g in range(NG)]
    for rd in range(2):
        hold += [("Ss", rd), ("Sw", rd), ("PV", rd)]
    hold += [("cS",), ("cO",)]
    raws = [("c", kv, n) for kv in range(2) for n in range(len(seqs))]
    for rd in range(2):
        raws += [(k, rd, b) for k in ("sk", "wk", "sv", "wv") for b in range(4)]
    return ({n: i for i, n in enumerate(ring)}, {n: i for i, n in enumerate(hold)}, last,
            {n: i for i, n in enumerate(chunks)}, {n: i for i, n in enumerate(raws)}, seqs, heads)


def bc(ap, axis, n):
    ap = ap.unsqueeze(axis)
    shape = list(ap.shape)
    shape[axis] = n
    return ap.broadcast_to(shape)


def build(nc, a, out, cat):
    ring, hold, chunk_last, chunks, raws, seqs, heads = plan()
    ctx = ExitStack()
    with ctx:
        sems = {}

        def sem(name):
            if name not in sems:
                sems[name] = ctx.enter_context(nc.semaphore(name))
            return sems[name]

        def sb(name, cols):
            return ctx.enter_context(nc.sbuf_tensor(name, [P, cols], F32))

        RS = [ctx.enter_context(nc.psum_tensor(f"ring{k}", [P, 1024], F32)) for k in range(3)]
        HOLD = ctx.enter_context(nc.psum_tensor("hold", [P, 1024], F32))
        psum_full = sem("psum_full")
        psum_free = [sem(f"psum_free{k}") for k in range(3)]
        hold_full, hold_free = sem("hold_full"), sem("hold_free")

        X = sb("x_res", KT * TOK)[:, :].rearrange("p (k t) -> p k t", k=KT)
        H = sb("h_norm", KT * TOK)[:, :].rearrange("p (k t) -> p k t", k=KT)
        MX = sb("mix", KT * TOK)[:, :].rearrange("p (k t) -> p k t", k=KT)
        W = sb("w_ring", WRING * WSLOT)[:, :].rearrange("p (s n) -> p s n", s=WRING)
        CST = sb("cst", sum(n for _, n in cat.values()))
        GV = sb("vectors", ROWV)
        ones = sb("ones", P)
        small = sb("small", 512)
        PGID = ctx.enter_context(nc.sbuf_tensor("page_of_partition", [P, DB], I32))
        PGROW = ctx.enter_context(nc.sbuf_tensor("page_rows", [P, DB], I32))
        RSTD = sb("rstd", TOK)
        MEAN = sb("mean_square", TOK)

        def cst(name):
            at, n = cat[name]
            return CST[:, at:at + n]
        ident = cst("ident")

        A = sb("arena", ARENA)
        top = {}

        def take(phase, n, first=None):
            at = top.get(phase, 0) if first is None else first
            top[phase] = at + n
            assert top[phase] <= ARENA, (phase, top[phase])
            return A[:, at:at + n]
        XST = take("x", 5 * DM).rearrange("p (t n) -> p t n", t=5)
        VECS = take("x", P)
        top["nsa"] = 0
        qT = take("nsa", NR * TOK).rearrange("p (r t) -> p r t", r=NR)
        qrT = take("nsa", NR * TOK).rearrange("p (r t) -> p r t", r=NR)
        kT = take("nsa", 2 * TOK).rearrange("p (s t) -> p s t", s=2)
        vtok = take("nsa", 5 * 2 * GW).rearrange("p (t s d) -> p t s d", t=5, s=2)
        qbd = take("nsa", 512).rearrange("p (k n) -> p k n", k=2)
        gates = take("nsa", 5 * 24).rearrange("p (t n) -> p t n", t=5)
        gsmp = take("nsa", 6).rearrange("p (r n) -> p r n", r=2)
        DEN = take("nsa", 4 * 24).rearrange("p (i n) -> p i n", i=4)
        RAW = take("nsa", RAWS * 1024).rearrange("p (s n) -> p s n", s=RAWS)
        XK = take("nsa", XKS * 1024).rearrange("p (s n) -> p s n", s=XKS)
        HX = take("nsa", 2 * 504).rearrange("p (s n) -> p s n", s=2)
        HT = take("nsa", 504)
        kcT = take("nsa", 9 * NCB).rearrange("p (b n) -> p b n", b=9)
        vc = take("nsa", 9 * GW).rearrange("p (b n) -> p b n", b=9)
        w2 = take("nsa", 2 * HD).rearrange("p (k n) -> p k n", k=2)
        otok = take("nsa", 5 * NSAW).rearrange("p (t n) -> p t n", t=5)
        T0 = top["nsa"]
        qtok = take("nsa", 5 * NSAW, T0).rearrange("p (t n) -> p t n", t=5)
        ckcv = take("nsa", 5 * 256).rearrange("p (t n) -> p t n", t=5)
        ksw = take("nsa", 5 * 256).rearrange("p (t s d) -> p t s d", t=5, s=2)
        rtmp = [take("nsa", 320) for _ in range(4)]
        Pb = take("nsa", 2 * 1024, T0).rearrange("p (s n) -> p s n", s=2)
        PTb = take("nsa", 2 * 1024).rearrange("p (s n) -> p s n", s=2)
        cP = take("nsa", 992)
        PTc = take("nsa", 2 * 1024).rearrange("p (s n) -> p s n", s=2)
        osum = take("nsa", 768)
        sS = take("nsa", 1056, T0)
        wS = take("nsa", 544)
        cS = take("nsa", 64)
        cPn = take("nsa", 64)
        sPT = take("nsa", 1024)
        mPT = take("nsa", 896)
        oacc = take("nsa", 384 + 128 + 64)
        hi = take("hg", 5 * 512).rearrange("p (t n) -> p t n", t=5)
        hB, hK, hQ, hG = [take("hg", HH * TOK).rearrange("p (h t) -> p h t", h=HH) for _ in range(4)]
        E0, qdec, kdec, gtmp = [take("hg", TOK) for _ in range(4)]
        LD, LE, LQ, LK = [take("hg", 2 * TOK).rearrange("p (s t) -> p s t", s=2) for _ in range(4)]
        kltok = take("hg", 640).rearrange("p (c n) -> p c n", c=5)
        Sst = take("hg", 4 * HK).rearrange("p (c n) -> p c n", c=4)
        S0 = take("hg", 2 * 1024).rearrange("p (s n) -> p s n", s=2)
        Snew = take("hg", 1024)
        Vbd = take("hg", 1024)
        Aacc, Atmp = take("hg", TOK), take("hg", TOK)
        mst = take("ca", 2048).rearrange("p (m n) -> p m n", m=2)
        mnT = take("ca", 2048).rearrange("p (k n) -> p k n", k=KT)
        mkT = take("ca", 2048).rearrange("p (k n) -> p k n", k=KT)
        mv = take("ca", 2048).rearrange("p (m n) -> p m n", m=2)
        QC = take("ca", KT * TOK).rearrange("p (k t) -> p k t", k=KT)
        xP, xPT = [take("ca", 2048).rearrange("p (s n) -> p s n", s=2) for _ in range(2)]
        qbc = take("ca", 2048).rearrange("p (k b n) -> p k b n", k=KT, b=DB)
        RC = take("ca", 3 * 2048).rearrange("p (s n) -> p s n", s=3)
        KX = take("ca", 2048).rearrange("p (s n) -> p s n", s=2)
        yP = take("ca", 256)
        yPT = take("ca", 256)
        hid = take("ffn", FT * TOK).rearrange("p (k t) -> p k t", k=FT)
        ftmp = take("ffn", 2 * TOK).rearrange("p (s t) -> p s t", s=2)
        ymid = take("ffn", 2 * 1024).rearrange("p (s n) -> p s n", s=2)
        cb, smx, snm = small[:, 0:2], small[:, 2:6], small[:, 6:10]
        pmx = small[:, 16:48]
        rc12 = small[:, 48:60]
        smx1, snm1, sden, coef = small[:, 60:64], small[:, 64:68], small[:, 68:72], small[:, 72:76]
        imp, drop, eqj, mn = small[:, 80:96], small[:, 96:112], small[:, 112:128], small[:, 128:130]
        ss, rs5, sm5, t5 = small[:, 130:135], small[:, 136:141], small[:, 192:197], small[:, 198:203]
        lb, lbn, lb1 = small[:, 144:148], small[:, 148:152], small[:, 152:156]
        xmx, xnm, xden = small[:, 160:168], small[:, 168:176], small[:, 176:184]
        msc = small[:, 184:186]
        epsb = small[:, 190:191]

        scr_g = nc.dram_tensor("scr_gates", (NSMP, 24), F32, kind="Internal").ap()
        scr_o = nc.dram_tensor("scr_o", (NSMP, NSAW), F32, kind="Internal").ap()

        def wsl(name):
            n = chunks[name]
            return W[:, n % WRING, :], wload[n % WRING], 16 * (n // WRING + 1)
        wload = [sem(f"weights_in{k}") for k in range(WRING)]
        rgather = [sem(f"raw_gathered{k}") for k in range(RAWS)]
        rload = [sem(f"raw_in{k}") for k in range(RAWS)]
        cload = [sem(f"cross_in{k}") for k in range(3)]
        sload = [sem(f"state_in{k}") for k in range(2)]

        def gathered_tile(name):
            return (name[0] == "c" and name[2] < 8) or name[0] in ("sk", "sv")

        def raw_count(name):
            n = raws[name]
            lst = list(raws)
            c = sum(gathered_tile(lst[m]) == gathered_tile(name) for m in range(n % RAWS, n + 1, RAWS))
            return (rgather if gathered_tile(name) else rload)[n % RAWS], 16 * c

        def raw_free(e, n):
            if n < RAWS:
                return
            k = list(raws)[n - RAWS]
            if k[0] == "c":
                full(e, ("xk", k[1], k[2]))
            elif k[0] in ("sk", "wk"):
                full(e, (k[0] + "T", k[1], k[2]))
            else:
                e.wait_ge(sem("values_used"), 8 * k[1] + (4 if k[0] == "wv" else 0) + k[2] + 1)

        def past(ap, L):
            w = 2 * LEVELS[L]
            return ap.rearrange("p (k w) -> p k w", w=w)[:, :, w // 2:w] if L else ap

        def before(ap, L):
            w = 2 * LEVELS[L]
            return ap.rearrange("p (k w) -> p k w", w=w)[:, :, 0:w // 2]

        def packed(ap, L):
            return ap.rearrange("p (k h) -> p k h", h=LEVELS[L])

        def full(e, key):
            e.wait_ge(psum_full, ring[key] + 1)

        def evac(e, key):
            e.wait_ge(psum_free[ring[key] % 3], ring[key] // 3 + 1)

        def slot(key):
            return RS[ring[key] % 3]

        def freed(key):
            return psum_free[ring[key] % 3]

        block = ctx.enter_context(nc.Block())

        @block.tensor
        def _(pe):
            mm, tr = nc.tensor.matmul, nc.tensor.transpose

            def open_item(key):
                i = ring[key]
                if i >= 3:
                    pe.wait_ge(psum_free[i % 3], i // 3)
                return RS[i % 3]

            def open_hold(key):
                if hold[key]:
                    pe.wait_ge(hold_free, hold[key])
                return HOLD

            def token_tiles(tt):
                return (tt * P, P) if tt < QT else (SEQ, NSMP)

            def norm_sum(n):
                ps = open_item(("sum", n))
                for k in range(KT):
                    pe.wait_ge(sem("squares"), 8 * n + k + 1)
                    for hf in range(2):
                        last = mm(ps[:, hf * 512:hf * 512 + HALF], ones[:, :], H[:, k, hf * HALF:(hf + 1) * HALF],
                                  start=(k == 0), stop=(k == KT - 1))
                last.then_inc(psum_full, 1)

            def token_major(name, cols, keys, sample=True):
                w, s, c = wsl(name)
                w = w[:, 0:KT * cols].rearrange("p (k n) -> p k n", k=KT)
                pe.wait_ge(s, c)
                ps = open_item(keys[0])
                for tt in range(QT):
                    for k in range(KT):
                        last = mm(ps[:, tt * cols:(tt + 1) * cols], H[:, k, tt * P:(tt + 1) * P], w[:, k, :],
                                  start=(k == 0), stop=(k == KT - 1))
                if sample:
                    last.then_inc(psum_full, 1)
                    ps = open_item(keys[1])
                    o = ps[0:NSMP, 0:cols]
                else:
                    o = ps[0:NSMP, 512:512 + cols]
                for k in range(KT):
                    last = mm(o, H[:, k, SEQ:TOK], w[:, k, :], start=(k == 0), stop=(k == KT - 1))
                last.then_inc(psum_full, 1)

            def feature_major(name, keys, rhs, wait_k=None):
                w, s, c = wsl(name)
                w = w.rearrange("p (k n) -> p k n", k=KT)
                pe.wait_ge(s, c)
                for m in range(2):
                    ps = open_item(keys[m])
                    for k in range(KT):
                        if wait_k:
                            wait_k(k)
                        for hf in range(2):
                            last = mm(ps[:, hf * 512:hf * 512 + HALF], w[:, k, m * P:(m + 1) * P],
                                      rhs[:, k, hf * HALF:(hf + 1) * HALF], start=(k == 0), stop=(k == KT - 1))
                    last.then_inc(psum_full, 1)

            def normed(n):
                return lambda k: pe.wait_ge(sem("normed"), 8 * n + k + 1)

            pe.wait_ge(sem("cst_in"), 16)
            pe.wait_ge(sem("vec_in"), 16 * 10)
            ps = open_item(("vec",))
            tr(ps[:, 0:ROWV], VECS[0:ROWV, :], ident[0:ROWV, 0:ROWV]).then_inc(psum_full, 1)
            pe.wait_ge(sem("x_in"), 32)
            for k in range(KT):
                ps = open_item(("xT", k))
                for tt in range(QT + 1):
                    at, n = token_tiles(tt)
                    last = tr(ps[:, at:at + n], XST[0:n, tt, k * P:(k + 1) * P], ident[0:n, 0:n])
                last.then_inc(psum_full, 1)
            pe.wait_ge(sem("ones"), 1)
            norm_sum(0)
            pe.wait_ge(sem("normed"), KT)
            for name, cols in (("cmp", 256), ("sel", 256), ("win", 256), ("gate", 24), ("q0", 256), ("q1", 256)):
                token_major((name,), cols, [(name, "p"), (name, "s")], sample=name != "gate")
            pe.wait_ge(sem("k_rotated"), 1)
            for s in range(2):
                ps = open_item(("kT", s))
                for tt in range(QT + 1):
                    at, n = token_tiles(tt)
                    last = tr(ps[:, at:at + n], ksw[0:n, tt, s, :], ident[0:n, 0:n])
                last.then_inc(psum_full, 1)
            for rot in range(2):
                if rot:
                    pe.wait_ge(sem("q_rotated"), 1)
                else:
                    evac(pe, ("q1", "s"))
                    evac(pe, ("q0", "s"))
                    evac(pe, ("q1", "p"))
                    evac(pe, ("q0", "p"))
                for r in range(NR):
                    ps = open_item(("qT", rot, r))
                    for tt in range(QT + 1):
                        at, n = token_tiles(tt)
                        last = tr(ps[:, at:at + n], qtok[0:n, tt, r * GW:(r + 1) * GW], ident[0:n, 0:n])
                    last.then_inc(psum_full, 1)

            def cmp_transpose(kv, n):
                s, c = raw_count(("c", kv, n))
                pe.wait_ge(s, c)
                raw = RAW[:, raws[("c", kv, n)] % RAWS, :]
                rows = P if n < 8 else SEQ // 8
                ps = open_item(("xk", kv, n))
                for j in range(8):
                    last = tr(ps[:, j * rows:(j + 1) * rows], raw[0:rows, j * GW:(j + 1) * GW],
                              ident[0:rows, 0:rows])
                last.then_inc(psum_full, 1)

            def cmp_hidden(kv, n):
                g4, j = seqs[n]
                rows, nb = (P, NCB) if n < 8 else (SEQ // 8, NPB)
                w = wsl(("w1", kv))[0].rearrange("p (k n) -> p k n", k=16)
                evac(pe, ("xk", kv, n))
                x = XK[:, n % XKS, 0:8 * rows].rearrange("p (m g s e) -> p m g e s", m=4, g=NG, e=2)
                if j == 0:
                    open_hold(("h", kv, g4))
                o = HOLD[:, j * 2 * NCB:j * 2 * NCB + 2 * nb].rearrange("p (g s) -> p g s", g=NG)
                for k in range(16):
                    half, e, m = k // 8, k // 4 % 2, k % 4
                    last = mm(o, w[:, k, :], x[:, m, :, e, half:half + nb], start=(k == 0), stop=(k == 15))
                if j == 3 or n == 8:
                    last.then_inc(hold_full, 1)

            def cmp_out(kv, g4):
                ps = open_item(("kvc", kv, g4))
                pe.wait_ge(sem("cmp_hid"), kv * 3 + g4 + 1)
                cnt, nb = (4, NCB) if g4 < 2 else (1, NPB)
                h = HX[:, g4 % 2, 0:cnt * 2 * nb].rearrange("p (b g n) -> p b g n", b=cnt, g=NG)
                for g in range(NG):
                    if kv == 0:
                        o = ps[g * HD:(g + 1) * HD, 0:cnt * nb].rearrange("p (b n) -> p b n", b=cnt)
                        last = mm(o, w2[:, 0, :], h[:, :, g, :], start=True, stop=True)
                    else:
                        for b in range(cnt):
                            last = mm(ps[0:nb, b * GW + g * HD:b * GW + (g + 1) * HD], h[:, b, g, :], w2[:, 1, :],
                                      start=True, stop=True)
                last.then_inc(psum_full, 1)

            pe.wait_ge(sem("w2_in"), 32)
            for kv in range(2):
                w, s, c = wsl(("w1", kv))
                w = w.rearrange("p (k n) -> p k n", k=16)
                pe.wait_ge(s, c)
                ps = open_item(("pe", kv))
                evac(pe, ("vec",))
                for k in range(16):
                    last = mm(ps[:, 0:1], w[:, k, :], GV[:, V_PEK + 16 * kv + k:V_PEK + 16 * kv + k + 1],
                              start=(k == 0), stop=(k == 15))
                last.then_inc(psum_full, 1)
                for n in range(len(seqs)):
                    cmp_transpose(kv, n)
                    if n == 6:
                        cmp_out(kv, 0)
                    if n == 8:
                        cmp_hidden(kv, n - 1)
                        cmp_out(kv, 1)
                    elif n:
                        cmp_hidden(kv, n - 1)
                cmp_hidden(kv, 8)
                cmp_out(kv, 2)

            evac(pe, ("qT", 1, NR - 1))
            evac(pe, ("qT", 1, NR - 2))
            evac(pe, ("qT", 1, NR - 3))
            evac(pe, ("kvc", 0, 2))
            ps = open_item(("pcs",))
            for r in range(NR):
                for i in range(QT):
                    for g in range(NG):
                        at = g * 512 + (r * QT + i) * NPB
                        last = mm(ps[:, at:at + NPB], qT[g * HD:(g + 1) * HD, r, i * P:(i + 1) * P],
                                  kcT[g * HD:(g + 1) * HD, 8, 0:NPB], start=True, stop=True)
            last.then_inc(psum_full, 1)

            def score(n):
                i, g, r = heads[n]
                ps = open_item(("S", n))
                for s in range(2):
                    last = mm(ps[:, s * 512:s * 512 + (i + 1) * P], qrT[g * HD:(g + 1) * HD, r, i * P:(i + 1) * P],
                              kT[g * HD:(g + 1) * HD, s, 0:(i + 1) * P], start=True, stop=True)
                last.then_inc(psum_full, 1)

            def probs_t(n):
                i = heads[n][0]
                ps = open_item(("PT", n))
                evac(pe, ("S", n))
                for s in range(2):
                    for k in range(i + 1):
                        at = (s * (i + 1) + k) * P
                        last = tr(ps[:, at:at + P], Pb[:, n % 2, s * 512 + k * P:s * 512 + (k + 1) * P], ident)
                last.then_inc(psum_full, 1)

            def weigh(n):
                i, g, r = heads[n]
                if r == 0:
                    open_hold(("o", i, g))
                if r == 0 and g == 0:
                    evac(pe, ("PTc", i))
                evac(pe, ("PT", n))
                o = HOLD[:, r * 3 * HD:(r + 1) * 3 * HD].rearrange("p (b d) -> p b d", b=3)
                hh = g * NR + r
                mm(o[:, 0], PTc[0:NPB, i % 2, hh * P:(hh + 1) * P], vc[0:NPB, 8, g * HD:(g + 1) * HD],
                   start=True, stop=True)
                for s in range(2):
                    for k in range(i + 1):
                        at = (s * (i + 1) + k) * P
                        last = mm(o[:, 1 + s], PTb[:, n % 2, at:at + P], vtok[:, k, s, g * HD:(g + 1) * HD],
                                  start=(k == 0), stop=(k == i))
                if r == NR - 1:
                    last.then_inc(hold_full, 1)

            score(0)
            score(1)
            for n in range(len(heads)):
                i = heads[n][0]
                if n % 8 == 0:
                    ps = open_item(("PTc", i))
                    pe.wait_ge(sem("cmp_probs"), 1)
                    for hh in range(NH):
                        last = tr(ps[0:NPB, hh * P:(hh + 1) * P],
                                  cP[:, (hh * QT + i) * NPB:(hh * QT + i + 1) * NPB], ident)
                    last.then_inc(psum_full, 1)
                probs_t(n)
                if n + 2 < len(heads):
                    score(n + 2)
                if n:
                    weigh(n - 1)
            weigh(len(heads) - 1)

            def raw_keys_t(kind, rd, b, tiles):
                s, c = raw_count((kind, rd, b))
                pe.wait_ge(s, c)
                ps = open_item((kind + "T", rd, b))
                for j in range(tiles):
                    last = tr(ps[:, j * P:(j + 1) * P], RAW[:, raws[(kind, rd, b)] % RAWS, j * P:(j + 1) * P], ident)
                last.then_inc(psum_full, 1)

            pe.wait_ge(sem("q_diag"), 2)
            evac(pe, ("kvc", 0, 0))
            evac(pe, ("kvc", 0, 1))
            for rd in range(2):
                qd = [qbd[:, k, rd * P:(rd + 1) * P] for k in range(2)]
                ps = open_item(("sms", rd))
                for b in range(4):
                    mm(ps[32 * b:32 * b + 32, 0:NCB], qd[0][:, 32 * b:32 * b + 32], kcT[:, 4 * rd + b, :],
                       start=True, stop=True)
                for s in range(2):
                    last = mm(ps[:, 64 + 32 * s:96 + 32 * s], qd[1], kT[:, s, SEQ:TOK], start=True, stop=True)
                last.then_inc(psum_full, 1)
                ps = open_item(("imp", rd))
                pe.wait_ge(sem("smp_cmp"), rd + 1)
                mm(ps[:, 0:64], cst("gsum"), cPn, start=True, stop=True).then_inc(psum_full, 1)
                for kind, tiles, hk in (("sk", 8, "Ss"), ("wk", 4, "Sw")):
                    for b in range(5):
                        if b < 4:
                            raw_keys_t(kind, rd, b, tiles)
                        if b == 1:
                            open_hold((hk, rd))
                        if b:
                            evac(pe, (kind + "T", rd, b - 1))
                            for c in range(tiles // 4):
                                last = mm(HOLD[32 * (b - 1):32 * b, c * 512:(c + 1) * 512],
                                          qd[1][:, 32 * (b - 1):32 * b], XK[:, (b - 1) % XKS, c * 512:(c + 1) * 512],
                                          start=True, stop=True)
                    last.then_inc(hold_full, 1)
                ps = open_item(("sPT", rd, 0))
                pe.wait_ge(sem("smp_sel"), rd + 1)
                for j in range(8):
                    last = tr(ps[:, j * P:(j + 1) * P], sS[:, j * P:(j + 1) * P], ident)
                last.then_inc(psum_full, 1)
                ps = open_item(("sPT", rd, 1))
                pe.wait_ge(sem("smp_win"), rd + 1)
                tr(ps[0:32, 0:P], sS[:, 1024:1056], ident)
                tr(ps[0:32, P:2 * P], wS[:, 512:544], ident)
                tr(ps[0:NCB, 2 * P:3 * P], cPn[:, 0:NCB], ident)
                for j in range(4):
                    last = tr(ps[:, (3 + j) * P:(4 + j) * P], wS[:, j * P:(j + 1) * P], ident)
                last.then_inc(psum_full, 1)
                evac(pe, ("sPT", rd, 0))
                evac(pe, ("sPT", rd, 1))
                open_hold(("PV", rd))
                for br, kind, tiles in ((1, "sv", 8), (2, "wv", 4)):
                    for b in range(4):
                        s, c = raw_count((kind, rd, b))
                        pe.wait_ge(s, c)
                        o = HOLD[32 * b:32 * b + 32, br * P:(br + 1) * P]
                        rows = slice(32 * b, 32 * b + 32)
                        pt = sPT if br == 1 else mPT[:, 384:896]
                        mm(o, mPT[0:32, (br - 1) * P + 32 * b:(br - 1) * P + 32 * b + 32], vtok[0:32, QT, br - 1, :],
                           start=True, stop=False)
                        for j in range(tiles):
                            last = mm(o, pt[:, j * P + 32 * b:j * P + 32 * b + 32],
                                      RAW[:, raws[(kind, rd, b)] % RAWS, j * P:(j + 1) * P],
                                      start=False, stop=(j == tiles - 1))
                        last.then_inc(sem("values_used"), 1)
                for b in range(4):
                    last = mm(HOLD[32 * b:32 * b + 32, 0:P], mPT[0:NCB, 2 * P + 32 * b:2 * P + 32 * b + 32],
                              vc[0:NCB, 4 * rd + b, :], start=True, stop=True)
                last.then_inc(hold_full, 1)
            pe.wait_ge(sem("nsa_normed"), 1)
            for f in range(4):
                ps = open_item(("nT", f))
                for tt in range(QT + 1):
                    at, n = token_tiles(tt)
                    last = tr(ps[:, at:at + n], otok[0:n, tt, f * P:(f + 1) * P], ident[0:n, 0:n])
                last.then_inc(psum_full, 1)

            for c in ("hi0", "hi1"):
                token_major((c,), 256, [(c, "p"), (c, "s")])
            for c in ("hf", "hq", "hg"):
                for n in range(2):
                    feature_major((c, n), [(c, 2 * n), (c, 2 * n + 1)], H)
            for h in range(HH):
                hs = slice(h * HK, (h + 1) * HK)
                ps = open_item(("klT", h))
                pe.wait_ge(sem("k_decayed"), h + 1)
                for tt in range(QT + 1):
                    at, n = token_tiles(tt)
                    last = tr(ps[0:n, tt * P:(tt + 1) * P], kdec[:, at:at + n], ident)
                last.then_inc(psum_full, 1)
                ps = open_item(("dS", h))
                evac(pe, ("klT", h))
                if h == 0:
                    for c in ("hi0", "hi1"):
                        evac(pe, (c, "p"))
                        evac(pe, (c, "s"))
                for c in range(QT):
                    last = mm(ps[:, c * HK:(c + 1) * HK], kltok[:, c, :], hi[:, c, hs], start=True, stop=True)
                last.then_inc(psum_full, 1)
                ps = open_item(("dSs", h))
                pe.wait_ge(sem("v_diag"), h + 1)
                for c in range(2):
                    last = mm(ps[:, c * 512:(c + 1) * 512], kltok[0:NSMP, QT, :], Vbd[0:NSMP, c * 512:(c + 1) * 512],
                              start=True, stop=True)
                last.then_inc(psum_full, 1)
                for L in range(len(LEVELS)):
                    ps = open_item(("A", h, L))
                    if L:
                        pe.wait_ge(sem("levels"), 2 * (h * 7 + L))
                        q, k = LQ[:, (h * 7 + L) % 2, :], LK[:, (h * 7 + L) % 2, :]
                    else:
                        q, k = hQ[:, h, :], hK[:, h, :]
                        evac(pe, ("hq", h))
                    nq = P // 2 if L else P
                    for c in range(QT):
                        last = mm(ps[:, c * nq:(c + 1) * nq], k[:, c * P:(c + 1) * P],
                                  past(q[:, c * P:(c + 1) * P], L), start=True, stop=True)
                    if LEVELS[L] < DS:
                        ns = NSMP // 2 if L else NSMP
                        last = mm(ps[0:NSMP, 512:512 + ns], k[:, SEQ:TOK], past(q[:, SEQ:TOK], L),
                                  start=True, stop=True)
                    last.then_inc(psum_full, 1)
                ps = open_item(("o", h))
                pe.wait_ge(sem("scores_done"), h + 1)
                pe.wait_ge(sem("states_done"), h + 1)
                pe.wait_ge(sem("q_decayed"), h + 1)
                pe.wait_ge(sload[h % 2], 16 * (h // 2 + 1))
                for c in range(QT):
                    cs = slice(c * P, (c + 1) * P)
                    if c:
                        mm(ps[:, cs], Sst[:, c - 1, :], qdec[:, cs], start=True, stop=False)
                    mm(ps[:, cs], hi[:, c, hs], Aacc[:, cs], start=(c == 0), stop=True)
                for b in range(DB):
                    mm(ps[:, 512 + DS * b:512 + DS * b + DS], S0[:, h % 2, b * HK:(b + 1) * HK],
                       qdec[:, SEQ + DS * b:SEQ + DS * b + DS], start=(b == 0), stop=False, skip_group_check=True)
                mm(ps[:, 512:TOK], hi[0:NSMP, QT, hs], Aacc[0:NSMP, SEQ:TOK], start=False, stop=True,
                   skip_group_check=True).then_inc(psum_full, 1)
                ps = open_item(("osum", h))
                pe.wait_ge(sem("o_squares"), h + 1)
                for hf in range(2):
                    last = mm(ps[:, hf * 512:hf * 512 + HALF], ones[:, :], gtmp[:, hf * HALF:(hf + 1) * HALF],
                              start=True, stop=True)
                last.then_inc(psum_full, 1)

            def mixed(k):
                if k < 4:
                    evac(pe, ("nT", k))
                else:
                    pe.wait_ge(sem("hg_out"), k - 3)
            for n in range(4):
                feature_major(("wout", n), [("wout", 2 * n), ("wout", 2 * n + 1)], MX, mixed if n == 0 else None)

            pe.wait_ge(sem("mem_in"), 16)
            for n in range(2):
                ps = open_item(("mT", n))
                for k in range(4):
                    for m in range(2):
                        last = tr(ps[:, k * MEM + m * P:k * MEM + (m + 1) * P],
                                  mst[:, m, (4 * n + k) * P:(4 * n + k + 1) * P], ident)
                last.then_inc(psum_full, 1)
            ps = open_item(("msum",))
            pe.wait_ge(sem("mem_squares"), 2)
            sq = mkT
            for k in range(KT):
                last = mm(ps[:, 0:MEM], ones[:, :], sq[:, k, :], start=(k == 0), stop=(k == KT - 1))
            last.then_inc(psum_full, 1)
            pe.wait_ge(sem("mem_normed"), 1)
            for c in ("wk", "wv"):
                for n in range(4):
                    w, s, cnt = wsl((c, n))
                    w = w.rearrange("p (k n) -> p k n", k=KT)
                    pe.wait_ge(s, cnt)
                    ps = open_item((c, n))
                    for m in range(2):
                        for k in range(KT):
                            last = mm(ps[:, m * 256:(m + 1) * 256], mnT[:, k, m * P:(m + 1) * P], w[:, k, :],
                                      start=(k == 0), stop=(k == KT - 1))
                    last.then_inc(psum_full, 1)
            for n in range(4):
                evac(pe, ("wk", n))
            for n in range(2):
                ps = open_item(("mkT", n))
                for k in range(4):
                    for m in range(2):
                        last = tr(ps[:, k * MEM + m * P:k * MEM + (m + 1) * P],
                                  mst[:, m, (4 * n + k) * P:(4 * n + k + 1) * P], ident)
                last.then_inc(psum_full, 1)
            norm_sum(1)
            for n in range(4):
                feature_major(("wq", n), [("wq", 2 * n), ("wq", 2 * n + 1)], H, normed(1) if n == 0 else None)

            for n in (5, 6, 7):
                evac(pe, ("wq", n))
            for n in range(2):
                evac(pe, ("mkT", n))
            for n in range(4):
                evac(pe, ("wv", n))
            for i in range(QT):
                cs = slice(i * P, (i + 1) * P)
                ps = open_item(("cS", i))
                for h in range(CH):
                    for k in range(2):
                        last = mm(ps[:, h * MEM:(h + 1) * MEM], QC[:, 2 * h + k, cs], mkT[:, 2 * h + k, :],
                                  start=(k == 0), stop=(k == 1))
                last.then_inc(psum_full, 1)
                ps = open_item(("cPT", i))
                pe.wait_ge(sem("cross_probs"), i + 1)
                for h in range(CH):
                    for m in range(2):
                        at = (2 * h + m) * P
                        last = tr(ps[:, at:at + P], xP[:, i % 2, at:at + P], ident)
                last.then_inc(psum_full, 1)
                ps = open_item(("cO", i))
                evac(pe, ("cPT", i))
                for d in range(KT):
                    for m in range(2):
                        at = (2 * (d // 2) + m) * P
                        last = mm(ps[:, d * P:(d + 1) * P], mv[:, m, d * P:(d + 1) * P], xPT[:, i % 2, at:at + P],
                                  start=(m == 0), stop=(m == 1))
                last.then_inc(psum_full, 1)
            pe.wait_ge(sem("cross_diag"), 1)
            parts = [(b, n) for b in range(DB) for n in range(2)]

            def mem_transpose(b, n):
                if n == 0:
                    pe.wait_ge(cload[b % 3], 16 * (b // 3 + 1))
                ps = open_item(("cx", b, n))
                raw = RC[:, b % 3, :].rearrange("p (j n) -> p j n", j=2)
                for k in range(4):
                    for j in range(2):
                        last = tr(ps[:, (2 * k + j) * P:(2 * k + j + 1) * P],
                                  raw[:, j, (4 * n + k) * P:(4 * n + k + 1) * P], ident)
                last.then_inc(psum_full, 1)

            mem_transpose(0, 0)
            open_hold(("cS",))
            for x, (b, n) in enumerate(parts):
                if x + 1 < len(parts):
                    mem_transpose(*parts[x + 1])
                evac(pe, ("cx", b, n))
                q = 32 * (b // 2)
                for k in range(4):
                    last = mm(HOLD[q:q + 32, 0:MEM], qbc[:, 4 * n + k, b, :], KX[:, x % 2, k * MEM:(k + 1) * MEM],
                              start=(b % 2 == 0 and n == 0 and k == 0), stop=(b % 2 == 1 and n == 1 and k == 3))
            last.then_inc(hold_full, 1)
            ps = open_item(("csPT",))
            pe.wait_ge(sem("cross_smp"), 1)
            for j in range(2):
                last = tr(ps[:, j * P:(j + 1) * P], yP[:, j * P:(j + 1) * P], ident)
            last.then_inc(psum_full, 1)
            evac(pe, ("csPT",))
            open_hold(("cO",))
            for b in range(DB):
                x = DB + b
                pe.wait_ge(cload[x % 3], 16 * (x // 3 + 1))
                raw = RC[:, x % 3, :].rearrange("p (j n) -> p j n", j=2)
                for d in range(KT):
                    for j in range(2):
                        at = j * P + 16 * b + 4 * (d // 2)
                        last = mm(HOLD[:, d * NSMP + DS * b:d * NSMP + DS * b + DS], raw[:, j, d * P:(d + 1) * P],
                                  yPT[:, at:at + DS], start=(j == 0), stop=(j == 1))
                last.then_inc(hold_full if b == DB - 1 else sem("cross_values_used"), 1)

            def crossed(k):
                if k == 0:
                    for i in range(QT):
                        evac(pe, ("cO", i))
                    pe.wait_ge(hold_free, hold[("cO",)] + 1)
            for n in range(4):
                feature_major(("wo", n), [("wo", 2 * n), ("wo", 2 * n + 1)], MX, crossed if n == 0 else None)

            norm_sum(2)
            for n in range(FT // 2):
                wg, sg, cg = wsl(("ffg", n))
                wu, su, cu = wsl(("ffu", n))
                pe.wait_ge(sg, cg)
                pe.wait_ge(su, cu)
                for m in range(2):
                    for name, w in (("ffg", wg), ("ffu", wu)):
                        w = w.rearrange("p (k n) -> p k n", k=KT)
                        ps = open_item((name, 2 * n + m))
                        for k in range(KT):
                            if n == 0 and m == 0 and name == "ffg":
                                pe.wait_ge(sem("normed"), 16 + k + 1)
                            for hf in range(2):
                                last = mm(ps[:, hf * 512:hf * 512 + HALF], w[:, k, m * P:(m + 1) * P],
                                          H[:, k, hf * HALF:(hf + 1) * HALF], start=(k == 0), stop=(k == KT - 1))
                        last.then_inc(psum_full, 1)
            for n in range(4):
                ps2 = [open_item(("ffd", 2 * n)), open_item(("ffd", 2 * n + 1))]
                for kc in range(3):
                    w, s, c = wsl(("ffd", n, kc))
                    w = w.rearrange("p (k n) -> p k n", k=KT)
                    pe.wait_ge(s, c)
                    for m in range(2):
                        for k in range(8 * kc, min(8 * kc + 8, FT)):
                            if n == 0 and m == 0:
                                pe.wait_ge(sem("hidden"), k + 1)
                            for hf in range(2):
                                last = mm(ps2[m][:, hf * 512:hf * 512 + HALF], w[:, k - 8 * kc, m * P:(m + 1) * P],
                                          hid[:, k, hf * HALF:(hf + 1) * HALF], start=(k == 0), stop=(k == FT - 1))
                        if kc == 2:
                            last.then_inc(psum_full, 1)
            norm_sum(3)
            pe.wait_ge(sem("normed"), 4 * KT)
            for tt in range(QT + 1):
                at, n = token_tiles(tt)
                ps = open_item(("y", tt))
                for k in range(KT):
                    last = tr(ps[0:n, k * P:(k + 1) * P], H[:, k, at:at + n], ident)
                last.then_inc(psum_full, 1)

        class Steps:
            def __init__(self, e, name):
                self.e, self.s, self.n = e, sem(name), 0

            def __call__(self, ins):
                ins.then_inc(self.s, 1)
                self.n += 1
                self.e.wait_ge(self.s, self.n)

        def halves(ps):
            return ps[:, :].rearrange("p (a t) -> p a t", a=2)[:, :, 0:HALF]

        def two(ap):
            return ap.rearrange("p (a t) -> p a t", a=2)

        def p4(ps, cols=256):
            return ps[:, 0:4 * cols].rearrange("p (t n) -> p t n", t=4)

        @block.scalar
        def _(act):
            fn = nc.scalar.activation
            step = Steps(act, "act_step")
            COPY, EXP = ACT.Copy, ACT.Exp

            def copy_out(key, out_, in_):
                full(act, key)
                fn(out_, in_, COPY).then_inc(freed(key), 1)

            rms_count = [0]

            def rsqrt(y, m):
                rms_count[0] += 1
                act.wait_ge(sem("mean_in"), rms_count[0])
                step(fn(y, m, ACT.Ln))
                fn(y, y, EXP, scale=-0.5).then_inc(sem("rsqrt_guess"), 1)

            copy_out(("vec",), GV[:, :], slot(("vec",))[:, 0:ROWV])
            for k in range(KT):
                copy_out(("xT", k), X[:, k, :], slot(("xT", k))[:, 0:TOK])
            rsqrt(RSTD[:, :], MEAN[:, :])
            act.wait_ge(sem("cleared"), 3)
            for name, dst in (("cmp", None), ("sel", 0), ("win", 1)):
                kp, ks_ = (name, "p"), (name, "s")
                full(act, kp)
                if dst is None:
                    fn(ckcv[:, 0:QT, :], p4(slot(kp)), COPY).then_inc(freed(kp), 1)
                    copy_out(ks_, ckcv[0:NSMP, QT, :], slot(ks_)[0:NSMP, 0:256])
                else:
                    step(fn(ksw[:, 0:QT, dst, :], p4(slot(kp))[:, :, 0:GW], COPY))
                    fn(vtok[:, 0:QT, dst, :], p4(slot(kp))[:, :, GW:256], COPY).then_inc(freed(kp), 1)
                    full(act, ks_)
                    step(fn(ksw[0:NSMP, QT, dst, :], slot(ks_)[0:NSMP, 0:GW], COPY))
                    fn(vtok[0:NSMP, QT, dst, :], slot(ks_)[0:NSMP, GW:256], COPY).then_inc(freed(ks_), 1)
            kp = ("gate", "p")
            full(act, kp)
            step(fn(gates[:, 0:QT, :], p4(slot(kp), 24), EXP, scale=-1.0))
            fn(gates[0:NSMP, QT, :], slot(kp)[0:NSMP, 512:536], EXP, scale=-1.0).then_inc(freed(kp), 1)
            for n in range(2):
                kp, ks_ = (f"q{n}", "p"), (f"q{n}", "s")
                q4 = qtok.rearrange("p t (r g d) -> p t r g d", r=NR, g=NG)
                copy_out(kp, q4[:, 0:QT, :, n, :], p4(slot(kp)).rearrange("p t (r d) -> p t r d", r=NR))
                copy_out(ks_, q4[0:NSMP, QT, :, n, :], slot(ks_)[0:NSMP, 0:256].rearrange("p (r d) -> p r d", r=NR))
            for s in range(2):
                copy_out(("kT", s), kT[:, s, :], slot(("kT", s))[:, 0:TOK])
            for rot in range(2):
                for r in range(NR):
                    copy_out(("qT", rot, r), (qrT if rot else qT)[:, r, :], slot(("qT", rot, r))[:, 0:TOK])

            def gelu_exp(n):
                act.wait_ge(sem("gelu_in"), n + 1)
                g4 = n % 3
                w = 504 if g4 < 2 else 2 * NPB
                fn(HT[:, 0:w], HT[:, 0:w], EXP, scale=-2 * 0.7978845608028654).then_inc(sem("gelu_exp"), 1)

            def cmp_result(kv, g4):
                key = ("kvc", kv, g4)
                cnt, nb = (4, NCB) if g4 < 2 else (1, NPB)
                if kv == 0:
                    copy_out(key, kcT[:, 4 * g4:4 * g4 + cnt, 0:nb],
                             slot(key)[:, 0:cnt * nb].rearrange("p (b n) -> p b n", b=cnt))
                else:
                    copy_out(key, vc[0:nb, 4 * g4:4 * g4 + cnt, :],
                             slot(key)[0:nb, 0:cnt * GW].rearrange("p (b n) -> p b n", b=cnt))

            for kv in range(2):
                copy_out(("pe", kv), cb[:, kv:kv + 1], slot(("pe", kv))[:, 0:1])
                for n in range(9):
                    rows = P if n < 8 else SEQ // 8
                    key = ("xk", kv, n)
                    full(act, key)
                    dst = XK[:, n % XKS, 0:8 * rows].rearrange("p (m g s) -> p m g s", m=4, g=NG)
                    from_ = slot(key)[:, 0:8 * rows].rearrange("p (m a s) -> p m a s", m=4, a=2)
                    for g in range(NG):
                        for e in range(2):
                            ins = fn(dst[e * HD:(e + 1) * HD, :, g, :], from_[g * HD:(g + 1) * HD, :, e, :], COPY)
                            if g and e:
                                ins.then_inc(freed(key), 1)
                            else:
                                step(ins)
                    if n == 5:
                        gelu_exp(3 * kv)
                    if n == 6:
                        cmp_result(kv, 0)
                gelu_exp(3 * kv + 1)
                cmp_result(kv, 1)
                gelu_exp(3 * kv + 2)
                cmp_result(kv, 2)

            act.wait_ge(sem("pcs_in"), 1)
            fn(cP, cP, EXP, scale=SCALE).then_inc(sem("pcs_exp"), 1)

            def exps(n):
                i, g, r = heads[n]
                act.wait_ge(sem("row_max"), n + 1)
                ps, L = slot(("S", n)), (i + 1) * P
                for s in range(2):
                    at = (g * NR + r) * 3 + 1 + s
                    ins = fn(Pb[:, n % 2, s * 512:s * 512 + L], ps[:, s * 512:s * 512 + L], EXP,
                             bias=snm[:, 2 * (n % 2) + s:2 * (n % 2) + s + 1], scale=SCALE,
                             accum_out=DEN[:, i, at:at + 1])
                    if s:
                        ins.then_inc(freed(("S", n)), 1)
                    else:
                        step(ins)

            exps(0)
            exps(1)
            for n in range(len(heads)):
                i = heads[n][0]
                if n % 8 == 0:
                    copy_out(("PTc", i), PTc[0:NPB, i % 2, :], slot(("PTc", i))[0:NPB, :])
                w = 2 * (i + 1) * P
                copy_out(("PT", n), PTb[:, n % 2, 0:w], slot(("PT", n))[:, 0:w])
                if n + 2 < len(heads):
                    exps(n + 2)

            for rd in range(2):
                act.wait_ge(sem("smp_cmp_in"), rd + 1)
                fn(cPn[:, 0:NCB], cS[:, 0:NCB], EXP, bias=snm1[:, 0:1], scale=SCALE,
                   accum_out=sden[:, 0:1]).then_inc(sem("smp_cmp_exp"), 1)
                for kind, w in (("sk", 1024), ("wk", 512)):
                    for b in range(4):
                        key = (kind + "T", rd, b)
                        copy_out(key, XK[:, b % XKS, 0:w], slot(key)[:, 0:w])
                act.wait_ge(sem("smp_sel_in"), rd + 1)
                fn(sS, sS, EXP, bias=snm1[:, 1:2], scale=SCALE,
                   accum_out=sden[:, 1:2]).then_inc(sem("smp_sel"), 1)
                act.wait_ge(sem("smp_win_in"), rd + 1)
                fn(wS, wS, EXP, bias=snm1[:, 2:3], scale=SCALE,
                   accum_out=sden[:, 2:3]).then_inc(sem("smp_win"), 1)
                copy_out(("sPT", rd, 0), sPT, slot(("sPT", rd, 0))[:, :])
                key = ("sPT", rd, 1)
                full(act, key)
                step(fn(mPT[0:32, 0:2 * P], slot(key)[0:32, 0:2 * P], COPY))
                step(fn(mPT[0:NCB, 2 * P:3 * P], slot(key)[0:NCB, 2 * P:3 * P], COPY))
                fn(mPT[:, 384:896], slot(key)[:, 384:896], COPY).then_inc(freed(key), 1)
            act.wait_ge(sem("otok_done"), 1)
            for tt in range(QT + 1):
                n = P if tt < QT else NSMP
                step(fn(Pb[0:n, 0, 0:NSAW], otok[0:n, tt, :], ACT.Square, accum_out=ss[0:n, tt:tt + 1]))
            act.sem_inc(sem("nsa_squares"), 1)
            rsqrt(rs5[:, 0:QT], sm5[:, 0:QT])
            rsqrt(rs5[0:NSMP, QT:QT + 1], sm5[0:NSMP, QT:QT + 1])
            act.sem_inc(sem("act_phase"), 1)

            act.wait_ge(sem("dve_phase"), 1)
            act.wait_ge(sem("store_phase"), 1)
            for n in range(2):
                kp, ks_ = (f"hi{n}", "p"), (f"hi{n}", "s")
                cs = slice(n * 256, (n + 1) * 256)
                copy_out(kp, hi[:, 0:QT, cs], p4(slot(kp)))
                copy_out(ks_, hi[0:NSMP, QT, cs], slot(ks_)[0:NSMP, 0:256])

            act.wait_ge(sem("lb_in"), 1)
            fn(lb, lb, EXP).then_inc(sem("lb_exp"), 1)

            def log_f(h):
                act.wait_ge(sem("forget_in"), h + 1)
                fn(hB[:, h, :], hB[:, h, :], ACT.Ln).then_inc(sem("forget_log"), 1)
            for h in range(HH):
                key = ("hf", h)
                full(act, key)
                fn(two(hK[:, h, :]), halves(slot(key)), EXP, scale=-1.0).then_inc(freed(key), 1)
            for h in range(HH):
                log_f(h)
                copy_out(("hq", h), two(hQ[:, h, :]), halves(slot(("hq", h))))
            for h in range(HH):
                key = ("hg", h)
                full(act, key)
                fn(two(hG[:, h, :]), halves(slot(key)), EXP, scale=-1.0).then_inc(sem("out_gate_exp"), 1)
            for h in range(HH):
                act.wait_ge(sem("decay_sum"), h + 1)
                if h:
                    act.wait_ge(sem("q_decayed"), h)
                    act.wait_ge(sem("states_done"), h)
                fn(E0, hB[:, h, :], EXP).then_inc(sem("decay_exp"), 1)
                act.wait_ge(sem("k_decay_in"), h + 1)
                fn(kdec, kdec, EXP).then_inc(sem("k_decay_exp"), 1)
                key = ("klT", h)
                full(act, key)
                step(fn(kltok[:, 0:QT, :], slot(key)[:, 0:512].rearrange("p (c n) -> p c n", c=4), COPY))
                fn(kltok[0:NSMP, QT, :], slot(key)[0:NSMP, 512:640], COPY).then_inc(freed(key), 1)
                for L in range(1, len(LEVELS)):
                    w = TOK if LEVELS[L] < DS else SEQ
                    x = h * 7 + L
                    act.wait_ge(sem("level_in"), 2 * x)
                    if x > 2:
                        act.wait_ge(sem("levels"), 2 * (x - 2))
                    fn(LE[:, x % 2, 0:w], LD[:, x % 2, 0:w], EXP, scale=-1.0).then_inc(sem("level_exp"), 1)
                key = ("o", h)
                full(act, key)
                if h:
                    act.wait_ge(sem("hg_out"), h)
                fn(gtmp, slot(key)[:, 0:TOK], ACT.Square).then_inc(sem("o_squares"), 1)
                rsqrt(RSTD[:, :], MEAN[:, :])
            act.wait_ge(sem("dve_phase"), 2)
            act.wait_ge(sem("store_phase"), 2)
            act.wait_ge(sem("mem_in"), 16)
            for n in range(2):
                copy_out(("mT", n), mnT[:, 4 * n:4 * n + 4, :],
                         slot(("mT", n))[:, :].rearrange("p (k n) -> p k n", k=4))
            rsqrt(RSTD[:, 0:MEM], MEAN[:, 0:MEM])
            for c, dst in (("wk", mst), ("wv", mv)):
                for n in range(4):
                    copy_out((c, n), dst[:, :, n * 256:(n + 1) * 256],
                             slot((c, n))[:, 0:512].rearrange("p (m n) -> p m n", m=2))
            for n in range(2):
                copy_out(("mkT", n), mkT[:, 4 * n:4 * n + 4, :],
                         slot(("mkT", n))[:, :].rearrange("p (k n) -> p k n", k=4))
            rsqrt(RSTD[:, :], MEAN[:, :])
            for n in range(KT):
                copy_out(("wq", n), two(QC[:, n, :]), halves(slot(("wq", n))))
            for i in range(QT):
                key = ("cS", i)
                act.wait_ge(sem("cross_max"), i + 1)
                for h in range(CH):
                    x = 4 * (i % 2) + h
                    ins = fn(xP[:, i % 2, h * MEM:(h + 1) * MEM], slot(key)[:, h * MEM:(h + 1) * MEM], EXP,
                             bias=xnm[:, x:x + 1], scale=CSCALE, accum_out=xden[:, x:x + 1])
                    if h == CH - 1:
                        ins.then_inc(freed(key), 1)
                    else:
                        step(ins)
                copy_out(("cPT", i), xPT[:, i % 2, :], slot(("cPT", i))[:, :])
                copy_out(("cO", i), MX[:, :, i * P:(i + 1) * P],
                         slot(("cO", i))[:, :].rearrange("p (k n) -> p k n", k=KT))
            for b in range(DB):
                for n in range(2):
                    copy_out(("cx", b, n), KX[:, n, :], slot(("cx", b, n))[:, :])
            act.wait_ge(sem("cross_smp_max"), 1)
            fn(yP, HOLD[:, 0:MEM], EXP, bias=msc[:, 0:1], scale=CSCALE,
               accum_out=msc[:, 1:2]).then_inc(hold_free, 1)
            copy_out(("csPT",), yPT, slot(("csPT",))[:, 0:MEM])
            act.wait_ge(hold_full, hold[("cO",)] + 1)
            fn(MX[:, :, SEQ:TOK], HOLD[:, 0:KT * NSMP].rearrange("p (k n) -> p k n", k=KT),
               COPY).then_inc(hold_free, 1)
            act.wait_ge(hold_free, len(hold))
            act.sem_inc(sem("act_phase"), 1)
            rsqrt(RSTD[:, :], MEAN[:, :])
            act.wait_ge(sem("dve_phase"), 3)
            act.wait_ge(sem("store_phase"), 3)
            for j in range(FT):
                key = ("ffg", j)
                full(act, key)
                if j >= 2:
                    act.wait_ge(sem("hidden"), j - 1)
                fn(two(ftmp[:, j % 2, :]), halves(slot(key)), EXP, scale=-1.0).then_inc(sem("gate_exp"), 1)
            rsqrt(RSTD[:, :], MEAN[:, :])
            for tt in range(QT + 1):
                n = P if tt < QT else NSMP
                if tt >= 2:
                    act.wait_ge(sem(f"y_out{tt % 2}"), 16 * (tt // 2))
                copy_out(("y", tt), ymid[0:n, tt % 2, :], slot(("y", tt))[0:n, :])

        @block.vector
        def _(dve):
            v = nc.vector
            tt_, ts, stt, cp = v.tensor_tensor, v.tensor_scalar, v.scalar_tensor_tensor, v.tensor_copy
            step = Steps(dve, "dve_step")
            gain_at = [V_MIX, V_CA, V_FFN, V_FIN]

            def square(k):
                tt_(H[:, k, :], X[:, k, :], X[:, k, :], ALU.mult).then_inc(sem("squares"), 1)

            rms_count = [0]

            def refine(y, m, t):
                rms_count[0] += 1
                dve.wait_ge(sem("rsqrt_guess"), rms_count[0])
                step(tt_(t, y, y, ALU.mult))
                step(tt_(t, t, m, ALU.mult))
                step(ts(t, t, -0.5, 1.5, ALU.mult, ALU.add))
                step(tt_(y, y, t, ALU.mult))

            def inverse_rms(key, n, width, scratch):
                full(dve, key)
                if n == TOK:
                    ts(two(MEAN[:, :]), halves(slot(key)), 1.0 / width, EPS, ALU.mult, ALU.add).then_inc(freed(key), 1)
                else:
                    ts(MEAN[:, 0:n], slot(key)[:, 0:n], 1.0 / width, EPS, ALU.mult, ALU.add).then_inc(freed(key), 1)
                evac(dve, key)
                dve.sem_inc(sem("mean_in"), 1)
                refine(RSTD[:, 0:n], MEAN[:, 0:n], scratch)

            def normalize(n):
                key = ("sum", n)
                inverse_rms(key, TOK, DM, H[:, 0, :])
                evac(dve, ("vec",))
                for k in range(KT):
                    g = GV[:, gain_at[n] + k:gain_at[n] + k + 1]
                    stt(H[:, k, :], X[:, k, :], g, RSTD[:, :], ALU.mult, ALU.mult).then_inc(sem("normed"), 1)

            def rotate(x, nh):
                x = x.rearrange("p t (h d) -> p t h d", h=nh)
                cs = cst("rope").rearrange("p (t n) -> p t n", t=5)
                cos, sin = bc(cs[:, :, 0:8], 2, nh), bc(cs[:, :, 8:16], 2, nh)
                x1, x2 = x[:, :, :, 0:8], x[:, :, :, 8:16]
                t = [r[:, 0:5 * nh * 8].rearrange("p (t h d) -> p t h d", t=5, h=nh) for r in rtmp]
                step(tt_(t[0], x1, cos, ALU.mult))
                step(tt_(t[1], x2, sin, ALU.mult))
                step(tt_(t[2], x1, sin, ALU.mult))
                step(tt_(t[3], x2, cos, ALU.mult))
                step(tt_(x1, t[0], t[1], ALU.subtract))
                return tt_(x2, t[2], t[3], ALU.add)

            for k in range(KT):
                evac(dve, ("xT", k))
                square(k)
            dve.wait_ge(sem("cst_in"), 16)
            normalize(0)
            for s in ("sel", "win"):
                evac(dve, (s, "p"))
                evac(dve, (s, "s"))
            rotate(ksw.rearrange("p t s d -> p t (s d)"), 4).then_inc(sem("k_rotated"), 1)
            evac(dve, ("gate", "p"))
            for g in (gates[:, 0:QT, :], gates[0:NSMP, QT, :]):
                step(ts(g, g, 1.0, None, ALU.add))
                step(v.reciprocal(g, g))
            dve.sem_inc(sem("gates_done"), 1)
            full(dve, ("qT", 0, NR - 1))
            rotate(qtok, NH).then_inc(sem("q_rotated"), 1)
            dve.wait_ge(sem("cleared"), 3)
            for rot in range(2):
                for r in range(NR):
                    evac(dve, ("qT", rot, r))
                src = qrT if rot else qT
                for g in range(NG):
                    for r in range(NR):
                        gs = slice(g * HD, (g + 1) * HD)
                        o = qbd[gs, rot, :].rearrange("p (b g r t) -> p b g r t", b=DB, g=NG, r=NR)[:, :, g, r, :]
                        step(cp(o, src[gs, r, SEQ:TOK].rearrange("p (b t) -> p b t", b=DB)))
                dve.sem_inc(sem("q_diag"), 1)

            def gelu(n):
                g4 = n % 3
                w = 504 if g4 < 2 else 2 * NPB
                x, t = HX[:, g4 % 2, 0:w], HT[:, 0:w]
                dve.wait_ge(hold_full, hold[("h", n // 3, g4)] + 1)
                evac(dve, ("pe", n // 3))
                ts(x, HOLD[:, 0:w], cb[:, n // 3:n // 3 + 1], None, ALU.add).then_inc(hold_free, 1)
                dve.wait_ge(hold_free, hold[("h", n // 3, g4)] + 1)
                step(tt_(t, x, x, ALU.mult))
                step(ts(t, t, 0.044715, 1.0, ALU.mult, ALU.add))
                tt_(t, t, x, ALU.mult).then_inc(sem("gelu_in"), 1)
                dve.wait_ge(sem("gelu_exp"), n + 1)
                step(ts(t, t, 1.0, None, ALU.add))
                step(v.reciprocal(t, t))
                tt_(x, x, t, ALU.mult).then_inc(sem("cmp_hid"), 1)

            for n in range(6):
                gelu(n)

            key = ("pcs",)
            dve.wait_ge(sem("t_stored"), 1)
            full(dve, key)
            c4 = cP.rearrange("p (g r n) -> p g r n", g=NG, r=NR)
            ps4 = slot(key)[:, :].rearrange("p (g n) -> p g n", g=2)[:, :, 0:496].rearrange("p g (r n) -> p g r n", r=NR)
            for g in range(NG):
                ins = tt_(c4[:, g], ps4[:, g], bc(cst("cadd"), 1, NR), ALU.add)
                if g:
                    ins.then_inc(freed(key), 1)
                    evac(dve, key)
                else:
                    step(ins)
            c3 = cP.rearrange("p (h n) -> p h n", n=NPB)
            step(v.tensor_reduce(pmx, c3, AX, ALU.max))
            tt_(c3, c3, bc(pmx, 2, NPB), ALU.subtract).then_inc(sem("pcs_in"), 1)
            dve.wait_ge(sem("pcs_exp"), 1)
            step(tt_(cP.rearrange("p (h n) -> p h n", h=NH), cP.rearrange("p (h n) -> p h n", h=NH),
                     bc(cst("cmul"), 1, NH), ALU.mult))
            den = DEN.rearrange("p i (h b) -> p h i b", b=3)[:, :, :, 0]
            step(v.tensor_reduce(den, cP.rearrange("p (h i n) -> p h i n", h=NH, i=QT), AX, ALU.add))
            ts(den, den, 1e-20, None, ALU.max).then_inc(sem("cmp_probs"), 1)
            dve.wait_ge(sem("cmp_probs"), 1)

            def row_max(n):
                i = heads[n][0]
                key = ("S", n)
                full(dve, key)
                s2 = slot(key)[:, :].rearrange("p (s n) -> p s n", s=2)
                diag = s2[:, :, i * P:(i + 1) * P]
                step(tt_(diag, diag, bc(cst("causal"), 1, 2), ALU.add))
                mx = smx[:, 2 * (n % 2):2 * (n % 2) + 2]
                step(v.tensor_reduce(mx, s2[:, :, 0:(i + 1) * P], AX, ALU.max))
                if n >= 2:
                    evac(dve, ("S", n - 2))
                ts(snm[:, 2 * (n % 2):2 * (n % 2) + 2], mx, -SCALE, None, ALU.mult).then_inc(sem("row_max"), 1)

            def mix_branches(i, g):
                dve.wait_ge(hold_full, hold[("o", i, g)] + 1)
                evac(dve, ("S", i * 8 + g * 4 + 3))
                step(v.reciprocal(rc12, DEN[:, i, g * 12:(g + 1) * 12]))
                step(tt_(rc12, rc12, gates[:, i, g * 12:(g + 1) * 12], ALU.mult))
                tt_(osum.rearrange("p (n d) -> p n d", n=12), HOLD[:, 0:768].rearrange("p (n d) -> p n d", n=12),
                    bc(rc12, 2, HD), ALU.mult).then_inc(hold_free, 1)
                dve.wait_ge(hold_free, hold[("o", i, g)] + 1)
                step(v.tensor_reduce(otok[:, i, g * 256:(g + 1) * 256].rearrange("p (r d) -> p r d", r=NR),
                                     osum.rearrange("p (r b d) -> p r d b", r=NR, b=3), AX, ALU.add))

            row_max(0)
            row_max(1)
            for n in range(len(heads)):
                if n + 2 < len(heads):
                    row_max(n + 2)
                if n and n % 4 == 0:
                    mix_branches((n - 1) // 8, (n - 1) // 4 % 2)
            mix_branches(QT - 1, 1)

            for rd in range(2):
                key = ("sms", rd)
                full(dve, key)
                ps = slot(key)
                step(cp(cS[:, 0:NCB], ps[:, 0:NCB]))
                if rd == 0:
                    step(v.memset(cPn, 0.0))
                step(tt_(sS[:, 1024:1056], ps[:, 64:96], cst(f"snew{rd}"), ALU.add))
                tt_(wS[:, 512:544], ps[:, 96:128], cst(f"snew{rd}"), ALU.add).then_inc(freed(key), 1)
                step(v.tensor_reduce(smx1[:, 0:1], cS[:, 0:NCB], AX, ALU.max))
                ts(snm1[:, 0:1], smx1[:, 0:1], -SCALE, None, ALU.mult).then_inc(sem("smp_cmp_in"), 1)
                dve.wait_ge(sem("smp_cmp_exp"), rd + 1)
                step(v.reciprocal(coef[:, 0:1], sden[:, 0:1]))
                ts(cPn, cPn, coef[:, 0:1], None, ALU.mult).then_inc(sem("smp_cmp"), 1)
                key = ("imp", rd)
                full(dve, key)
                v.tensor_reduce(imp, slot(key)[:, 0:64].rearrange("p (j c) -> p j c", c=4), AX,
                                ALU.add).then_inc(freed(key), 1)
                evac(dve, key)
                step(v.tensor_reduce(mn[:, 0:1], imp[:, 1:15], AX, ALU.min))
                step(stt(eqj[:, 0:14], imp[:, 1:15], mn[:, 0:1], cst("jidx")[:, 1:15], ALU.is_le, ALU.mult))
                step(v.tensor_reduce(mn[:, 1:2], eqj[:, 0:14], AX, ALU.max))
                step(ts(drop, cst("jidx"), mn[:, 1:2], NEG, ALU.is_equal, ALU.mult))
                dve.wait_ge(hold_full, hold[("Ss", rd)] + 1)
                for q in range(2):
                    ins = tt_(sS[:, q * 512:(q + 1) * 512].rearrange("p (j k e) -> p j k e", j=4, k=16),
                              HOLD[:, q * 512:(q + 1) * 512].rearrange("p (j k e) -> p j k e", j=4, k=16),
                              bc(drop, 2, 8).unsqueeze(1).broadcast_to([P, 4, 16, 8]), ALU.add)
                    if q:
                        ins.then_inc(hold_free, 1)
                        dve.wait_ge(hold_free, hold[("Ss", rd)] + 1)
                    else:
                        step(ins)
                step(v.tensor_reduce(smx1[:, 1:2], sS, AX, ALU.max))
                ts(snm1[:, 1:2], smx1[:, 1:2], -SCALE, None, ALU.mult).then_inc(sem("smp_sel_in"), 1)
                dve.wait_ge(hold_full, hold[("Sw", rd)] + 1)
                cp(wS[:, 0:512], HOLD[:, 0:512]).then_inc(hold_free, 1)
                dve.wait_ge(hold_free, hold[("Sw", rd)] + 1)
                w0 = wS[:, 0:512].rearrange("p (j n) -> p j n", j=4)[:, :, 0]
                step(tt_(w0, w0, cst("swin"), ALU.add))
                step(v.tensor_reduce(smx1[:, 2:3], wS, AX, ALU.max))
                ts(snm1[:, 2:3], smx1[:, 2:3], -SCALE, None, ALU.mult).then_inc(sem("smp_win_in"), 1)
                dve.wait_ge(sem("smp_sel"), rd + 1)
                dve.wait_ge(sem("smp_win"), rd + 1)
                dve.wait_ge(sem("gsmp_in"), 16 * 8)
                step(v.reciprocal(coef[:, 1:3], sden[:, 1:3]))
                step(tt_(coef[:, 1:3], coef[:, 1:3], gsmp[:, rd, 1:3], ALU.mult))
                step(cp(coef[:, 0:1], gsmp[:, rd, 0:1]))
                dve.wait_ge(hold_full, hold[("PV", rd)] + 1)
                acc = oacc[:, 0:384].rearrange("p (b d) -> p b d", b=3)
                tt_(acc, HOLD[:, 0:384].rearrange("p (b d) -> p b d", b=3), bc(coef[:, 0:3], 2, P),
                    ALU.mult).then_inc(hold_free, 1)
                dve.wait_ge(hold_free, hold[("PV", rd)] + 1)
                o2, o3 = oacc[:, 384:512], oacc[:, 512:576]
                step(v.tensor_reduce(o2, acc.rearrange("p b d -> p d b"), AX, ALU.add))
                step(ts(o2[:, 0:HD], o2[:, 0:HD], cst("isg")[:, 0:1], None, ALU.mult))
                if rd:
                    dve.wait_ge(sem("smp_o_out"), 16 * 4)
                stt(o3, o2[:, HD:P], cst("isg")[:, 1:2], o2[:, 0:HD], ALU.mult, ALU.add).then_inc(sem("smp_o"), 1)
            dve.wait_ge(sem("smp_o_in"), 16)
            dve.sem_inc(sem("otok_done"), 1)
            dve.wait_ge(sem("nsa_squares"), 1)
            for n, tl in ((P, slice(0, QT)), (NSMP, slice(QT, QT + 1))):
                step(ts(sm5[0:n, tl], ss[0:n, tl], 1.0 / NSAW, EPS, ALU.mult, ALU.add))
                dve.sem_inc(sem("mean_in"), 1)
                refine(rs5[0:n, tl], sm5[0:n, tl], t5[0:n, tl])
                step(tt_(otok[0:n, tl, :], otok[0:n, tl, :], bc(rs5[0:n, tl], 2, NSAW), ALU.mult))
            dve.sem_inc(sem("nsa_normed"), 1)
            for f in range(4):
                key = ("nT", f)
                full(dve, key)
                ts(MX[:, f, :], slot(key)[:, 0:TOK], GV[:, V_NSA + f:V_NSA + f + 1], None,
                   ALU.mult).then_inc(freed(key), 1)
                evac(dve, key)
            dve.sem_inc(sem("dve_phase"), 1)

            dve.wait_ge(sem("act_phase"), 1)
            dve.wait_ge(sem("store_phase"), 1)
            step(v.memset(LK.rearrange("p s t -> p (s t)"), 0.0))
            step(tt_(lb, GV[:, V_LB + 4:V_LB + 8], GV[:, V_LB:V_LB + 4], ALU.subtract))
            dve.sem_inc(sem("lb_in"), 1)
            dve.wait_ge(sem("lb_exp"), 1)
            step(ts(lb, lb, 1.0, None, ALU.add))
            step(v.reciprocal(lb, lb))
            step(ts(lb1, lb, -1.0, 1.0, ALU.mult, ALU.add))
            step(ts(lbn, lb1, -1.0, None, ALU.mult))
            for h in range(HH):
                evac(dve, ("hf", h))
                K, B = hK[:, h, :], hB[:, h, :]
                step(ts(K, K, 1.0, None, ALU.add))
                step(v.reciprocal(K, K))
                ts(B, K, lb1[:, h:h + 1], lb[:, h:h + 1], ALU.mult, ALU.add).then_inc(sem("forget_in"), 1)
                step(ts(K, K, lbn[:, h:h + 1], lb1[:, h:h + 1], ALU.mult, ALU.add))
            for h in range(HH):
                B = hB[:, h, :]
                dve.wait_ge(sem("forget_log"), h + 1)
                v.tensor_tensor_scan(B, cst("reset"), B, 0.0, ALU.mult, ALU.add).then_inc(sem("decay_sum"), 1)
            for h in range(HH):
                key = ("hg", h)
                G = hG[:, h, :]
                dve.wait_ge(sem("out_gate_exp"), h + 1)
                step(ts(G, G, 1.0, None, ALU.add))
                step(v.reciprocal(G, G))
                tt_(two(G), two(G), halves(slot(key)), ALU.mult).then_inc(freed(key), 1)
            for h in range(HH):
                B, K, Q = hB[:, h, :], hK[:, h, :], hQ[:, h, :]
                dve.wait_ge(sem("decay_sum"), HH)
                if h:
                    full(dve, ("klT", h - 1))
                for at, n, w in ((0, QT, P), (SEQ, DB, DS)):
                    b3 = B[:, at:at + n * w].rearrange("p (c w) -> p c w", c=n)
                    k3 = kdec[:, at:at + n * w].rearrange("p (c w) -> p c w", c=n)
                    step(tt_(k3, b3[:, :, w - 1:w].broadcast_to([P, n, w]), b3, ALU.subtract))
                dve.sem_inc(sem("k_decay_in"), 1)
                dve.wait_ge(sem("k_decay_exp"), h + 1)
                tt_(kdec, K, kdec, ALU.mult).then_inc(sem("k_decayed"), 1)
                evac(dve, ("hq", h))
                dve.wait_ge(sem("decay_exp"), h + 1)
                if h:
                    full(dve, ("o", h - 1))
                tt_(qdec, Q, E0, ALU.mult).then_inc(sem("q_decayed"), 1)
                for c in ("hi0", "hi1"):
                    evac(dve, (c, "s"))
                if h:
                    full(dve, ("dSs", h - 1))
                tt_(Vbd[0:NSMP, :].rearrange("p (b e) -> p b e", b=DB),
                    bc(hi[0:NSMP, QT, h * HK:(h + 1) * HK], 1, DB), bc(cst("bsel")[0:NSMP, :], 2, HK),
                    ALU.mult).then_inc(sem("v_diag"), 1)
                if h:
                    dve.wait_ge(sem("hg_stored"), 32 * h)
                key = ("dS", h)
                full(dve, key)
                step(cp(Sst[:, 0, :], slot(key)[:, 0:HK]))
                for c in range(1, QT):
                    ins = stt(Sst[:, c, :], Sst[:, c - 1, :], E0[:, c * P + P - 1:c * P + P],
                              slot(key)[:, c * HK:(c + 1) * HK], ALU.mult, ALU.add)
                    if c == QT - 1:
                        ins.then_inc(freed(key), 1)
                        evac(dve, key)
                    else:
                        step(ins)
                key = ("dSs", h)
                full(dve, key)
                dve.wait_ge(sload[h % 2], 16 * (h // 2 + 1))
                ebl = E0[:, SEQ:TOK].rearrange("p (b t) -> p b t", t=DS)[:, :, DS - 1]
                step(tt_(Snew.rearrange("p (b e) -> p b e", b=DB), S0[:, h % 2, :].rearrange("p (b e) -> p b e", b=DB),
                         bc(ebl, 2, HK), ALU.mult))
                tt_(Snew, Snew, slot(key)[:, :], ALU.add).then_inc(freed(key), 1)
                evac(dve, key)
                dve.sem_inc(sem("states_done"), 1)
                for L in range(len(LEVELS)):
                    x = h * 7 + L
                    if L < 7:
                        w = TOK if LEVELS[L + 1] < DS else SEQ
                        nx = L + 1
                        dve.wait_ge(sem("level_exp"), h * 7 + nx)
                        if nx >= 3:
                            full(dve, ("A", h, nx - 2))
                        y = (h * 7 + nx) % 2
                        tt_(past(LQ[:, y, 0:w], nx), past(Q[:, 0:w], nx), past(LE[:, y, 0:w], nx),
                            ALU.mult).then_inc(sem("levels"), 1)
                        tt_(before(LK[:, y, 0:w], nx), before(K[:, 0:w], nx), before(LE[:, y, 0:w], nx),
                            ALU.mult).then_inc(sem("levels"), 1)
                    key = ("A", h, L)
                    full(dve, key)
                    if L == 0:
                        m = cst("hmask")[:, 0:P]
                        step(tt_(Aacc[0:NSMP, SEQ:TOK], slot(key)[0:NSMP, 512:512 + NSMP], m[0:NSMP, 0:NSMP],
                                 ALU.mult))
                        tt_(Aacc[:, 0:SEQ].rearrange("p (c n) -> p c n", c=QT),
                            slot(key)[:, 0:SEQ].rearrange("p (c n) -> p c n", c=QT), bc(m, 1, QT),
                            ALU.mult).then_inc(freed(key), 1)
                        evac(dve, key)
                        continue
                    m = cst("hmask")[:, P + (L - 1) * P // 2:P + L * P // 2]
                    if LEVELS[L] < DS:
                        ns = NSMP // 2
                        step(tt_(Atmp[0:NSMP, 0:ns], slot(key)[0:NSMP, 512:512 + ns], m[0:NSMP, 0:ns], ALU.mult))
                        acc = past(Aacc[0:NSMP, SEQ:TOK], L)
                        step(tt_(acc, acc, packed(Atmp[0:NSMP, 0:ns], L), ALU.add))
                    tt_(Atmp[:, 0:SEQ // 2].rearrange("p (c n) -> p c n", c=QT),
                        slot(key)[:, 0:SEQ // 2].rearrange("p (c n) -> p c n", c=QT), bc(m, 1, QT),
                        ALU.mult).then_inc(freed(key), 1)
                    evac(dve, key)
                    acc = past(Aacc[:, 0:SEQ], L)
                    step(tt_(acc, acc, packed(Atmp[:, 0:SEQ // 2], L), ALU.add))
                dve.sem_inc(sem("scores_done"), 1)
                key = ("osum", h)
                inverse_rms(key, TOK, HK, Atmp)
                key = ("o", h)
                stt(MX[:, 4 + h, :], slot(key)[:, 0:TOK], GV[:, V_HG + h:V_HG + h + 1], RSTD[:, :], ALU.mult,
                    ALU.mult).then_inc(freed(key), 1)
                evac(dve, key)
                evac(dve, ("hg", h))
                tt_(MX[:, 4 + h, :], MX[:, 4 + h, :], hG[:, h, :], ALU.mult).then_inc(sem("hg_out"), 1)
            dve.wait_ge(sem("hg_out"), HH)
            dve.sem_inc(sem("dve_phase"), 1)

            def residual(name, n_norm):
                for m in range(KT):
                    key = (name, m)
                    full(dve, key)
                    tt_(two(X[:, m, :]), two(X[:, m, :]), halves(slot(key)), ALU.add).then_inc(freed(key), 1)
                    evac(dve, key)
                    square(m)
            residual("wout", 1)

            dve.wait_ge(sem("store_phase"), 2)
            for n in range(2):
                evac(dve, ("mT", n))
                x = mnT[:, 4 * n:4 * n + 4, :]
                tt_(mkT[:, 4 * n:4 * n + 4, :], x, x, ALU.mult).then_inc(sem("mem_squares"), 1)
            key = ("msum",)
            r = RSTD[:, 0:MEM]
            inverse_rms(key, MEM, DM, xP[:, 0, 0:MEM])
            for k in range(KT):
                step(stt(mnT[:, k, :], mnT[:, k, :], GV[:, V_MEM + k:V_MEM + k + 1], r, ALU.mult, ALU.mult))
            dve.sem_inc(sem("mem_normed"), 1)
            normalize(1)

            for i in range(QT):
                key = ("cS", i)
                full(dve, key)
                x = slice(4 * (i % 2), 4 * (i % 2) + 4)
                if i >= 2:
                    dve.wait_ge(sem("cross_probs"), i - 1)
                step(v.tensor_reduce(xmx[:, x], slot(key)[:, :].rearrange("p (h n) -> p h n", h=CH), AX, ALU.max))
                ts(xnm[:, x], xmx[:, x], -CSCALE, None, ALU.mult).then_inc(sem("cross_max"), 1)
                evac(dve, key)
                step(v.reciprocal(xden[:, x], xden[:, x]))
                xp = xP[:, i % 2, :].rearrange("p (h n) -> p h n", h=CH)
                tt_(xp, xp, bc(xden[:, x], 2, MEM), ALU.mult).then_inc(sem("cross_probs"), 1)
                if i == 0:
                    dve.wait_ge(sem("cross_cleared"), 1)
                    for n in range(KT):
                        evac(dve, ("wq", n))
                        for b2 in range(2):
                            at = 16 * b2 + 4 * (n // 2)
                            step(cp(qbc[:, n, b2::2, at:at + DS],
                                    QC[:, n, SEQ:TOK].rearrange("p (b t) -> p b t", b=DB)[:, b2::2, :]))
                    dve.sem_inc(sem("cross_diag"), 1)
            dve.wait_ge(hold_full, hold[("cS",)] + 1)
            step(v.tensor_reduce(xmx[:, 0:1], HOLD[:, 0:MEM], AX, ALU.max))
            ts(msc[:, 0:1], xmx[:, 0:1], -CSCALE, None, ALU.mult).then_inc(sem("cross_smp_max"), 1)
            dve.wait_ge(hold_free, hold[("cS",)] + 1)
            step(v.reciprocal(msc[:, 1:2], msc[:, 1:2]))
            ts(yP, yP, msc[:, 1:2], None, ALU.mult).then_inc(sem("cross_smp"), 1)
            dve.wait_ge(sem("cross_smp"), 1)
            residual("wo", 2)
            dve.sem_inc(sem("dve_phase"), 1)
            normalize(2)
            dve.wait_ge(sem("act_phase"), 2)
            dve.wait_ge(sem("store_phase"), 3)
            for j in range(FT):
                t = ftmp[:, j % 2, :]
                dve.wait_ge(sem("gate_exp"), j + 1)
                step(ts(t, t, 1.0, None, ALU.add))
                step(v.reciprocal(t, t))
                key = ("ffg", j)
                tt_(two(t), two(t), halves(slot(key)), ALU.mult).then_inc(freed(key), 1)
                evac(dve, key)
                key = ("ffu", j)
                full(dve, key)
                tt_(two(hid[:, j, :]), two(t), halves(slot(key)), ALU.mult).then_inc(sem("hidden"), 1)
                dve.wait_ge(sem("hidden"), j + 1)
                dve.sem_inc(freed(key), 1)
            residual("ffd", 3)
            normalize(3)

        @block.gpsimd
        def _(pool):
            g = nc.gpsimd
            for n in range(2):
                for b in range(DB):
                    rows = (WIN - DS) * GW
                    src = a["cache_win_" + "kv"[n]].rearrange("l b t g d -> (l b) (t g d)")[b, DS * GW:WIN * GW]
                    dst = out["s_win_" + "kv"[n]].rearrange("l b t g d -> (l b) (t g d)")[b, 0:rows]
                    g.dma_start(dst.rearrange("(a n) -> a n", a=16),
                                src.rearrange("(a n) -> a n", a=16)).then_inc(sem("win_out"), 16)
            g.memset(ones[:, :], 1.0).then_inc(sem("ones"), 1)
            gather_list = [k for k in raws if gathered_tile(k)]
            gathered = [0]

            def gather(count):
                for name in gather_list[gathered[0]:gathered[0] + count]:
                    n = raws[name]
                    raw_free(pool, n)
                    if name[0] == "c":
                        src, b = a["cache_cmp_" + "kv"[name[1]]], name[2]
                    else:
                        src, b = a["cache_sel_" + name[0][1]], 4 * name[1] + name[2]
                    g.indirect_dma_start(RAW[:, n % RAWS, :], None, src.rearrange(
                        "l n (r t) g d -> (l n r) (t g d)", r=PROWS), bass.IndirectOffsetOnAxis(
                            PGROW[:, b:b + 1], axis=0)).then_inc(rgather[n % RAWS], 16)
                gathered[0] += count
            pool.wait_ge(psum_full, ring[("xT", KT - 1)] + 1)
            g.memset(qbd.rearrange("p k n -> p (k n)"), 0.0).then_inc(sem("cleared"), 1)
            g.memset(qtok[:, QT, :], 0.0).then_inc(sem("cleared"), 1)
            g.memset(ksw[:, QT, :, :].rearrange("p s d -> p (s d)"), 0.0).then_inc(sem("cleared"), 1)
            pool.wait_ge(sem("pages_in"), 16 * NPAGE)
            pool.wait_ge(sem("cst_in"), 16)
            g.tensor_scalar(PGROW[:, :], PGID[:, :], float(PROWS), cst("page_row"), ALU.mult,
                            ALU.add).then_inc(sem("page_rows"), 1)
            pool.wait_ge(sem("page_rows"), 1)
            gather(RAWS)

            def flat(name):
                return out[name].rearrange("l b t g d -> (l b t) (g d)")

            def store_rows(kind, src, s):
                g.dma_start(flat("p_" + kind).rearrange("(t p) c -> p t c", p=P), src[:, 0:QT]).then_inc(s, 16)
            counts = {"kv_out": 0}

            def kv_store(kind, src):
                store_rows(kind, src, sem("kv_out"))
                counts["kv_out"] += 16
                if kind[:3] != "win":
                    g.dma_start(flat("s_" + kind), src[0:NSMP, QT]).then_inc(sem("kv_out"), 16)
                    counts["kv_out"] += 16
                else:
                    for b in range(DB):
                        at = b * WIN + WIN - DS
                        g.dma_start(flat("s_" + kind)[at:at + DS, :],
                                    src[DS * b:DS * b + DS, QT]).then_inc(sem("kv_out"), 16)
                        counts["kv_out"] += 16
            evac(pool, ("cmp", "p"))
            for n in range(2):
                store_rows("cmp_" + "kv"[n], ckcv[:, :, n * GW:(n + 1) * GW], sem("cmp_rows_out"))
            evac(pool, ("cmp", "s"))
            for n in range(2):
                g.dma_start(flat("s_cmp_" + "kv"[n]), ckcv[0:NSMP, QT, n * GW:(n + 1) * GW]).then_inc(sem("kv_out"), 16)
                counts["kv_out"] += 16
            for s, name in enumerate(("sel", "win")):
                evac(pool, (name, "p"))
                evac(pool, (name, "s"))
                kv_store(name + "_v", vtok[:, :, s, :])
            pool.wait_ge(sem("k_rotated"), 1)
            for s, name in enumerate(("sel", "win")):
                kv_store(name + "_k", ksw[:, :, s, :])
            pool.wait_ge(sem("gates_done"), 1)
            g.dma_start(scr_g, gates[0:NSMP, QT, :]).then_inc(sem("gsmp_out"), 16)
            pool.wait_ge(sem("gsmp_out"), 16)
            for b in range(DB):
                rd, q = b // 4, 32 * (b % 4)
                g.dma_start(gsmp[q:q + 32, rd, :],
                            scr_g[DS * b:DS * b + DS, :].rearrange("t (h n) -> h t n", h=NH)).then_inc(sem("gsmp_in"), 16)
            gather(16 - RAWS)
            pool.wait_ge(sem("kv_out"), counts["kv_out"])
            pool.wait_ge(sem("cmp_rows_out"), 32)
            pool.sem_inc(sem("t_stored"), 1)
            gather(12)

            def samples_out(rd):
                pool.wait_ge(sem("smp_o"), rd + 1)
                for b in range(4):
                    t0 = 16 * rd + 4 * b
                    g.dma_start(scr_o[t0:t0 + DS, :].rearrange("t (h d) -> h t d", h=NH),
                                oacc[32 * b:32 * b + 32, 512:576]).then_inc(sem("smp_o_out"), 16)
            samples_out(0)
            gather(4)
            samples_out(1)
            pool.wait_ge(sem("smp_o_out"), 16 * DB)
            g.dma_start(otok[0:NSMP, QT, :], scr_o).then_inc(sem("smp_o_in"), 16)
            pool.sem_inc(sem("store_phase"), 1)
            for h in range(HH):
                pool.wait_ge(sem("decay_sum"), h + 1)
                for L in range(1, len(LEVELS)):
                    x = h * 7 + L
                    n = TOK if LEVELS[L] < DS else SEQ
                    w = 2 * LEVELS[L]
                    if x > 2:
                        pool.wait_ge(sem("level_exp"), x - 2)
                    b3 = hB[:, h, 0:n].rearrange("p (k w) -> p k w", w=w)
                    d3 = LD[:, x % 2, 0:n].rearrange("p (k w) -> p k w", w=w)
                    hw = w // 2
                    ref = b3[:, :, hw - 1:hw].broadcast_to([P, n // w, hw])
                    g.tensor_tensor(d3[:, :, 0:hw], b3[:, :, 0:hw], ref, ALU.subtract).then_inc(sem("level_in"), 1)
                    g.tensor_tensor(d3[:, :, hw:w], ref, b3[:, :, hw:w], ALU.subtract).then_inc(sem("level_in"), 1)
                pool.wait_ge(sem("states_done"), h + 1)
                g.dma_start(out["p_hgrn"][0, 0, h], Sst[:, QT - 1, :]).then_inc(sem("hg_stored"), 16)
                g.dma_start(out["s_hgrn"][0, :, h].rearrange("b d e -> d b e"),
                            Snew.rearrange("p (b e) -> p b e", b=DB)).then_inc(sem("hg_stored"), 16)
            pool.wait_ge(sem("hg_stored"), 32 * HH)
            pool.sem_inc(sem("store_phase"), 1)
            pool.wait_ge(sem("dve_phase"), 2)
            g.memset(qbc.rearrange("p k b n -> p (k b n)"), 0.0).then_inc(sem("cross_cleared"), 1)
            for c, name, src in (("wk", "p_mem_k", mst), ("wv", "p_mem_v", mv)):
                for n in range(4):
                    evac(pool, (c, n))
                g.dma_start(out[name].rearrange("l b (m p) h d -> p (l b m) (h d)", p=P), src).then_inc(sem("mem_out"), 16)
            pool.wait_ge(sem("mem_out"), 32)
            pool.sem_inc(sem("store_phase"), 1)
            pool.wait_ge(sem("win_out"), 16 * 2 * DB)

        @block.sync
        def _(sp):
            def cols(name, at, n):
                return a[name][0, :, at:at + n].rearrange("(k p) n -> p k n", p=P)

            src = {("cmp",): cols("w_in", C_CK, 256), ("sel",): cols("w_in", C_SK, 256),
                   ("win",): cols("w_in", C_WK, 256), ("gate",): cols("w_in", C_G, 24)}
            for n in range(2):
                src[(f"q{n}",)] = cols("w_in", C_Q + 256 * n, 256)
                src[(f"hi{n}",)] = cols("w_in", C_HI + 256 * n, 256)
                src[("w1", n)] = a["cmp_w1_" + "kv"[n]][0].rearrange("(k p) n -> p k n", p=P)
                for c, at in (("hf", C_HF), ("hq", C_HQ), ("hg", C_HG)):
                    src[(c, n)] = cols("w_in", at + 256 * n, 256)
            for n in range(4):
                for c, name in (("wout", "w_out"), ("wk", "ca_wk"), ("wv", "ca_wv"), ("wq", "ca_wq"), ("wo", "ca_wo")):
                    src[(c, n)] = cols(name, 256 * n, 256)
                for k in range(3):
                    r1 = min(1024 * (k + 1), FFN)
                    src[("ffd", n, k)] = a["ffn_w_down"][0, 1024 * k:r1, 256 * n:256 * n + 256].rearrange(
                        "(k p) n -> p k n", p=P)
            for n in range(FT // 2):
                src[("ffg", n)] = cols("ffn_w_gate", 256 * n, 256)
                src[("ffu", n)] = cols("ffn_w_up", 256 * n, 256)
            order = list(chunks)

            def weights(name):
                n = chunks[name]
                if n >= WRING:
                    sp.wait_ge(psum_full, chunk_last[order[n - WRING]] + 1)
                s = src[name]
                kk, w = s.shape[1], s.shape[2]
                sp.dma_start(W[:, n % WRING, 0:kk * w].rearrange("p (k n) -> p k n", k=kk), s).then_inc(
                    wload[n % WRING], 16)

            def raw_tile(name):
                n = raws[name]
                slot_, s = RAW[:, n % RAWS, :], rload[n % RAWS]
                kind = name[0]
                if kind == "c" and name[2] == 8:
                    raw_free(sp, n)
                    sp.wait_ge(sem("cmp_rows_out"), 32)
                    sp.dma_start(slot_[0:SEQ // 8, :], out["p_cmp_" + "kv"[name[1]]].rearrange(
                        "l b (p t) g d -> (l b p) (t g d)", t=8)).then_inc(s, 16)
                elif kind in ("wk", "wv"):
                    raw_free(sp, n)
                    b = 4 * name[1] + name[2]
                    sp.dma_start(slot_[:, 0:512], a["cache_win_" + kind[1]][0, b].rearrange(
                        "(p t) g d -> p (t g d)", t=4)).then_inc(s, 16)

            sp.dma_start(XST[:, 0:QT, :], a["x_prompt"][0].rearrange("(t p) n -> p t n", p=P)).then_inc(sem("x_in"), 16)
            sp.dma_start(XST[0:NSMP, QT, :], a["x_sample"].rearrange("b t n -> (b t) n")).then_inc(sem("x_in"), 16)
            sp.dma_start(CST[:, :], a["tables"]).then_inc(sem("cst_in"), 16)
            for name, at, rows in (("norm_mix", V_MIX, 8), ("norm_ca", V_CA, 8), ("norm_mem", V_MEM, 8),
                                   ("norm_ffn", V_FFN, 8), ("nsa_out_norm", V_NSA, 4), ("hg_out_norm", V_HG, 4)):
                sp.dma_start(VECS[at:at + rows, :], a[name][0].rearrange("(k p) -> k p", p=P)).then_inc(sem("vec_in"), 16)
            sp.dma_start(VECS[V_FIN:V_FIN + 8, :], a["final_norm"].rearrange("(k p) -> k p", p=P)).then_inc(sem("vec_in"), 16)
            sp.dma_start(VECS[V_LB:V_LB + 8, :], a["hg_lb_logits"].rearrange("l (k p) -> (l k) p", p=P)).then_inc(
                sem("vec_in"), 16)
            for n in range(2):
                sp.dma_start(VECS[V_PEK + 16 * n:V_PEK + 16 * n + 16, :], a["cmp_pe_" + "kv"[n]][0].rearrange(
                    "(k t) d -> k (t d)", t=2)).then_inc(sem("vec_in"), 16)
                sp.dma_start(w2[:, n, :], a["cmp_w2_" + "kv"[n]][0]).then_inc(sem("w2_in"), 16)
            for c in order[0:4]:
                weights(c)
            for n in range(NPAGE):
                sp.dma_start(PGID[n * PROWS:(n + 1) * PROWS, :],
                             bc(a["page_table"][:, n], 0, PROWS),
                             allow_slow_non_contiguous=True).then_inc(sem("pages_in"), 16)
            for n in range(RAWS):
                raw_tile(list(raws)[n])
            for c in order[4:8]:
                weights(c)
            for n in range(RAWS, len(raws)):
                if n == 9 + 5:
                    weights(order[8])
                raw_tile(list(raws)[n])
                if n == 24:
                    for c in order[9:12]:
                        weights(c)
            for c in order[12:14]:
                weights(c)

            def state(h):
                if h >= 2:
                    full(sp, ("o", h - 2))
                    sp.wait_ge(sem("states_done"), h - 1)
                sp.dma_start(S0[:, h % 2, :].rearrange("p (b e) -> p b e", b=DB),
                             a["state_hgrn"][0, :, h].rearrange("b d e -> d b e")).then_inc(sload[h % 2], 16)
            full(sp, ("nT", 3))
            for e in ("act_phase", "dve_phase", "store_phase"):
                sp.wait_ge(sem(e), 1)
            state(0)
            state(1)
            for c in order[14:20]:
                weights(c)
            state(2)
            state(3)
            for e in ("dve_phase", "store_phase"):
                sp.wait_ge(sem(e), 2)
            sp.dma_start(mst, a["mem_prompt"][0].rearrange("(m p) n -> p m n", p=P)).then_inc(sem("mem_in"), 16)

            def cross(x):
                if 3 <= x < DB + 3:
                    full(sp, ("cx", x - 3, 1))
                elif x >= DB + 3:
                    sp.wait_ge(sem("cross_values_used"), x - 3 - DB + 1)
                src_ = a["cache_mem_" + ("k" if x < DB else "v")][0, x % DB]
                sp.dma_start(RC[:, x % 3, :], src_.rearrange("(p j) h d -> p (j h d)", j=2)).then_inc(cload[x % 3], 16)
            for x in range(3):
                cross(x)
            last_q = order.index(("wo", 0))
            for c in order[20:last_q]:
                weights(c)
            for x in range(3, 2 * DB):
                cross(x)
                if x == 4:
                    for c in order[last_q:last_q + 4]:
                        weights(c)
            for c in order[last_q + 4:]:
                weights(c)
            for tt in range(QT + 1):
                evac(sp, ("y", tt))
                if tt < QT:
                    dst, n = out["y_prompt"][0, tt * P:(tt + 1) * P, :], P
                else:
                    dst, n = out["y_sample"].rearrange("b t n -> (b t) n"), NSMP
                sp.dma_start(dst, ymid[0:n, tt % 2, :]).then_inc(sem(f"y_out{tt % 2}"), 16)
            sp.wait_ge(sem("y_out0"), 48)
            sp.wait_ge(sem("y_out1"), 32)


_OUTS = [("y_prompt", (1, SEQ, DM)), ("y_sample", (DB, DS, DM))]
_OUTS += [(f"p_{k}_{x}", (1, 1, SEQ, NG, HD)) for k in ("cmp", "sel", "win") for x in "kv"]
_OUTS += [("p_hgrn", (1, 1, HH, HK, HK)), ("p_mem_k", (1, 1, MEM, CH, CD)), ("p_mem_v", (1, 1, MEM, CH, CD))]
_OUTS += [(f"s_{k}_{x}", (1, DB, DS, NG, HD)) for k in ("cmp", "sel") for x in "kv"]
_OUTS += [(f"s_win_{x}", (1, DB, WIN, NG, HD)) for x in "kv"]
_OUTS += [("s_hgrn", (1, DB, HH, HK, HK))]


def kernel(**inputs):
    import concourse.bacc as bacc
    from concourse.bass_utils import run_bass_kernel_spmd

    nc = bacc.Bacc("TRN2", target_bir_lowering=False, num_devices=1)
    arrays, a, out = {}, {}, {}
    cat, tables = constants()
    for name, x in list(inputs.items()) + [("tables", tables)]:
        x = np.ascontiguousarray(x)
        arrays[f"in_{name}"] = x
        a[name] = nc.dram_tensor(f"in_{name}", x.shape, mybir.dt.from_np(x.dtype), kind="ExternalInput").ap()
    for name, shape in _OUTS:
        out[name] = nc.dram_tensor(f"out_{name}", shape, F32, kind="ExternalOutput").ap()
    build(nc, a, out, cat)
    r = run_bass_kernel_spmd(nc, [arrays], core_ids=[0])
    return tuple(r.results[0][f"out_{name}"] for name, _ in _OUTS)
```

```python
from contextlib import ExitStack

import numpy as np
import concourse.bass as bass
from concourse import mybir

F32 = mybir.dt.float32
F32R = mybir.dt.float32r
I32 = mybir.dt.int32
ALU = mybir.AluOpType
ACT = mybir.ActivationFunctionType
AX = mybir.AxisListType.X

P = 128
DM = 1024
KT = DM // P
SEQ = 512
DB, DS = 8, 4
NSMP = DB * DS
TOK = SEQ + NSMP
HALF = TOK // 2
QT = SEQ // P
PAST, PAGE = 1024, 128
NPAGE = PAST // PAGE
PROWS = P // NPAGE
NH, NG, HD = 8, 2, 64
NR = NH // NG
GW = NG * HD
NSAW = NH * HD
STR = 16
SELB = 64
WIN = 512
CHID = 128
HH, HK = 4, 128
MEM = 256
CH, CD = 4, 256
FFN = 2816
FT = FFN // P
EPS = 1e-6
NEG = -1e30
SCALE = HD ** -0.5
CSCALE = CD ** -0.5
CSEG = PAST // STR
NCB = CSEG - 1
PSEG = SEQ // STR
NPB = PSEG - 1
C_Q, C_G, C_CK, C_SK, C_WK, C_HQ, C_HF, C_HI, C_HG = 0, 512, 536, 792, 1048, 1304, 1816, 2328, 2840
LEVELS = [0, 1, 2, 4, 8, 16, 32, 64]
WRING, WSLOT = 2, KT * 256
ARENA = 27700
RAWS, XKS = 4, 2
ROWV = 88
V_MIX, V_CA, V_MEM, V_FFN, V_FIN, V_NSA, V_HG, V_LB, V_PEK, V_PEV = 0, 8, 16, 24, 32, 40, 44, 48, 56, 72


def constants():
    f = np.float32
    rows = np.arange(P)
    parts = {}
    parts["ident"] = np.eye(P)
    parts["causal"] = np.where(rows[None, :] <= rows[:, None], 0.0, NEG)
    t = np.arange(QT)[None, :, None] * P + rows[:, None, None]
    ok = (np.arange(NPB) * STR + 2 * STR - 1)[None, None, :] <= t
    parts["cadd"] = np.where(ok, 0.0, NEG).reshape(P, -1)
    parts["cmul"] = ok.astype(f).reshape(P, -1)
    s, u = rows[:, None], rows[None, :]

    def level(s, u, L):
        if L == 0:
            return s == u
        return (s // (2 * L) == u // (2 * L)) & (s % (2 * L) < L) & (u % (2 * L) >= L)
    parts["hmask"] = np.concatenate([level(s, u[:, rows % (2 * L) >= L] if L else u, L) for L in LEVELS], 1)
    reset = np.ones(TOK)
    reset[0:SEQ:P] = 0
    reset[SEQ::DS] = 0
    parts["reset"] = np.tile(reset, (P, 1))
    pos = np.concatenate([np.arange(SEQ), PAST + np.tile(np.arange(DS), 32)]).reshape(QT + 1, P).T
    inv = f(500000.0) ** (-np.arange(8, dtype=f) / f(8))
    ang = pos.astype(f)[:, :, None] * inv
    parts["rope"] = np.concatenate([np.cos(ang), np.sin(ang)], -1).reshape(P, -1)
    b4, t4 = rows // 32, rows % 4
    kb, kt = np.arange(NSMP) // DS, np.arange(NSMP) % DS
    for r in range(2):
        new = (kb[None, :] == 4 * r + b4[:, None]) & (kt[None, :] <= t4[:, None])
        parts[f"snew{r}"] = np.where(new, 0.0, NEG)
    parts["swin"] = np.where(np.arange(4)[None, :] > t4[:, None], 0.0, NEG)
    grp = b4 * 8 + (rows % 32 // 16) * 4 + t4
    parts["gsum"] = grp[:, None] == grp[None, :]
    parts["jidx"] = np.tile(np.arange(16), (P, 1))
    parts["isg"] = np.stack([rows % 32 // 16 == 0, rows % 32 // 16 == 1], 1)
    parts["page_row"] = rows[:, None] % PROWS
    parts["bsel"] = (rows[:, None] // DS == np.arange(DB)[None, :])
    at, cols = {}, []
    n = 0
    for k, v in parts.items():
        at[k] = (n, v.shape[1])
        n += v.shape[1]
        cols.append(v.astype(f))
    return at, np.ascontiguousarray(np.concatenate(cols, 1), dtype=f)


def plan():
    ring, last, chunks = [], {}, []
    splits, free, signalled = [], [], [0]

    def item(*n):
        ring.append(n)

    def chunk(*n):
        chunks.append(n)

    def used(*n):
        last[n] = len(ring) - 1

    def half(*n, key=None):
        if key is None:
            signalled[0] += 1
        splits.append(n)
        free.append(("item", key) if key else ("signal", signalled[0]))

    def by_feature(c, n):
        chunk(c, n)
        for m in range(2):
            item(c, 2 * n + m)
            half(c, n, m, key=(c, 2 * n + m))
    item("vec")
    for k in range(KT):
        item("xT", k)
    item("sum", 0)
    for c in ("cmp", "sel", "win", "gate", "q0", "q1"):
        chunk(c)
        item(c, "p")
        if c != "gate":
            item(c, "s")
            half(c, 0)
            half(c, 1, key=(c, "s"))
        else:
            half(c, 0, key=(c, "p"))
        if c == "q0":
            item("gateT")
    for s in range(2):
        item("kT", s)
    for rot in range(2):
        for r in range(NR):
            item("qT", rot, r)
    seqs = [(g, j) for g in range(2) for j in range(4)] + [(2, 0)]
    for kv in range(2):
        chunk("w1", kv)
        item("pe", kv)
        for n in range(len(seqs)):
            item("xk", kv, n)
            if kv and n == 1:
                item("kvc", 0, 2)
            if kv and n == 3:
                item("pcs")
            if n == 7:
                item("kvc", kv, 0)
        item("kvc", kv, 1)
        used("w1", kv)
    heads = [(i, g, r) for i in range(QT) for g in range(NG) for r in range(NR)]
    item("S", 0)
    item("kvc", 1, 2)
    item("S", 1)
    for n in range(len(heads)):
        if n % 8 == 0:
            item("PTc", n // 8)
        item("PT", n)
        if n + 2 < len(heads):
            item("S", n + 2)
    for rd in range(2):
        item("sms", rd)
        item("imp", rd)
        for b in range(4):
            item("skT", rd, b)
        for b in range(4):
            item("wkT", rd, b)
        item("sPT", rd, 0)
        item("sPT", rd, 1)
    for c in ("hi0", "hi1"):
        chunk(c)
        item(c, "p")
        item(c, "s")
        half(c, 0)
        half(c, 1, key=(c, "s"))
    for c in ("hf", "hq", "hg"):
        for n in range(2):
            by_feature(c, n)
    for f in range(4):
        item("nT", f)
    for h in range(HH):
        for n in ("klT", "dS", "dSs"):
            item(n, h)
        for L in range(len(LEVELS)):
            item("A", h, L)
        item("o", h)
        item("osum", h)
    for n in range(4):
        by_feature("wout", n)
    for n in range(2):
        item("mT", n)
    item("msum")
    item("sum", 1)
    for c in ("wk", "wv"):
        for n in range(4):
            chunk(c, n)
            item(c, n)
            half(c, n, 0)
            half(c, n, 1, key=(c, n))
    for n in range(2):
        item("mkT", n)
    for n in range(4):
        by_feature("wq", n)
    item("cS", 0)
    item("cS", 1)
    for i in range(QT):
        item("cPT", i)
        item("cO", i)
        if i + 2 < QT:
            item("cS", i + 2)
    for b in range(DB):
        for n in range(2):
            item("cx", b, n)
    item("csPT")
    item("csO")
    for n in range(4):
        by_feature("wo", n)
    item("sum", 2)
    for n in range(FT // 2):
        by_feature("ffg", n)
        by_feature("ffu", n)
    for n in range(4):
        item("ffd", 2 * n)
        item("ffd", 2 * n + 1)
        for k in range(3):
            chunk("ffd", n, k)
            for m in range(2):
                half("ffd", n, k, m, key=("ffd", 2 * n + m) if k == 2 else None)
    item("sum", 3)
    for tt in range(QT + 1):
        item("y", tt)
    hold = [("h", kv, g) for kv in range(2) for g in range(3)] + [("o", i, g) for i in range(QT) for g in range(NG)]
    for rd in range(2):
        hold += [("Ss", rd), ("Sw", rd), ("PV", rd)]
    hold += [("cS",), ("cO",)]
    raws = [("c", kv, n) for kv in range(2) for n in range(len(seqs))]
    for rd in range(2):
        raws += [(k, rd, b) for k in ("sk", "wk", "sv", "wv") for b in range(4)]
    return ({n: i for i, n in enumerate(ring)}, {n: i for i, n in enumerate(hold)}, last,
            {n: i for i, n in enumerate(chunks)}, {n: i for i, n in enumerate(splits)}, free,
            {n: i for i, n in enumerate(raws)}, seqs, heads)


def bc(ap, axis, n):
    ap = ap.unsqueeze(axis)
    shape = list(ap.shape)
    shape[axis] = n
    return ap.broadcast_to(shape)


def build(nc, a, out, cat):
    ring, hold, chunk_last, chunks, splits, split_free, raws, seqs, heads = plan()
    ctx = ExitStack()
    with ctx:
        sems = {}

        def sem(name):
            if name not in sems:
                sems[name] = ctx.enter_context(nc.semaphore(name))
            return sems[name]

        base = {}

        def sb(name, cols):
            base[name] = nc.sbuf_base
            return ctx.enter_context(nc.sbuf_tensor(name, [P, cols], F32))

        RS = [ctx.enter_context(nc.psum_tensor(f"ring{k}", [P, 1024], F32)) for k in range(3)]
        HOLD = ctx.enter_context(nc.psum_tensor("hold", [P, 1024], F32))
        psum_full = sem("psum_full")
        psum_free = [sem(f"psum_free{k}") for k in range(3)]
        hold_full, hold_free = sem("hold_full"), sem("hold_free")

        X = sb("x_res", KT * TOK)[:, :].rearrange("p (k t) -> p k t", k=KT)
        H = sb("h_norm", KT * TOK)[:, :].rearrange("p (k t) -> p k t", k=KT)
        MX = sb("mix", KT * TOK)[:, :].rearrange("p (k t) -> p k t", k=KT)
        W = sb("w_ring", WRING * WSLOT)[:, :].rearrange("p (s n) -> p s n", s=WRING)
        CST = sb("cst", sum(n for _, n in cat.values()))
        GV = sb("vectors", ROWV)
        ones = sb("ones", P)
        small = sb("small", 512)
        PGID = ctx.enter_context(nc.sbuf_tensor("page_of_partition", [P, DB], I32))
        PGROW = ctx.enter_context(nc.sbuf_tensor("page_rows", [P, DB], I32))
        RSTD = sb("rstd", TOK)
        MEAN = sb("mean_square", TOK)

        def cst(name):
            at, n = cat[name]
            return CST[:, at:at + n]
        ident = cst("ident")

        WH, WL = [ctx.enter_context(nc.sbuf_tensor(n, [P, 2048], F32R))[:, :].rearrange("p (s n) -> p s n", s=2)
                  for n in ("weight_hi", "weight_lo")]
        A = sb("arena", ARENA)
        top = {}

        def take(phase, n, first=None):
            at = top.get(phase, 0) if first is None else first
            top[phase] = at + n
            assert top[phase] <= ARENA, (phase, top[phase])
            return A[:, at:at + n]
        XST = take("x", 5 * DM).rearrange("p (t n) -> p t n", t=5)
        VECS = take("x", P)
        top["nsa"] = 0
        otok = take("nsa", 5 * NSAW).rearrange("p (t n) -> p t n", t=5)
        top["hg"] = top["nsa"]
        qT = take("nsa", NR * TOK).rearrange("p (r t) -> p r t", r=NR)
        qrT = take("nsa", NR * TOK).rearrange("p (r t) -> p r t", r=NR)
        kT = take("nsa", 2 * TOK).rearrange("p (s t) -> p s t", s=2)
        vtok = take("nsa", 5 * 2 * GW).rearrange("p (t s d) -> p t s d", t=5, s=2)
        qbd = take("nsa", 512).rearrange("p (k n) -> p k n", k=2)
        gates = take("nsa", 5 * 24).rearrange("p (t n) -> p t n", t=5)
        gsmp = take("nsa", 6).rearrange("p (r n) -> p r n", r=2)
        DEN = take("nsa", 4 * 24).rearrange("p (i n) -> p i n", i=4)
        RAW = take("nsa", RAWS * 1024).rearrange("p (s n) -> p s n", s=RAWS)
        XK = take("nsa", XKS * 1024).rearrange("p (s n) -> p s n", s=XKS)
        HX = take("nsa", 2 * 504).rearrange("p (s n) -> p s n", s=2)
        HT = take("nsa", 504)
        qr0 = XK.rearrange("p s n -> p (s n)").rearrange("p (r t) -> p r t", r=NR)
        gateT = XK[:, 0, 0:TOK]
        kcT = take("nsa", 9 * NCB).rearrange("p (b n) -> p b n", b=9)
        vc = take("nsa", 9 * GW).rearrange("p (b n) -> p b n", b=9)
        w2 = take("nsa", 2 * HD).rearrange("p (k n) -> p k n", k=2)
        T0 = top["nsa"]
        qtok = take("nsa", 5 * NSAW, T0).rearrange("p (t n) -> p t n", t=5)
        ckcv = take("nsa", 5 * 256).rearrange("p (t n) -> p t n", t=5)
        ksw = take("nsa", 5 * 256).rearrange("p (t s d) -> p t s d", t=5, s=2)
        rtmp = [take("nsa", 320) for _ in range(4)]
        Pb = take("nsa", 2 * 1024, T0).rearrange("p (s n) -> p s n", s=2)
        PTb = take("nsa", 2 * 1024).rearrange("p (s n) -> p s n", s=2)
        cP = take("nsa", 992)
        PTc = take("nsa", 2 * 1024).rearrange("p (s n) -> p s n", s=2)
        osum = take("nsa", 768)
        sS = take("nsa", 1056, T0)
        wS = take("nsa", 544)
        cS = take("nsa", 64)
        cPn = take("nsa", 64)
        sPT = take("nsa", 1024)
        mPT = take("nsa", 896)
        oacc = take("nsa", 384 + 128 + 64)
        hi = take("hg", 5 * 512).rearrange("p (t n) -> p t n", t=5)
        hB, hK, hQ, hG = [take("hg", HH * TOK).rearrange("p (h t) -> p h t", h=HH) for _ in range(4)]
        E0, qdec, kdec, gtmp = [take("hg", TOK) for _ in range(4)]
        LD, LE, LQ, LK = [take("hg", 2 * TOK).rearrange("p (s t) -> p s t", s=2) for _ in range(4)]
        kltok = take("hg", 640).rearrange("p (c n) -> p c n", c=5)
        Sst = take("hg", 4 * HK).rearrange("p (c n) -> p c n", c=4)
        S0 = take("hg", 2 * 1024).rearrange("p (s n) -> p s n", s=2)
        Snew = take("hg", 1024)
        Vbd = take("hg", 1024)
        Aacc, Atmp = take("hg", TOK), take("hg", TOK)
        mst = take("ca", 2048).rearrange("p (m n) -> p m n", m=2)
        mnT = take("ca", 2048).rearrange("p (k n) -> p k n", k=KT)
        mkT = take("ca", 2048).rearrange("p (k n) -> p k n", k=KT)
        mv = take("ca", 2048).rearrange("p (m n) -> p m n", m=2)
        QC = take("ca", KT * TOK).rearrange("p (k t) -> p k t", k=KT)
        xp_at = top["ca"]
        xP, xPT = [take("ca", 2048).rearrange("p (s n) -> p s n", s=2) for _ in range(2)]
        qbc = take("ca", 2048).rearrange("p (k b n) -> p k b n", k=KT, b=DB)
        RC = take("ca", 3 * 2048).rearrange("p (s n) -> p s n", s=3)
        KX = take("ca", 2048).rearrange("p (s n) -> p s n", s=2)
        yP = take("ca", 256)
        yPT = take("ca", 512).rearrange("p (j b n) -> p j b n", j=2, b=DB)
        crow = QC.rearrange("p k t -> p (k t)")[:, 0:DM]
        def rounded(name, at, n):
            return nc.alloc_sbuf_tensor_at(name, [P, n], F32R, offset=at)[:, :]
        HIDH, HIDL = [rounded(n, base["arena"] + 4 * FT * TOK * x, FT * TOK).rearrange("p (k t) -> p k t", k=FT)
                      for x, n in enumerate(("hidden_hi", "hidden_lo"))]
        take("ffn", 2 * FT * TOK)
        ftmp, NT = [take("ffn", 2 * TOK).rearrange("p (s t) -> p s t", s=2) for _ in range(2)]
        htmp = take("ffn", TOK)
        ymid = take("y", 2 * 1024).rearrange("p (s n) -> p s n", s=2)
        OPH, OPL = [rounded(n, base[over], KT * TOK).rearrange("p (k t) -> p k t", k=KT)
                    for n, over in (("operand_hi", "h_norm"), ("operand_lo", "mix"))]
        MNH, MNL = [rounded(n, base["arena"] + 4 * at, 2048).rearrange("p (k n) -> p k n", k=KT)
                    for n, at in (("mem_hi", xp_at), ("mem_lo", xp_at + 2048))]
        SQ = [H, QC, QC, H]
        NTS = [A[:, 0:2 * TOK].rearrange("p (s t) -> p s t", s=2), KX[:, :, 0:TOK], NT]
        cb, smx, snm = small[:, 0:2], small[:, 2:6], small[:, 6:10]
        pmx = small[:, 16:48]
        rc12 = small[:, 48:60]
        smx1, snm1, sden, coef = small[:, 60:64], small[:, 64:68], small[:, 68:72], small[:, 72:76]
        imp, drop, eqj, mn = small[:, 80:96], small[:, 96:112], small[:, 112:128], small[:, 128:130]
        ss, rs5, sm5, t5 = small[:, 130:135], small[:, 136:141], small[:, 192:197], small[:, 198:203]
        lb, lbn, lb1 = small[:, 144:148], small[:, 148:152], small[:, 152:156]
        xmx, xnm, xden = small[:, 160:168], small[:, 168:176], small[:, 176:184]
        msc = small[:, 184:186]
        epsb = small[:, 190:191]

        scr_g = nc.dram_tensor("scr_gates", (NSMP, 24), F32, kind="Internal").ap()
        scr_o = nc.dram_tensor("scr_o", (NSMP, NSAW), F32, kind="Internal").ap()

        def wsl(name):
            n = chunks[name]
            return W[:, n % WRING, :], wload[n % WRING], 16 * (n // WRING + 1)
        wload = [sem(f"weights_in{k}") for k in range(WRING)]
        rgather = [sem(f"raw_gathered{k}") for k in range(RAWS)]
        rload = [sem(f"raw_in{k}") for k in range(RAWS)]
        cload = [sem(f"cross_in{k}") for k in range(3)]
        sload = [sem(f"state_in{k}") for k in range(2)]

        def gathered_tile(name):
            return (name[0] == "c" and name[2] < 8) or name[0] in ("sk", "sv")

        def raw_count(name):
            n = raws[name]
            lst = list(raws)
            c = sum(gathered_tile(lst[m]) == gathered_tile(name) for m in range(n % RAWS, n + 1, RAWS))
            return (rgather if gathered_tile(name) else rload)[n % RAWS], 16 * c

        def raw_free(e, n):
            if n < RAWS:
                return
            k = list(raws)[n - RAWS]
            if k[0] == "c":
                full(e, ("xk", k[1], k[2]))
            elif k[0] in ("sk", "wk"):
                full(e, (k[0] + "T", k[1], k[2]))
            else:
                e.wait_ge(sem("values_used"), 8 * k[1] + (4 if k[0] == "wv" else 0) + k[2] + 1)

        def past(ap, L):
            w = 2 * LEVELS[L]
            return ap.rearrange("p (k w) -> p k w", w=w)[:, :, w // 2:w] if L else ap

        def before(ap, L):
            w = 2 * LEVELS[L]
            return ap.rearrange("p (k w) -> p k w", w=w)[:, :, 0:w // 2]

        def packed(ap, L):
            return ap.rearrange("p (k h) -> p k h", h=LEVELS[L])

        BY_ROWS, KH = ("cmp", "sel", "win", "q0", "q1", "hi0", "hi1", "wk", "wv"), KT // 2

        def split_view(name):
            w, s, c = wsl(name[:-1])
            if name[0] in BY_ROWS:
                w = w[:, :].rearrange("p (k n) -> p k n", k=KT)
                return w[:, name[-1] * KH:(name[-1] + 1) * KH], KH, 256, s, c
            kk = FT - 2 * KT if name[0] == "ffd" and name[2] == 2 else KT
            wide, cols = (24, 24) if name[0] == "gate" else (256, P)
            w = w[:, 0:kk * wide].rearrange("p (k n) -> p k n", k=kk)
            return w[:, :, name[-1] * cols:(name[-1] + 1) * cols], kk, cols, s, c

        def half_of(T, x, kk=KT, cols=P):
            return T[:, x % 2, 0:kk * cols].rearrange("p (k n) -> p k n", k=kk)

        def split_slot_free(e, x):
            if x < 2:
                return
            kind, what = split_free[x - 2]
            if kind == "item":
                full(e, what)
            else:
                e.wait_ge(sem("half_used"), what)

        class SplitsLo:
            def __init__(self, e, ops, first):
                self.e, self.ops, self.x = e, ops, first

            def upto(self, x):
                while self.x <= x:
                    w, kk, cols, _, _ = split_view(list(splits)[self.x])
                    self.e.wait_ge(sem("weights_hi"), self.x + 1)
                    self.ops.tensor_tensor(half_of(WL, self.x, kk, cols), w,
                                           half_of(WH, self.x, kk, cols).bitcast(F32), ALU.subtract).then_inc(
                                               sem("weights_lo"), 1)
                    self.x += 1
        DVE_SPLITS = splits[("q1", 1)]

        def full(e, key):
            e.wait_ge(psum_full, ring[key] + 1)

        def evac(e, key):
            e.wait_ge(psum_free[ring[key] % 3], ring[key] // 3 + 1)

        def slot(key):
            return RS[ring[key] % 3]

        def freed(key):
            return psum_free[ring[key] % 3]

        block = ctx.enter_context(nc.Block())

        @block.tensor
        def _(pe):
            mm, tr = nc.tensor.matmul, nc.tensor.transpose

            def open_item(key):
                i = ring[key]
                if i >= 3:
                    pe.wait_ge(psum_free[i % 3], i // 3)
                return RS[i % 3]

            def open_hold(key):
                if hold[key]:
                    pe.wait_ge(hold_free, hold[key])
                return HOLD

            def token_tiles(tt):
                return (tt * P, P) if tt < QT else (SEQ, NSMP)

            def norm_sum(n):
                ps = open_item(("sum", n))
                for k in range(KT):
                    pe.wait_ge(sem("squares"), 8 * n + k + 1)
                    for hf in range(2):
                        last = mm(ps[:, hf * 512:hf * 512 + HALF], ones[:, :], SQ[n][:, k, hf * HALF:(hf + 1) * HALF],
                                  start=(k == 0), stop=(k == KT - 1))
                last.then_inc(psum_full, 1)

            passes = ((0, 0), (0, 1), (1, 0))

            def token_major(name, keys):
                ps = [None, None]
                for m in range(2):
                    x = splits[(name, m)]
                    pe.wait_ge(sem("weights_lo"), x + 1)
                    if name == "cmp":
                        pe.wait_ge(sem("normed"), (m + 1) * KH)
                    w = [half_of(T, x, KH, 256) for T in (WH, WL)]
                    if m == 0:
                        ps[0] = open_item(keys[0])
                    for tt in range(QT):
                        for k in range(KH):
                            for i, (pw, px) in enumerate(passes):
                                last = mm(ps[0][:, tt * 256:(tt + 1) * 256],
                                          (OPH, OPL)[px][:, m * KH + k, tt * P:(tt + 1) * P], w[pw][:, k, :],
                                          start=(m == 0 and k == 0 and i == 0 and tt % 2 == 0),
                                          stop=(m == 1 and k == KH - 1 and i == 2), skip_group_check=True)
                    if m == 1:
                        last.then_inc(psum_full, 1)
                    else:
                        ps[1] = open_item(keys[1])
                    for k in range(KH):
                        for i, (pw, px) in enumerate(passes):
                            last = mm(ps[1][0:NSMP, 0:256], (OPH, OPL)[px][:, m * KH + k, SEQ:TOK], w[pw][:, k, :],
                                      start=(m == 0 and k == 0 and i == 0),
                                      stop=(m == 1 and k == KH - 1 and i == 2))
                    last.then_inc(psum_full if m else sem("half_used"), 1)

            def nothing(k):
                pass

            def split_product(name, ps, rows, xh, xl, ready, first, final, cols=P):
                x = splits[name]
                pe.wait_ge(sem("weights_lo"), x + 1)
                for i, k in enumerate(rows):
                    ready(k)
                    for p, (pw, px) in enumerate(passes):
                        for hf in range(2):
                            last = mm(ps[0:cols, hf * 512:hf * 512 + HALF],
                                      half_of((WH, WL)[pw], x, KT, cols)[:, i, :],
                                      (xh, xl)[px][:, k, hf * HALF:(hf + 1) * HALF],
                                      start=(first and i == 0 and p == 0), stop=(final and i == len(rows) - 1 and p == 2))
                return last

            def feature_major(c, n, ready=nothing):
                for m in range(2):
                    ps = open_item((c, 2 * n + m))
                    split_product((c, n, m), ps, range(KT), OPH, OPL, ready if m == 0 else nothing,
                                  True, True).then_inc(psum_full, 1)

            def normed(n):
                return lambda k: pe.wait_ge(sem("normed"), 8 * n + k + 1)

            pe.wait_ge(sem("cst_in"), 16)
            pe.wait_ge(sem("vec_in"), 16 * 10)
            ps = open_item(("vec",))
            tr(ps[:, 0:ROWV], VECS[0:ROWV, :], ident[0:ROWV, 0:ROWV]).then_inc(psum_full, 1)
            pe.wait_ge(sem("x_in"), 32)
            for k in range(KT):
                ps = open_item(("xT", k))
                for tt in range(QT + 1):
                    at, n = token_tiles(tt)
                    last = tr(ps[:, at:at + n], XST[0:n, tt, k * P:(k + 1) * P], ident[0:n, 0:n])
                last.then_inc(psum_full, 1)
            pe.wait_ge(sem("ones"), 1)
            norm_sum(0)
            for name in ("cmp", "sel", "win"):
                token_major(name, [(name, "p"), (name, "s")])
            split_product(("gate", 0), open_item(("gate", "p")), range(KT), OPH, OPL, nothing, True, True,
                          cols=24).then_inc(psum_full, 1)
            token_major("q0", [("q0", "p"), ("q0", "s")])
            ps = open_item(("gateT",))
            evac(pe, ("gate", "p"))
            for tt in range(QT + 1):
                at, n = token_tiles(tt)
                last = tr(ps[0:n, tt * 24:(tt + 1) * 24], gateT[0:24, at:at + n], ident[0:24, 0:24])
            last.then_inc(psum_full, 1)
            token_major("q1", [("q1", "p"), ("q1", "s")])
            pe.wait_ge(sem("k_rotated"), 1)
            for s in range(2):
                ps = open_item(("kT", s))
                for tt in range(QT + 1):
                    at, n = token_tiles(tt)
                    last = tr(ps[:, at:at + n], ksw[0:n, tt, s, :], ident[0:n, 0:n])
                last.then_inc(psum_full, 1)
            for rot in range(2):
                if rot:
                    pe.wait_ge(sem("q_rotated"), 1)
                else:
                    evac(pe, ("q1", "s"))
                    evac(pe, ("q0", "s"))
                    evac(pe, ("q1", "p"))
                    evac(pe, ("q0", "p"))
                for r in range(NR):
                    ps = open_item(("qT", rot, r))
                    for tt in range(QT + 1):
                        at, n = token_tiles(tt)
                        last = tr(ps[:, at:at + n], qtok[0:n, tt, r * GW:(r + 1) * GW], ident[0:n, 0:n])
                    last.then_inc(psum_full, 1)

            def cmp_transpose(kv, n):
                s, c = raw_count(("c", kv, n))
                pe.wait_ge(s, c)
                raw = RAW[:, raws[("c", kv, n)] % RAWS, :]
                rows = P if n < 8 else SEQ // 8
                ps = open_item(("xk", kv, n))
                for j in range(8):
                    last = tr(ps[:, j * rows:(j + 1) * rows], raw[0:rows, j * GW:(j + 1) * GW],
                              ident[0:rows, 0:rows])
                    if j < 7:
                        yield
                last.then_inc(psum_full, 1)
                yield

            def cmp_hidden(kv, n, between=()):
                between = iter(between)
                g4, j = seqs[n]
                rows, nb = (P, NCB) if n < 8 else (SEQ // 8, NPB)
                w = wsl(("w1", kv))[0].rearrange("p (k n) -> p k n", k=16)
                evac(pe, ("xk", kv, n))
                x = XK[:, n % XKS, 0:8 * rows].rearrange("p (m g s e) -> p m g e s", m=4, g=NG, e=2)
                if j == 0:
                    open_hold(("h", kv, g4))
                o = HOLD[:, j * 2 * NCB:j * 2 * NCB + 2 * nb].rearrange("p (g s) -> p g s", g=NG)
                for k in range(16):
                    half, e, m = k // 8, k // 4 % 2, k % 4
                    last = mm(o, w[:, k, :], x[:, m, :, e, half:half + nb], start=(k == 0), stop=(k == 15))
                    if k == 15 and (j == 3 or n == 8):
                        last.then_inc(hold_full, 1)
                    next(between, None)

            def cmp_out(kv, g4):
                ps = open_item(("kvc", kv, g4))
                pe.wait_ge(sem("cmp_hid"), kv * 3 + g4 + 1)
                cnt, nb = (4, NCB) if g4 < 2 else (1, NPB)
                h = HX[:, g4 % 2, 0:cnt * 2 * nb].rearrange("p (b g n) -> p b g n", b=cnt, g=NG)
                for g in range(NG):
                    if kv == 0:
                        o = ps[g * HD:(g + 1) * HD, 0:cnt * nb].rearrange("p (b n) -> p b n", b=cnt)
                        last = mm(o, w2[:, 0, :], h[:, :, g, :], start=True, stop=True)
                    else:
                        for b in range(cnt):
                            last = mm(ps[0:nb, b * GW + g * HD:b * GW + (g + 1) * HD], h[:, b, g, :], w2[:, 1, :],
                                      start=True, stop=True)
                last.then_inc(psum_full, 1)

            def compressed_scores():
                evac(pe, ("qT", 1, NR - 1))
                evac(pe, ("qT", 1, NR - 2))
                evac(pe, ("qT", 1, NR - 3))
                evac(pe, ("kvc", 0, 2))
                ps = open_item(("pcs",))
                for r in range(NR):
                    for i in range(QT):
                        for g in range(NG):
                            at = g * 512 + (r * QT + i) * NPB
                            last = mm(ps[:, at:at + NPB], qT[g * HD:(g + 1) * HD, r, i * P:(i + 1) * P],
                                      kcT[g * HD:(g + 1) * HD, 8, 0:NPB], start=True, stop=True)
                last.then_inc(psum_full, 1)

            pe.wait_ge(sem("w2_in"), 32)
            for kv in range(2):
                w, s, c = wsl(("w1", kv))
                w = w.rearrange("p (k n) -> p k n", k=16)
                pe.wait_ge(s, c)
                ps = open_item(("pe", kv))
                evac(pe, ("vec",))
                for k in range(16):
                    last = mm(ps[:, 0:1], w[:, k, :], GV[:, V_PEK + 16 * kv + k:V_PEK + 16 * kv + k + 1],
                              start=(k == 0), stop=(k == 15))
                last.then_inc(psum_full, 1)
                for _ in cmp_transpose(kv, 0):
                    pass
                for n in range(1, len(seqs)):
                    cmp_hidden(kv, n - 1, cmp_transpose(kv, n))
                    if kv and n == 1:
                        cmp_out(0, 2)
                    if kv and n == 3:
                        compressed_scores()
                    if n == 7:
                        cmp_out(kv, 0)
                cmp_hidden(kv, 8)
                cmp_out(kv, 1)

            def score(n):
                i, g, r = heads[n]
                if n == 0:
                    pe.wait_ge(sem("q0_copied"), 1)
                if r == 0 and i == 0:
                    pe.wait_ge(sem("q_padded"), g + 1)
                ps = open_item(("S", n))
                for s in range(2):
                    last = mm(ps[:, s * 512:s * 512 + (i + 1) * P], (qrT if g else qr0)[:, r, i * P:(i + 1) * P],
                              kT[:, s, 0:(i + 1) * P], start=True, stop=True)
                last.then_inc(psum_full, 1)

            def probs_t(n):
                i = heads[n][0]
                ps = open_item(("PT", n))
                evac(pe, ("S", n))
                for s in range(2):
                    for k in range(i + 1):
                        at = (s * (i + 1) + k) * P
                        last = tr(ps[:, at:at + P], Pb[:, n % 2, s * 512 + k * P:s * 512 + (k + 1) * P], ident)
                last.then_inc(psum_full, 1)

            def weigh(n):
                i, g, r = heads[n]
                if r == 0:
                    open_hold(("o", i, g))
                if r == 0 and g == 0:
                    evac(pe, ("PTc", i))
                evac(pe, ("PT", n))
                o = HOLD[:, r * 3 * HD:(r + 1) * 3 * HD].rearrange("p (b d) -> p b d", b=3)
                hh = g * NR + r
                mm(o[:, 0], PTc[0:NPB, i % 2, hh * P:(hh + 1) * P], vc[0:NPB, 8, g * HD:(g + 1) * HD],
                   start=True, stop=True)
                for s in range(2):
                    for k in range(i + 1):
                        at = (s * (i + 1) + k) * P
                        last = mm(o[:, 1 + s], PTb[:, n % 2, at:at + P], vtok[:, k, s, g * HD:(g + 1) * HD],
                                  start=(k == 0), stop=(k == i))
                if r == NR - 1:
                    last.then_inc(hold_full, 1)

            score(0)
            cmp_out(1, 2)
            score(1)
            for n in range(len(heads)):
                i = heads[n][0]
                if n % 8 == 0:
                    ps = open_item(("PTc", i))
                    pe.wait_ge(sem("cmp_probs"), 1)
                    for hh in range(NH):
                        last = tr(ps[0:NPB, hh * P:(hh + 1) * P],
                                  cP[:, (hh * QT + i) * NPB:(hh * QT + i + 1) * NPB], ident)
                    last.then_inc(psum_full, 1)
                probs_t(n)
                if n + 2 < len(heads):
                    score(n + 2)
                if n:
                    weigh(n - 1)
            weigh(len(heads) - 1)

            def raw_keys_t(kind, rd, b, tiles):
                s, c = raw_count((kind, rd, b))
                pe.wait_ge(s, c)
                ps = open_item((kind + "T", rd, b))
                for j in range(tiles):
                    last = tr(ps[:, j * P:(j + 1) * P], RAW[:, raws[(kind, rd, b)] % RAWS, j * P:(j + 1) * P], ident)
                last.then_inc(psum_full, 1)

            pe.wait_ge(sem("q_diag"), 2)
            evac(pe, ("kvc", 0, 0))
            evac(pe, ("kvc", 0, 1))
            for rd in range(2):
                qd = [qbd[:, k, rd * P:(rd + 1) * P] for k in range(2)]
                ps = open_item(("sms", rd))
                for b in range(4):
                    mm(ps[32 * b:32 * b + 32, 0:NCB], qd[0][:, 32 * b:32 * b + 32], kcT[:, 4 * rd + b, :],
                       start=True, stop=True)
                for s in range(2):
                    last = mm(ps[:, 64 + 32 * s:96 + 32 * s], qd[1], kT[:, s, SEQ:TOK], start=True, stop=True)
                last.then_inc(psum_full, 1)
                ps = open_item(("imp", rd))
                pe.wait_ge(sem("smp_cmp"), rd + 1)
                mm(ps[:, 0:64], cst("gsum"), cPn, start=True, stop=True).then_inc(psum_full, 1)
                for kind, tiles, hk in (("sk", 8, "Ss"), ("wk", 4, "Sw")):
                    for b in range(5):
                        if b < 4:
                            raw_keys_t(kind, rd, b, tiles)
                        if b == 1:
                            open_hold((hk, rd))
                        if b:
                            evac(pe, (kind + "T", rd, b - 1))
                            for c in range(tiles // 4):
                                last = mm(HOLD[32 * (b - 1):32 * b, c * 512:(c + 1) * 512],
                                          qd[1][:, 32 * (b - 1):32 * b], XK[:, (b - 1) % XKS, c * 512:(c + 1) * 512],
                                          start=True, stop=True)
                    last.then_inc(hold_full, 1)
                ps = open_item(("sPT", rd, 0))
                pe.wait_ge(sem("smp_sel"), rd + 1)
                for j in range(8):
                    last = tr(ps[:, j * P:(j + 1) * P], sS[:, j * P:(j + 1) * P], ident)
                last.then_inc(psum_full, 1)
                ps = open_item(("sPT", rd, 1))
                pe.wait_ge(sem("smp_win"), rd + 1)
                tr(ps[0:32, 0:P], sS[:, 1024:1056], ident)
                tr(ps[0:32, P:2 * P], wS[:, 512:544], ident)
                tr(ps[0:NCB, 2 * P:3 * P], cPn[:, 0:NCB], ident)
                for j in range(4):
                    last = tr(ps[:, (3 + j) * P:(4 + j) * P], wS[:, j * P:(j + 1) * P], ident)
                last.then_inc(psum_full, 1)
                evac(pe, ("sPT", rd, 0))
                evac(pe, ("sPT", rd, 1))
                open_hold(("PV", rd))
                for br, kind, tiles in ((1, "sv", 8), (2, "wv", 4)):
                    for b in range(4):
                        s, c = raw_count((kind, rd, b))
                        pe.wait_ge(s, c)
                        o = HOLD[32 * b:32 * b + 32, br * P:(br + 1) * P]
                        rows = slice(32 * b, 32 * b + 32)
                        pt = sPT if br == 1 else mPT[:, 384:896]
                        mm(o, mPT[0:32, (br - 1) * P + 32 * b:(br - 1) * P + 32 * b + 32], vtok[0:32, QT, br - 1, :],
                           start=True, stop=False)
                        for j in range(tiles):
                            last = mm(o, pt[:, j * P + 32 * b:j * P + 32 * b + 32],
                                      RAW[:, raws[(kind, rd, b)] % RAWS, j * P:(j + 1) * P],
                                      start=False, stop=(j == tiles - 1))
                        last.then_inc(sem("values_used"), 1)
                for b in range(4):
                    last = mm(HOLD[32 * b:32 * b + 32, 0:P], mPT[0:NCB, 2 * P + 32 * b:2 * P + 32 * b + 32],
                              vc[0:NCB, 4 * rd + b, :], start=True, stop=True)
                last.then_inc(hold_full, 1)
            for c in ("hi0", "hi1"):
                token_major(c, [(c, "p"), (c, "s")])
            for c in ("hf", "hq", "hg"):
                for n in range(2):
                    feature_major(c, n)
            pe.wait_ge(sem("nsa_normed"), 1)
            for f in range(4):
                ps = open_item(("nT", f))
                for tt in range(QT + 1):
                    at, n = token_tiles(tt)
                    last = tr(ps[:, at:at + n], otok[0:n, tt, f * P:(f + 1) * P], ident[0:n, 0:n])
                last.then_inc(psum_full, 1)
            for h in range(HH):
                hs = slice(h * HK, (h + 1) * HK)
                ps = open_item(("klT", h))
                pe.wait_ge(sem("k_decayed"), h + 1)
                for tt in range(QT + 1):
                    at, n = token_tiles(tt)
                    last = tr(ps[0:n, tt * P:(tt + 1) * P], kdec[:, at:at + n], ident)
                last.then_inc(psum_full, 1)
                ps = open_item(("dS", h))
                evac(pe, ("klT", h))
                if h == 0:
                    for c in ("hi0", "hi1"):
                        evac(pe, (c, "p"))
                        evac(pe, (c, "s"))
                for c in range(QT):
                    last = mm(ps[:, c * HK:(c + 1) * HK], kltok[:, c, :], hi[:, c, hs], start=True, stop=True)
                last.then_inc(psum_full, 1)
                ps = open_item(("dSs", h))
                pe.wait_ge(sem("v_diag"), h + 1)
                for c in range(2):
                    last = mm(ps[:, c * 512:(c + 1) * 512], kltok[0:NSMP, QT, :], Vbd[0:NSMP, c * 512:(c + 1) * 512],
                              start=True, stop=True)
                last.then_inc(psum_full, 1)
                for L in range(len(LEVELS)):
                    ps = open_item(("A", h, L))
                    if L:
                        pe.wait_ge(sem("levels"), 2 * (h * 7 + L))
                        q, k = LQ[:, (h * 7 + L) % 2, :], LK[:, (h * 7 + L) % 2, :]
                    else:
                        q, k = hQ[:, h, :], hK[:, h, :]
                        evac(pe, ("hq", h))
                    nq = P // 2 if L else P
                    for c in range(QT):
                        last = mm(ps[:, c * nq:(c + 1) * nq], k[:, c * P:(c + 1) * P],
                                  past(q[:, c * P:(c + 1) * P], L), start=True, stop=True)
                    if LEVELS[L] < DS:
                        ns = NSMP // 2 if L else NSMP
                        last = mm(ps[0:NSMP, 512:512 + ns], k[:, SEQ:TOK], past(q[:, SEQ:TOK], L),
                                  start=True, stop=True)
                    last.then_inc(psum_full, 1)
                ps = open_item(("o", h))
                pe.wait_ge(sem("scores_done"), h + 1)
                pe.wait_ge(sem("states_done"), h + 1)
                pe.wait_ge(sem("q_decayed"), h + 1)
                pe.wait_ge(sload[h % 2], 16 * (h // 2 + 1))
                for c in range(QT):
                    cs = slice(c * P, (c + 1) * P)
                    if c:
                        mm(ps[:, cs], Sst[:, c - 1, :], qdec[:, cs], start=True, stop=False)
                    mm(ps[:, cs], hi[:, c, hs], Aacc[:, cs], start=(c == 0), stop=True)
                for b in range(DB):
                    mm(ps[:, 512 + DS * b:512 + DS * b + DS], S0[:, h % 2, b * HK:(b + 1) * HK],
                       qdec[:, SEQ + DS * b:SEQ + DS * b + DS], start=(b == 0), stop=False, skip_group_check=True)
                mm(ps[:, 512:TOK], hi[0:NSMP, QT, hs], Aacc[0:NSMP, SEQ:TOK], start=False, stop=True,
                   skip_group_check=True).then_inc(psum_full, 1)
                ps = open_item(("osum", h))
                pe.wait_ge(sem("o_squares"), h + 1)
                for hf in range(2):
                    last = mm(ps[:, hf * 512:hf * 512 + HALF], ones[:, :], gtmp[:, hf * HALF:(hf + 1) * HALF],
                              start=True, stop=True)
                last.then_inc(psum_full, 1)

            def mixed(k):
                pe.wait_ge(sem("mixed"), k + 1)
            for n in range(4):
                feature_major("wout", n, mixed if n == 0 else nothing)

            pe.wait_ge(sem("mem_in"), 16)
            for n in range(2):
                ps = open_item(("mT", n))
                for k in range(4):
                    for m in range(2):
                        last = tr(ps[:, k * MEM + m * P:k * MEM + (m + 1) * P],
                                  mst[:, m, (4 * n + k) * P:(4 * n + k + 1) * P], ident)
                last.then_inc(psum_full, 1)
            ps = open_item(("msum",))
            pe.wait_ge(sem("mem_squares"), 2)
            sq = mkT
            for k in range(KT):
                last = mm(ps[:, 0:MEM], ones[:, :], sq[:, k, :], start=(k == 0), stop=(k == KT - 1))
            last.then_inc(psum_full, 1)
            norm_sum(1)
            pe.wait_ge(sem("mem_normed"), 1)
            for c in ("wk", "wv"):
                for n in range(4):
                    ps = open_item((c, n))
                    for hf in range(2):
                        x = splits[(c, n, hf)]
                        pe.wait_ge(sem("weights_lo"), x + 1)
                        for m in range(2):
                            for k in range(KH):
                                for i, (pw, px) in enumerate(passes):
                                    last = mm(ps[:, m * 256:(m + 1) * 256],
                                              (MNH, MNL)[px][:, hf * KH + k, m * P:(m + 1) * P],
                                              half_of((WH, WL)[pw], x, KH, 256)[:, k, :],
                                              start=(m == 0 and hf == 0 and k == 0 and i == 0),
                                              stop=(hf == 1 and k == KH - 1 and i == 2), skip_group_check=True)
                        last.then_inc(psum_full if hf else sem("half_used"), 1)
            for n in range(4):
                evac(pe, ("wk", n))
            for n in range(2):
                ps = open_item(("mkT", n))
                for k in range(4):
                    for m in range(2):
                        last = tr(ps[:, k * MEM + m * P:k * MEM + (m + 1) * P],
                                  mst[:, m, (4 * n + k) * P:(4 * n + k + 1) * P], ident)
                last.then_inc(psum_full, 1)
            for n in range(4):
                feature_major("wq", n, normed(1) if n == 0 else nothing)

            for n in (5, 6, 7):
                evac(pe, ("wq", n))
            for n in range(2):
                evac(pe, ("mkT", n))
            for n in range(4):
                evac(pe, ("wv", n))
            def cross_score(i):
                cs = slice(i * P, (i + 1) * P)
                ps = open_item(("cS", i))
                for h in range(CH):
                    for k in range(2):
                        last = mm(ps[:, h * MEM:(h + 1) * MEM], QC[:, 2 * h + k, cs], mkT[:, 2 * h + k, :],
                                  start=(k == 0), stop=(k == 1))
                last.then_inc(psum_full, 1)

            cross_score(0)
            cross_score(1)
            for i in range(QT):
                ps = open_item(("cPT", i))
                pe.wait_ge(sem("cross_probs"), i + 1)
                for h in range(CH):
                    for m in range(2):
                        at = (2 * h + m) * P
                        last = tr(ps[:, at:at + P], xP[:, i % 2, at:at + P], ident)
                last.then_inc(psum_full, 1)
                ps = open_item(("cO", i))
                evac(pe, ("cPT", i))
                for d in range(KT):
                    for m in range(2):
                        at = (2 * (d // 2) + m) * P
                        last = mm(ps[:, d * P:(d + 1) * P], mv[:, m, d * P:(d + 1) * P], xPT[:, i % 2, at:at + P],
                                  start=(m == 0), stop=(m == 1))
                last.then_inc(psum_full, 1)
                if i + 2 < QT:
                    cross_score(i + 2)
            pe.wait_ge(sem("cross_diag"), 1)
            parts = [(b, n) for b in range(DB) for n in range(2)]

            def mem_transpose(b, n):
                if n == 0:
                    pe.wait_ge(cload[b % 3], 16 * (b // 3 + 1))
                ps = open_item(("cx", b, n))
                raw = RC[:, b % 3, :].rearrange("p (j n) -> p j n", j=2)
                for k in range(4):
                    for j in range(2):
                        last = tr(ps[:, (2 * k + j) * P:(2 * k + j + 1) * P],
                                  raw[:, j, (4 * n + k) * P:(4 * n + k + 1) * P], ident)
                last.then_inc(psum_full, 1)

            mem_transpose(0, 0)
            open_hold(("cS",))
            for x, (b, n) in enumerate(parts):
                if x + 1 < len(parts):
                    mem_transpose(*parts[x + 1])
                evac(pe, ("cx", b, n))
                q = 32 * (b // 2)
                for k in range(4):
                    last = mm(HOLD[q:q + 32, 0:MEM], qbc[:, 4 * n + k, b, :], KX[:, x % 2, k * MEM:(k + 1) * MEM],
                              start=(b % 2 == 0 and n == 0 and k == 0), stop=(b % 2 == 1 and n == 1 and k == 3))
            last.then_inc(hold_full, 1)
            ps = open_item(("csPT",))
            pe.wait_ge(sem("cross_smp"), 1)
            for j in range(2):
                last = tr(ps[:, j * P:(j + 1) * P], yP[:, j * P:(j + 1) * P], ident)
            last.then_inc(psum_full, 1)
            evac(pe, ("csPT",))
            open_hold(("cO",))
            for b in range(DB):
                x = DB + b
                pe.wait_ge(cload[x % 3], 16 * (x // 3 + 1))
                raw = RC[:, x % 3, :].rearrange("p (j n) -> p j n", j=2)
                q = 32 * (b // 2)
                for hf in range(2):
                    for j in range(2):
                        last = mm(HOLD[q:q + 32, hf * 512:(hf + 1) * 512], yPT[:, j, b, :],
                                  raw[:, j, hf * 512:(hf + 1) * 512], start=(b % 2 == 0 and j == 0),
                                  stop=(b % 2 == 1 and j == 1))
                last.then_inc(hold_full if b == DB - 1 else sem("cross_values_used"), 1)
            ps = open_item(("csO",))
            pe.wait_ge(hold_free, hold[("cO",)] + 1)
            for d in range(KT):
                last = tr(ps[:, d * P:(d + 1) * P], crow[:, d * P:(d + 1) * P], ident)
            last.then_inc(psum_full, 1)

            def crossed(k):
                pe.wait_ge(sem("crossed"), k + 1)
            for n in range(4):
                feature_major("wo", n, crossed if n == 0 else nothing)

            norm_sum(2)
            def hidden(k):
                pe.wait_ge(sem("hidden"), k + 1)

            for n in range(FT // 2):
                feature_major("ffg", n, normed(2) if n == 0 else nothing)
                feature_major("ffu", n)
            for n in range(4):
                ps2 = [open_item(("ffd", 2 * n)), open_item(("ffd", 2 * n + 1))]
                for kc in range(3):
                    for m in range(2):
                        split_product(("ffd", n, kc, m), ps2[m], range(8 * kc, min(8 * kc + 8, FT)), HIDH, HIDL,
                                      hidden if n == 0 and m == 0 else nothing, kc == 0, kc == 2).then_inc(
                                          sem("half_used") if kc < 2 else psum_full, 1)
            norm_sum(3)
            pe.wait_ge(sem("normed"), 4 * KT)
            for tt in range(QT + 1):
                at, n = token_tiles(tt)
                ps = open_item(("y", tt))
                for k in range(KT):
                    last = tr(ps[0:n, k * P:(k + 1) * P], H[:, k, at:at + n], ident)
                last.then_inc(psum_full, 1)

        class Steps:
            def __init__(self, e, name):
                self.e, self.s, self.n = e, sem(name), 0

            def __call__(self, ins):
                ins.then_inc(self.s, 1)
                self.n += 1
                self.e.wait_ge(self.s, self.n)

        def halves(ps):
            return ps[:, :].rearrange("p (a t) -> p a t", a=2)[:, :, 0:HALF]

        def two(ap):
            return ap.rearrange("p (a t) -> p a t", a=2)

        def p4(ps, cols=256):
            return ps[:, 0:4 * cols].rearrange("p (t n) -> p t n", t=4)

        @block.scalar
        def _(act):
            fn = nc.scalar.activation
            step = Steps(act, "act_step")
            COPY, EXP = ACT.Copy, ACT.Exp

            def copy_out(key, out_, in_):
                full(act, key)
                fn(out_, in_, COPY).then_inc(freed(key), 1)

            rms_count = [0]

            def rsqrt(y, m):
                rms_count[0] += 1
                act.wait_ge(sem("mean_in"), rms_count[0])
                step(fn(y, m, ACT.Ln))
                fn(y, y, EXP, scale=-0.5).then_inc(sem("rsqrt_guess"), 1)

            split_next = [0]

            def split_to(x):
                while split_next[0] <= x:
                    y = split_next[0]
                    w, kk, cols, loaded, c = split_view(list(splits)[y])
                    act.wait_ge(loaded, c)
                    split_slot_free(act, y)
                    fn(half_of(WH, y, kk, cols), w, COPY).then_inc(sem("weights_hi"), 1)
                    split_next[0] += 1

            def normalized_hi(n):
                for k in range(KT):
                    act.wait_ge(sem("normed_raw"), KT * n + k + 1)
                    fn(OPH[:, k, :], NTS[n][:, k % 2, :], COPY).then_inc(sem("normed_hi"), 1)
                    yield k

            copy_out(("vec",), GV[:, :], slot(("vec",))[:, 0:ROWV])
            for k in range(KT):
                copy_out(("xT", k), X[:, k, :], slot(("xT", k))[:, 0:TOK])
            split_to(1)
            rsqrt(RSTD[:, :], MEAN[:, :])
            for _ in normalized_hi(0):
                pass
            act.wait_ge(sem("cleared"), 3)
            for name, dst in (("cmp", None), ("sel", 0), ("win", 1)):
                kp, ks_ = (name, "p"), (name, "s")
                x = splits[(name, 0)]
                split_to(x + 2)
                full(act, kp)
                if dst is None:
                    fn(ckcv[:, 0:QT, :], p4(slot(kp)), COPY).then_inc(freed(kp), 1)
                    split_to(x + 3)
                    copy_out(ks_, ckcv[0:NSMP, QT, :], slot(ks_)[0:NSMP, 0:256])
                else:
                    step(fn(ksw[:, 0:QT, dst, :], p4(slot(kp))[:, :, 0:GW], COPY))
                    fn(vtok[:, 0:QT, dst, :], p4(slot(kp))[:, :, GW:256], COPY).then_inc(freed(kp), 1)
                    split_to(x + 3)
                    full(act, ks_)
                    step(fn(ksw[0:NSMP, QT, dst, :], slot(ks_)[0:NSMP, 0:GW], COPY))
                    fn(vtok[0:NSMP, QT, dst, :], slot(ks_)[0:NSMP, GW:256], COPY).then_inc(freed(ks_), 1)
            copy_out(("gate", "p"), two(gateT[0:24, :]), halves(slot(("gate", "p")))[0:24])
            split_to(splits[("q0", 1)])
            for n in range(2):
                kp, ks_ = (f"q{n}", "p"), (f"q{n}", "s")
                q4 = qtok.rearrange("p t (r g d) -> p t r g d", r=NR, g=NG)
                if n == 0:
                    split_to(splits[("q1", 0)])
                copy_out(kp, q4[:, 0:QT, :, n, :], p4(slot(kp)).rearrange("p t (r d) -> p t r d", r=NR))
                if n == 0:
                    split_to(splits[("q1", 1)])
                copy_out(ks_, q4[0:NSMP, QT, :, n, :], slot(ks_)[0:NSMP, 0:256].rearrange("p (r d) -> p r d", r=NR))
                if n == 0:
                    key = ("gateT",)
                    full(act, key)
                    step(fn(gates[:, 0:QT, :], p4(slot(key), 24), EXP, scale=-1.0))
                    fn(gates[0:NSMP, QT, :], slot(key)[0:NSMP, QT * 24:(QT + 1) * 24], EXP,
                       scale=-1.0).then_inc(freed(key), 1)
            for s in range(2):
                copy_out(("kT", s), kT[:, s, :], slot(("kT", s))[:, 0:TOK])
            for rot in range(2):
                for r in range(NR):
                    copy_out(("qT", rot, r), (qrT if rot else qT)[:, r, :], slot(("qT", rot, r))[:, 0:TOK])

            def gelu_exp(n):
                act.wait_ge(sem("gelu_in"), n + 1)
                g4 = n % 3
                w = 504 if g4 < 2 else 2 * NPB
                fn(HT[:, 0:w], HT[:, 0:w], EXP, scale=-2 * 0.7978845608028654).then_inc(sem("gelu_exp"), 1)

            def cmp_result(kv, g4):
                key = ("kvc", kv, g4)
                cnt, nb = (4, NCB) if g4 < 2 else (1, NPB)
                if kv == 0:
                    copy_out(key, kcT[:, 4 * g4:4 * g4 + cnt, 0:nb],
                             slot(key)[:, 0:cnt * nb].rearrange("p (b n) -> p b n", b=cnt))
                else:
                    copy_out(key, vc[0:nb, 4 * g4:4 * g4 + cnt, :],
                             slot(key)[0:nb, 0:cnt * GW].rearrange("p (b n) -> p b n", b=cnt))

            for kv in range(2):
                copy_out(("pe", kv), cb[:, kv:kv + 1], slot(("pe", kv))[:, 0:1])
                for n in range(9):
                    rows = P if n < 8 else SEQ // 8
                    key = ("xk", kv, n)
                    full(act, key)
                    dst = XK[:, n % XKS, 0:8 * rows].rearrange("p (m g s) -> p m g s", m=4, g=NG)
                    from_ = slot(key)[:, 0:8 * rows].rearrange("p (m a s) -> p m a s", m=4, a=2)
                    for g in range(NG):
                        for e in range(2):
                            ins = fn(dst[e * HD:(e + 1) * HD, :, g, :], from_[g * HD:(g + 1) * HD, :, e, :], COPY)
                            if g and e:
                                ins.then_inc(freed(key), 1)
                            else:
                                step(ins)
                    if kv and n == 1:
                        cmp_result(0, 2)
                    if kv and n == 4:
                        act.wait_ge(sem("pcs_in"), 1)
                        fn(cP, cP, EXP, scale=SCALE).then_inc(sem("pcs_exp"), 1)
                    if n == 6:
                        gelu_exp(3 * kv)
                    if n == 7:
                        cmp_result(kv, 0)
                gelu_exp(3 * kv + 1)
                cmp_result(kv, 1)
                if kv:
                    act.wait_ge(hold_full, hold[("h", 1, 2)] + 1)
                    fn(qr0[0:HD], qrT[0:HD, :, 0:SEQ], COPY).then_inc(sem("q0_copied"), 1)
                gelu_exp(3 * kv + 2)
            cmp_result(1, 2)
            split_to(splits[("hi0", 1)])

            def exps(n):
                i, g, r = heads[n]
                act.wait_ge(sem("row_max"), n + 1)
                ps, L = slot(("S", n)), (i + 1) * P
                for s in range(2):
                    at = (g * NR + r) * 3 + 1 + s
                    ins = fn(Pb[:, n % 2, s * 512:s * 512 + L], ps[:, s * 512:s * 512 + L], EXP,
                             bias=snm[:, 2 * (n % 2) + s:2 * (n % 2) + s + 1], scale=SCALE,
                             accum_out=DEN[:, i, at:at + 1])
                    if s:
                        ins.then_inc(freed(("S", n)), 1)
                    else:
                        step(ins)

            exps(0)
            exps(1)
            for n in range(len(heads)):
                i = heads[n][0]
                if n % 8 == 0:
                    copy_out(("PTc", i), PTc[0:NPB, i % 2, :], slot(("PTc", i))[0:NPB, :])
                w = 2 * (i + 1) * P
                copy_out(("PT", n), PTb[:, n % 2, 0:w], slot(("PT", n))[:, 0:w])
                if n + 2 < len(heads):
                    exps(n + 2)

            for rd in range(2):
                act.wait_ge(sem("smp_cmp_in"), rd + 1)
                fn(cPn[:, 0:NCB], cS[:, 0:NCB], EXP, bias=snm1[:, 0:1], scale=SCALE,
                   accum_out=sden[:, 0:1]).then_inc(sem("smp_cmp_exp"), 1)
                for kind, w in (("sk", 1024), ("wk", 512)):
                    for b in range(4):
                        key = (kind + "T", rd, b)
                        copy_out(key, XK[:, b % XKS, 0:w], slot(key)[:, 0:w])
                act.wait_ge(sem("smp_sel_in"), rd + 1)
                fn(sS, sS, EXP, bias=snm1[:, 1:2], scale=SCALE,
                   accum_out=sden[:, 1:2]).then_inc(sem("smp_sel"), 1)
                act.wait_ge(sem("smp_win_in"), rd + 1)
                fn(wS, wS, EXP, bias=snm1[:, 2:3], scale=SCALE,
                   accum_out=sden[:, 2:3]).then_inc(sem("smp_win"), 1)
                copy_out(("sPT", rd, 0), sPT, slot(("sPT", rd, 0))[:, :])
                key = ("sPT", rd, 1)
                full(act, key)
                step(fn(mPT[0:32, 0:2 * P], slot(key)[0:32, 0:2 * P], COPY))
                step(fn(mPT[0:NCB, 2 * P:3 * P], slot(key)[0:NCB, 2 * P:3 * P], COPY))
                fn(mPT[:, 384:896], slot(key)[:, 384:896], COPY).then_inc(freed(key), 1)
            split_to(splits[("hi1", 0)])
            act.wait_ge(sem("otok_done"), 1)
            for tt in range(QT + 1):
                n = P if tt < QT else NSMP
                step(fn(Pb[0:n, 0, 0:NSAW], otok[0:n, tt, :], ACT.Square, accum_out=ss[0:n, tt:tt + 1]))
            act.sem_inc(sem("nsa_squares"), 1)
            rsqrt(rs5[:, 0:QT], sm5[:, 0:QT])
            rsqrt(rs5[0:NSMP, QT:QT + 1], sm5[0:NSMP, QT:QT + 1])
            act.sem_inc(sem("act_phase"), 1)

            act.wait_ge(sem("dve_phase"), 1)
            act.wait_ge(sem("store_phase"), 1)
            for n in range(2):
                kp, ks_ = (f"hi{n}", "p"), (f"hi{n}", "s")
                cs = slice(n * 256, (n + 1) * 256)
                x = splits[(f"hi{n}", 0)]
                split_to(x + 2)
                copy_out(kp, hi[:, 0:QT, cs], p4(slot(kp)))
                split_to(x + 3)
                copy_out(ks_, hi[0:NSMP, QT, cs], slot(ks_)[0:NSMP, 0:256])

            act.wait_ge(sem("lb_in"), 1)
            fn(lb, lb, EXP).then_inc(sem("lb_exp"), 1)

            def log_f(h):
                act.wait_ge(sem("forget_in"), h + 1)
                fn(hB[:, h, :], hB[:, h, :], ACT.Ln).then_inc(sem("forget_log"), 1)
            for h in range(HH):
                key = ("hf", h)
                full(act, key)
                fn(two(hK[:, h, :]), halves(slot(key)), EXP, scale=-1.0).then_inc(freed(key), 1)
                split_to(splits[("hf", 0, 0)] + h + 2)
            for h in range(HH):
                log_f(h)
                copy_out(("hq", h), two(hQ[:, h, :]), halves(slot(("hq", h))))
                split_to(splits[("hq", 0, 0)] + h + 2)
            for h in range(HH):
                key = ("hg", h)
                full(act, key)
                fn(two(hG[:, h, :]), halves(slot(key)), EXP, scale=-1.0).then_inc(sem("out_gate_exp"), 1)
                split_to(splits[("hg", 0, 0)] + h + 2)

            def mixed_hi(k):
                fn(OPH[:, k, :], MX[:, k, :], COPY).then_inc(sem("mixed_hi"), 1)
            for f in range(4):
                evac(act, ("nT", f))
                mixed_hi(f)
            def decays(h):
                act.wait_ge(sem("decay_sum"), h + 1)
                if h:
                    act.wait_ge(sem("q_decayed"), h)
                    act.wait_ge(sem("states_done"), h)
                fn(E0, hB[:, h, :], EXP).then_inc(sem("decay_exp"), 1)
                act.wait_ge(sem("k_decay_in"), h + 1)
                fn(kdec, kdec, EXP).then_inc(sem("k_decay_exp"), 1)
            decays(0)
            for h in range(HH):
                key = ("klT", h)
                full(act, key)
                step(fn(kltok[:, 0:QT, :], slot(key)[:, 0:512].rearrange("p (c n) -> p c n", c=4), COPY))
                fn(kltok[0:NSMP, QT, :], slot(key)[0:NSMP, 512:640], COPY).then_inc(freed(key), 1)
                for L in range(1, len(LEVELS)):
                    w = TOK if LEVELS[L] < DS else SEQ
                    x = h * 7 + L
                    act.wait_ge(sem("level_in"), 2 * x)
                    if x > 2:
                        act.wait_ge(sem("levels"), 2 * (x - 2))
                    fn(LE[:, x % 2, 0:w], LD[:, x % 2, 0:w], EXP, scale=-1.0).then_inc(sem("level_exp"), 1)
                if h:
                    act.wait_ge(sem("hg_out"), h)
                    mixed_hi(3 + h)
                if h + 1 < HH:
                    decays(h + 1)
                key = ("o", h)
                full(act, key)
                if h:
                    act.wait_ge(sem("hg_out"), h)
                fn(gtmp, slot(key)[:, 0:TOK], ACT.Square).then_inc(sem("o_squares"), 1)
                rsqrt(RSTD[:, :], MEAN[:, :])
            act.wait_ge(sem("hg_out"), HH)
            mixed_hi(3 + HH)
            split_to(splits[("wk", 0, 1)])
            act.wait_ge(sem("dve_phase"), 2)
            act.wait_ge(sem("store_phase"), 2)
            act.wait_ge(sem("mem_in"), 16)
            for n in range(2):
                copy_out(("mT", n), mnT[:, 4 * n:4 * n + 4, :],
                         slot(("mT", n))[:, :].rearrange("p (k n) -> p k n", k=4))
            rsqrt(RSTD[:, 0:MEM], MEAN[:, 0:MEM])
            for k in range(KT):
                act.wait_ge(sem("mem_raw"), k + 1)
                fn(MNH[:, k, :], mnT[:, k, :], COPY).then_inc(sem("mem_hi"), 1)
            rsqrt(RSTD[:, :], MEAN[:, :])

            def mem_out(c, n):
                copy_out((c, n), (mst if c == "wk" else mv)[:, :, n * 256:(n + 1) * 256],
                         slot((c, n))[:, 0:512].rearrange("p (m n) -> p m n", m=2))
            for k in normalized_hi(1):
                split_to(splits[("wk", 0, 0)] + 2 + k)
                if k % 2:
                    mem_out("wk", k // 2)
            for n in range(4):
                x = splits[("wv", n, 0)]
                split_to(x + 2)
                mem_out("wv", n)
                split_to(x + 3)
            for n in range(2):
                copy_out(("mkT", n), mkT[:, 4 * n:4 * n + 4, :],
                         slot(("mkT", n))[:, :].rearrange("p (k n) -> p k n", k=4))
            for n in range(KT):
                copy_out(("wq", n), two(QC[:, n, :]), halves(slot(("wq", n))))
                split_to(splits[("wq", 0, 0)] + n + 2)
            def cross_exps(i):
                key = ("cS", i)
                act.wait_ge(sem("cross_max"), i + 1)
                for h in range(CH):
                    x = 4 * (i % 2) + h
                    ins = fn(xP[:, i % 2, h * MEM:(h + 1) * MEM], slot(key)[:, h * MEM:(h + 1) * MEM], EXP,
                             bias=xnm[:, x:x + 1], scale=CSCALE, accum_out=xden[:, x:x + 1])
                    if h == CH - 1:
                        ins.then_inc(freed(key), 1)
                    else:
                        step(ins)
            cross_exps(0)
            for i in range(QT):
                if i + 1 < QT:
                    cross_exps(i + 1)
                copy_out(("cPT", i), xPT[:, i % 2, :], slot(("cPT", i))[:, :])
                copy_out(("cO", i), MX[:, :, i * P:(i + 1) * P],
                         slot(("cO", i))[:, :].rearrange("p (k n) -> p k n", k=KT))
            for b in range(DB):
                for n in range(2):
                    copy_out(("cx", b, n), KX[:, n, :], slot(("cx", b, n))[:, :])
            act.wait_ge(sem("cross_smp_max"), 1)
            fn(yP, HOLD[:, 0:MEM], EXP, bias=msc[:, 0:1], scale=CSCALE,
               accum_out=msc[:, 1:2]).then_inc(hold_free, 1)
            act.wait_ge(sem("cross_cleared"), 2)
            key = ("csPT",)
            full(act, key)
            for b2 in range(2):
                ins = fn(yPT[:, :, b2::2, 16 * b2:16 * b2 + 16],
                         slot(key)[:, 0:MEM].rearrange("p (j b c n) -> p j b c n", j=2, b=DB // 2, c=2)[:, :, :, b2, :],
                         COPY)
                if b2:
                    ins.then_inc(freed(key), 1)
                else:
                    step(ins)
            act.wait_ge(hold_full, hold[("cO",)] + 1)
            fn(crow, HOLD[:, :], COPY).then_inc(hold_free, 1)
            key = ("csO",)
            full(act, key)
            for h in range(CH):
                ins = fn(MX[:, 2 * h:2 * h + 2, SEQ:TOK].rearrange("p k (b t) -> p k b t", b=DB),
                         slot(key)[:, 2 * h * P:(2 * h + 2) * P].rearrange("p (k b h t) -> p k b h t", k=2, b=DB,
                                                                          h=CH)[:, :, :, h, :], COPY)
                if h < CH - 1:
                    step(ins)
            ins.then_inc(freed(key), 1)
            evac(act, key)
            act.wait_ge(hold_free, len(hold))
            for i in range(QT):
                evac(act, ("cO", i))
            for k in range(KT):
                fn(OPH[:, k, :], MX[:, k, :], COPY).then_inc(sem("crossed_hi"), 1)
            act.sem_inc(sem("act_phase"), 1)
            split_to(splits[("ffg", 0, 1)])
            rsqrt(RSTD[:, :], MEAN[:, :])
            act.wait_ge(sem("dve_phase"), 3)
            act.wait_ge(sem("store_phase"), 3)
            for _ in normalized_hi(2):
                pass
            F0 = splits[("ffg", 0, 0)]
            for n in range(FT // 2):
                for m in range(2):
                    j = 2 * n + m
                    key = ("ffg", j)
                    full(act, key)
                    if j >= 2:
                        act.wait_ge(sem("hidden"), j - 1)
                    fn(two(ftmp[:, m, :]), halves(slot(key)), EXP, scale=-1.0).then_inc(sem("gate_exp"), 1)
                    split_to(F0 + 4 * n + m + 2)
                for m in range(2):
                    j = 2 * n + m
                    split_to(F0 + 4 * n + m + 4)
                    act.wait_ge(sem("hidden_raw"), j + 1)
                    fn(HIDH[:, j, :], htmp, COPY).then_inc(sem("hidden_hi"), 1)
            split_to(len(splits) - 1)
            rsqrt(RSTD[:, :], MEAN[:, :])
            for tt in range(QT + 1):
                n = P if tt < QT else NSMP
                if tt >= 2:
                    act.wait_ge(sem(f"y_out{tt % 2}"), 16 * (tt // 2))
                copy_out(("y", tt), ymid[0:n, tt % 2, :], slot(("y", tt))[0:n, :])

        @block.vector
        def _(dve):
            v = nc.vector
            tt_, ts, stt, cp = v.tensor_tensor, v.tensor_scalar, v.scalar_tensor_tensor, v.tensor_copy
            step = Steps(dve, "dve_step")
            gain_at = [V_MIX, V_CA, V_FFN, V_FIN]

            def square(k):
                tt_(SQ[norm_of[0]][:, k, :], X[:, k, :], X[:, k, :], ALU.mult).then_inc(sem("squares"), 1)
            norm_of = [0]

            rms_count = [0]

            def refine(y, m, t):
                rms_count[0] += 1
                dve.wait_ge(sem("rsqrt_guess"), rms_count[0])
                step(tt_(t, y, y, ALU.mult))
                step(tt_(t, t, m, ALU.mult))
                step(ts(t, t, -0.5, 1.5, ALU.mult, ALU.add))
                step(tt_(y, y, t, ALU.mult))

            def inverse_rms(key, n, width, scratch):
                full(dve, key)
                if n == TOK:
                    ts(two(MEAN[:, :]), halves(slot(key)), 1.0 / width, EPS, ALU.mult, ALU.add).then_inc(freed(key), 1)
                else:
                    ts(MEAN[:, 0:n], slot(key)[:, 0:n], 1.0 / width, EPS, ALU.mult, ALU.add).then_inc(freed(key), 1)
                evac(dve, key)
                dve.sem_inc(sem("mean_in"), 1)
                refine(RSTD[:, 0:n], MEAN[:, 0:n], scratch)

            def normalize(n):
                key = ("sum", n)
                inverse_rms(key, TOK, DM, H[:, 0, :])
                evac(dve, ("vec",))
                for k in range(KT):
                    g = GV[:, gain_at[n] + k:gain_at[n] + k + 1]
                    stt(H[:, k, :], X[:, k, :], g, RSTD[:, :], ALU.mult, ALU.mult).then_inc(sem("normed"), 1)

            def normalize_split(n):
                inverse_rms(("sum", n), TOK, DM, SQ[n][:, 0, :])
                evac(dve, ("vec",))
                for k in range(KT + 1):
                    if k < KT:
                        if k > 1:
                            dve.wait_ge(sem("normed"), KT * n + k - 1)
                        g = GV[:, gain_at[n] + k:gain_at[n] + k + 1]
                        stt(NTS[n][:, k % 2, :], X[:, k, :], g, RSTD[:, :], ALU.mult, ALU.mult).then_inc(
                            sem("normed_raw"), 1)
                    if k:
                        dve.wait_ge(sem("normed_hi"), KT * n + k)
                        tt_(OPL[:, k - 1, :], NTS[n][:, (k - 1) % 2, :], OPH[:, k - 1, :].bitcast(F32),
                            ALU.subtract).then_inc(sem("normed"), 1)

            def rotate(x, nh):
                x = x.rearrange("p t (h d) -> p t h d", h=nh)
                cs = cst("rope").rearrange("p (t n) -> p t n", t=5)
                cos, sin = bc(cs[:, :, 0:8], 2, nh), bc(cs[:, :, 8:16], 2, nh)
                x1, x2 = x[:, :, :, 0:8], x[:, :, :, 8:16]
                t = [r[:, 0:5 * nh * 8].rearrange("p (t h d) -> p t h d", t=5, h=nh) for r in rtmp]
                step(tt_(t[0], x1, cos, ALU.mult))
                step(tt_(t[1], x2, sin, ALU.mult))
                step(tt_(t[2], x1, sin, ALU.mult))
                step(tt_(t[3], x2, cos, ALU.mult))
                step(tt_(x1, t[0], t[1], ALU.subtract))
                return tt_(x2, t[2], t[3], ALU.add)

            for k in range(KT):
                evac(dve, ("xT", k))
                square(k)
            dve.wait_ge(sem("cst_in"), 16)
            lo = SplitsLo(dve, v, 0)
            lo.upto(1)
            normalize_split(0)
            lo.upto(splits[("q0", 0)])
            for s in ("sel", "win"):
                evac(dve, (s, "p"))
                evac(dve, (s, "s"))
            rotate(ksw.rearrange("p t s d -> p t (s d)"), 4).then_inc(sem("k_rotated"), 1)
            lo.upto(splits[("q0", 1)])
            lo.upto(splits[("q1", 0)])
            evac(dve, ("gateT",))
            for g in (gates[:, 0:QT, :], gates[0:NSMP, QT, :]):
                step(ts(g, g, 1.0, None, ALU.add))
                step(v.reciprocal(g, g))
            dve.sem_inc(sem("gates_done"), 1)
            lo.upto(DVE_SPLITS)
            full(dve, ("qT", 0, NR - 1))
            rotate(qtok, NH).then_inc(sem("q_rotated"), 1)
            dve.wait_ge(sem("cleared"), 3)
            for rot in range(2):
                for r in range(NR):
                    evac(dve, ("qT", rot, r))
                src = qrT if rot else qT
                for g in range(NG):
                    for r in range(NR):
                        gs = slice(g * HD, (g + 1) * HD)
                        o = qbd[gs, rot, :].rearrange("p (b g r t) -> p b g r t", b=DB, g=NG, r=NR)[:, :, g, r, :]
                        step(cp(o, src[gs, r, SEQ:TOK].rearrange("p (b t) -> p b t", b=DB)))
                dve.sem_inc(sem("q_diag"), 1)

            def gelu(n):
                g4 = n % 3
                w = 504 if g4 < 2 else 2 * NPB
                x, t = HX[:, g4 % 2, 0:w], HT[:, 0:w]
                dve.wait_ge(hold_full, hold[("h", n // 3, g4)] + 1)
                evac(dve, ("pe", n // 3))
                ts(x, HOLD[:, 0:w], cb[:, n // 3:n // 3 + 1], None, ALU.add).then_inc(hold_free, 1)
                dve.wait_ge(hold_free, hold[("h", n // 3, g4)] + 1)
                step(tt_(t, x, x, ALU.mult))
                step(ts(t, t, 0.044715, 1.0, ALU.mult, ALU.add))
                tt_(t, t, x, ALU.mult).then_inc(sem("gelu_in"), 1)
                dve.wait_ge(sem("gelu_exp"), n + 1)
                step(ts(t, t, 1.0, None, ALU.add))
                step(v.reciprocal(t, t))
                tt_(x, x, t, ALU.mult).then_inc(sem("cmp_hid"), 1)

            for n in range(3):
                gelu(n)

            key = ("pcs",)
            dve.wait_ge(sem("t_stored"), 1)
            full(dve, key)
            c4 = cP.rearrange("p (g r n) -> p g r n", g=NG, r=NR)
            ps4 = slot(key)[:, :].rearrange("p (g n) -> p g n", g=2)[:, :, 0:496].rearrange("p g (r n) -> p g r n", r=NR)
            for g in range(NG):
                ins = tt_(c4[:, g], ps4[:, g], bc(cst("cadd"), 1, NR), ALU.add)
                if g:
                    ins.then_inc(freed(key), 1)
                    evac(dve, key)
                else:
                    step(ins)
            c3 = cP.rearrange("p (h n) -> p h n", n=NPB)
            step(v.tensor_reduce(pmx, c3, AX, ALU.max))
            tt_(c3, c3, bc(pmx, 2, NPB), ALU.subtract).then_inc(sem("pcs_in"), 1)
            dve.wait_ge(sem("pcs_exp"), 1)
            step(tt_(cP.rearrange("p (h n) -> p h n", h=NH), cP.rearrange("p (h n) -> p h n", h=NH),
                     bc(cst("cmul"), 1, NH), ALU.mult))
            den = DEN.rearrange("p i (h b) -> p h i b", b=3)[:, :, :, 0]
            step(v.tensor_reduce(den, cP.rearrange("p (h i n) -> p h i n", h=NH, i=QT), AX, ALU.add))
            ts(den, den, 1e-20, None, ALU.max).then_inc(sem("cmp_probs"), 1)
            dve.wait_ge(sem("cmp_probs"), 1)
            for n in range(3, 6):
                gelu(n)

            def row_max(n):
                i = heads[n][0]
                key = ("S", n)
                full(dve, key)
                s2 = slot(key)[:, :].rearrange("p (s n) -> p s n", s=2)
                diag = s2[:, :, i * P:(i + 1) * P]
                step(tt_(diag, diag, bc(cst("causal"), 1, 2), ALU.add))
                mx = smx[:, 2 * (n % 2):2 * (n % 2) + 2]
                step(v.tensor_reduce(mx, s2[:, :, 0:(i + 1) * P], AX, ALU.max))
                if n >= 2:
                    evac(dve, ("S", n - 2))
                ts(snm[:, 2 * (n % 2):2 * (n % 2) + 2], mx, -SCALE, None, ALU.mult).then_inc(sem("row_max"), 1)

            def mix_branches(i, g):
                dve.wait_ge(hold_full, hold[("o", i, g)] + 1)
                evac(dve, ("S", i * 8 + g * 4 + 3))
                step(v.reciprocal(rc12, DEN[:, i, g * 12:(g + 1) * 12]))
                step(tt_(rc12, rc12, gates[:, i, g * 12:(g + 1) * 12], ALU.mult))
                tt_(osum.rearrange("p (n d) -> p n d", n=12), HOLD[:, 0:768].rearrange("p (n d) -> p n d", n=12),
                    bc(rc12, 2, HD), ALU.mult).then_inc(hold_free, 1)
                dve.wait_ge(hold_free, hold[("o", i, g)] + 1)
                step(v.tensor_reduce(otok[:, i, g * 256:(g + 1) * 256].rearrange("p (r d) -> p r d", r=NR),
                                     osum.rearrange("p (r b d) -> p r d b", r=NR, b=3), AX, ALU.add))

            row_max(0)
            row_max(1)
            for n in range(len(heads)):
                if n + 2 < len(heads):
                    row_max(n + 2)
                if n and n % 4 == 0:
                    mix_branches((n - 1) // 8, (n - 1) // 4 % 2)
            mix_branches(QT - 1, 1)

            for rd in range(2):
                key = ("sms", rd)
                full(dve, key)
                ps = slot(key)
                step(cp(cS[:, 0:NCB], ps[:, 0:NCB]))
                if rd == 0:
                    step(v.memset(cPn, 0.0))
                step(tt_(sS[:, 1024:1056], ps[:, 64:96], cst(f"snew{rd}"), ALU.add))
                tt_(wS[:, 512:544], ps[:, 96:128], cst(f"snew{rd}"), ALU.add).then_inc(freed(key), 1)
                step(v.tensor_reduce(smx1[:, 0:1], cS[:, 0:NCB], AX, ALU.max))
                ts(snm1[:, 0:1], smx1[:, 0:1], -SCALE, None, ALU.mult).then_inc(sem("smp_cmp_in"), 1)
                dve.wait_ge(sem("smp_cmp_exp"), rd + 1)
                step(v.reciprocal(coef[:, 0:1], sden[:, 0:1]))
                ts(cPn, cPn, coef[:, 0:1], None, ALU.mult).then_inc(sem("smp_cmp"), 1)
                key = ("imp", rd)
                full(dve, key)
                v.tensor_reduce(imp, slot(key)[:, 0:64].rearrange("p (j c) -> p j c", c=4), AX,
                                ALU.add).then_inc(freed(key), 1)
                evac(dve, key)
                step(v.tensor_reduce(mn[:, 0:1], imp[:, 1:15], AX, ALU.min))
                step(stt(eqj[:, 0:14], imp[:, 1:15], mn[:, 0:1], cst("jidx")[:, 1:15], ALU.is_le, ALU.mult))
                step(v.tensor_reduce(mn[:, 1:2], eqj[:, 0:14], AX, ALU.max))
                step(ts(drop, cst("jidx"), mn[:, 1:2], NEG, ALU.is_equal, ALU.mult))
                dve.wait_ge(hold_full, hold[("Ss", rd)] + 1)
                for q in range(2):
                    ins = tt_(sS[:, q * 512:(q + 1) * 512].rearrange("p (j k e) -> p j k e", j=4, k=16),
                              HOLD[:, q * 512:(q + 1) * 512].rearrange("p (j k e) -> p j k e", j=4, k=16),
                              bc(drop, 2, 8).unsqueeze(1).broadcast_to([P, 4, 16, 8]), ALU.add)
                    if q:
                        ins.then_inc(hold_free, 1)
                        dve.wait_ge(hold_free, hold[("Ss", rd)] + 1)
                    else:
                        step(ins)
                step(v.tensor_reduce(smx1[:, 1:2], sS, AX, ALU.max))
                ts(snm1[:, 1:2], smx1[:, 1:2], -SCALE, None, ALU.mult).then_inc(sem("smp_sel_in"), 1)
                dve.wait_ge(hold_full, hold[("Sw", rd)] + 1)
                cp(wS[:, 0:512], HOLD[:, 0:512]).then_inc(hold_free, 1)
                dve.wait_ge(hold_free, hold[("Sw", rd)] + 1)
                w0 = wS[:, 0:512].rearrange("p (j n) -> p j n", j=4)[:, :, 0]
                step(tt_(w0, w0, cst("swin"), ALU.add))
                step(v.tensor_reduce(smx1[:, 2:3], wS, AX, ALU.max))
                ts(snm1[:, 2:3], smx1[:, 2:3], -SCALE, None, ALU.mult).then_inc(sem("smp_win_in"), 1)
                dve.wait_ge(sem("smp_sel"), rd + 1)
                dve.wait_ge(sem("smp_win"), rd + 1)
                dve.wait_ge(sem("gsmp_in"), 16 * 8)
                step(v.reciprocal(coef[:, 1:3], sden[:, 1:3]))
                step(tt_(coef[:, 1:3], coef[:, 1:3], gsmp[:, rd, 1:3], ALU.mult))
                step(cp(coef[:, 0:1], gsmp[:, rd, 0:1]))
                dve.wait_ge(hold_full, hold[("PV", rd)] + 1)
                acc = oacc[:, 0:384].rearrange("p (b d) -> p b d", b=3)
                tt_(acc, HOLD[:, 0:384].rearrange("p (b d) -> p b d", b=3), bc(coef[:, 0:3], 2, P),
                    ALU.mult).then_inc(hold_free, 1)
                dve.wait_ge(hold_free, hold[("PV", rd)] + 1)
                o2, o3 = oacc[:, 384:512], oacc[:, 512:576]
                step(v.tensor_reduce(o2, acc.rearrange("p b d -> p d b"), AX, ALU.add))
                step(ts(o2[:, 0:HD], o2[:, 0:HD], cst("isg")[:, 0:1], None, ALU.mult))
                if rd:
                    dve.wait_ge(sem("smp_o_out"), 16 * 4)
                stt(o3, o2[:, HD:P], cst("isg")[:, 1:2], o2[:, 0:HD], ALU.mult, ALU.add).then_inc(sem("smp_o"), 1)
            dve.wait_ge(sem("smp_o_in"), 16)
            dve.sem_inc(sem("otok_done"), 1)
            dve.wait_ge(sem("nsa_squares"), 1)
            for n, tl in ((P, slice(0, QT)), (NSMP, slice(QT, QT + 1))):
                step(ts(sm5[0:n, tl], ss[0:n, tl], 1.0 / NSAW, EPS, ALU.mult, ALU.add))
                dve.sem_inc(sem("mean_in"), 1)
                refine(rs5[0:n, tl], sm5[0:n, tl], t5[0:n, tl])
                step(tt_(otok[0:n, tl, :], otok[0:n, tl, :], bc(rs5[0:n, tl], 2, NSAW), ALU.mult))
            dve.sem_inc(sem("nsa_normed"), 1)
            dve.sem_inc(sem("dve_phase"), 1)

            dve.wait_ge(sem("act_phase"), 1)
            dve.wait_ge(sem("store_phase"), 1)
            step(v.memset(LK.rearrange("p s t -> p (s t)"), 0.0))
            step(tt_(lb, GV[:, V_LB + 4:V_LB + 8], GV[:, V_LB:V_LB + 4], ALU.subtract))
            dve.sem_inc(sem("lb_in"), 1)
            dve.wait_ge(sem("lb_exp"), 1)
            step(ts(lb, lb, 1.0, None, ALU.add))
            step(v.reciprocal(lb, lb))
            step(ts(lb1, lb, -1.0, 1.0, ALU.mult, ALU.add))
            step(ts(lbn, lb1, -1.0, None, ALU.mult))
            for h in range(HH):
                evac(dve, ("hf", h))
                K, B = hK[:, h, :], hB[:, h, :]
                step(ts(K, K, 1.0, None, ALU.add))
                step(v.reciprocal(K, K))
                ts(B, K, lb1[:, h:h + 1], lb[:, h:h + 1], ALU.mult, ALU.add).then_inc(sem("forget_in"), 1)
                step(ts(K, K, lbn[:, h:h + 1], lb1[:, h:h + 1], ALU.mult, ALU.add))
            for h in range(HH):
                B = hB[:, h, :]
                dve.wait_ge(sem("forget_log"), h + 1)
                v.tensor_tensor_scan(B, cst("reset"), B, 0.0, ALU.mult, ALU.add).then_inc(sem("decay_sum"), 1)
            for h in range(HH):
                key = ("hg", h)
                G = hG[:, h, :]
                dve.wait_ge(sem("out_gate_exp"), h + 1)
                step(ts(G, G, 1.0, None, ALU.add))
                step(v.reciprocal(G, G))
                tt_(two(G), two(G), halves(slot(key)), ALU.mult).then_inc(freed(key), 1)
            for f in range(4):
                key = ("nT", f)
                full(dve, key)
                ts(MX[:, f, :], slot(key)[:, 0:TOK], GV[:, V_NSA + f:V_NSA + f + 1], None,
                   ALU.mult).then_inc(freed(key), 1)
                evac(dve, key)

            def mixed_lo(k):
                dve.wait_ge(sem("mixed_hi"), k + 1)
                tt_(OPL[:, k, :], MX[:, k, :], OPH[:, k, :].bitcast(F32), ALU.subtract).then_inc(sem("mixed"), 1)
            for f in range(4):
                mixed_lo(f)
            def keys_decayed(h):
                B, K = hB[:, h, :], hK[:, h, :]
                dve.wait_ge(sem("decay_sum"), HH)
                if h:
                    full(dve, ("klT", h - 1))
                for at, n, w in ((0, QT, P), (SEQ, DB, DS)):
                    b3 = B[:, at:at + n * w].rearrange("p (c w) -> p c w", c=n)
                    k3 = kdec[:, at:at + n * w].rearrange("p (c w) -> p c w", c=n)
                    step(tt_(k3, b3[:, :, w - 1:w].broadcast_to([P, n, w]), b3, ALU.subtract))
                dve.sem_inc(sem("k_decay_in"), 1)
                for c in ("hi0", "hi1"):
                    evac(dve, (c, "s"))
                if h:
                    full(dve, ("dSs", h - 1))
                tt_(Vbd[0:NSMP, :].rearrange("p (b e) -> p b e", b=DB),
                    bc(hi[0:NSMP, QT, h * HK:(h + 1) * HK], 1, DB), bc(cst("bsel")[0:NSMP, :], 2, HK),
                    ALU.mult).then_inc(sem("v_diag"), 1)
                dve.wait_ge(sem("k_decay_exp"), h + 1)
                tt_(kdec, K, kdec, ALU.mult).then_inc(sem("k_decayed"), 1)
            keys_decayed(0)
            for h in range(HH):
                B, K, Q = hB[:, h, :], hK[:, h, :], hQ[:, h, :]
                evac(dve, ("hq", h))
                dve.wait_ge(sem("decay_exp"), h + 1)
                if h:
                    full(dve, ("o", h - 1))
                tt_(qdec, Q, E0, ALU.mult).then_inc(sem("q_decayed"), 1)
                if h:
                    dve.wait_ge(sem("hg_stored"), 32 * h)
                key = ("dS", h)
                full(dve, key)
                step(cp(Sst[:, 0, :], slot(key)[:, 0:HK]))
                for c in range(1, QT):
                    ins = stt(Sst[:, c, :], Sst[:, c - 1, :], E0[:, c * P + P - 1:c * P + P],
                              slot(key)[:, c * HK:(c + 1) * HK], ALU.mult, ALU.add)
                    if c == QT - 1:
                        ins.then_inc(freed(key), 1)
                        evac(dve, key)
                    else:
                        step(ins)
                key = ("dSs", h)
                full(dve, key)
                dve.wait_ge(sload[h % 2], 16 * (h // 2 + 1))
                ebl = E0[:, SEQ:TOK].rearrange("p (b t) -> p b t", t=DS)[:, :, DS - 1]
                step(tt_(Snew.rearrange("p (b e) -> p b e", b=DB), S0[:, h % 2, :].rearrange("p (b e) -> p b e", b=DB),
                         bc(ebl, 2, HK), ALU.mult))
                tt_(Snew, Snew, slot(key)[:, :], ALU.add).then_inc(freed(key), 1)
                evac(dve, key)
                dve.sem_inc(sem("states_done"), 1)
                for L in range(len(LEVELS)):
                    x = h * 7 + L
                    if L < 7:
                        w = TOK if LEVELS[L + 1] < DS else SEQ
                        nx = L + 1
                        dve.wait_ge(sem("level_exp"), h * 7 + nx)
                        if nx >= 3:
                            full(dve, ("A", h, nx - 2))
                        y = (h * 7 + nx) % 2
                        tt_(past(LQ[:, y, 0:w], nx), past(Q[:, 0:w], nx), past(LE[:, y, 0:w], nx),
                            ALU.mult).then_inc(sem("levels"), 1)
                        tt_(before(LK[:, y, 0:w], nx), before(K[:, 0:w], nx), before(LE[:, y, 0:w], nx),
                            ALU.mult).then_inc(sem("levels"), 1)
                    key = ("A", h, L)
                    full(dve, key)
                    if L == 0:
                        m = cst("hmask")[:, 0:P]
                        step(tt_(Aacc[0:NSMP, SEQ:TOK], slot(key)[0:NSMP, 512:512 + NSMP], m[0:NSMP, 0:NSMP],
                                 ALU.mult))
                        tt_(Aacc[:, 0:SEQ].rearrange("p (c n) -> p c n", c=QT),
                            slot(key)[:, 0:SEQ].rearrange("p (c n) -> p c n", c=QT), bc(m, 1, QT),
                            ALU.mult).then_inc(freed(key), 1)
                        evac(dve, key)
                        continue
                    m = cst("hmask")[:, P + (L - 1) * P // 2:P + L * P // 2]
                    if LEVELS[L] < DS:
                        ns = NSMP // 2
                        step(tt_(Atmp[0:NSMP, 0:ns], slot(key)[0:NSMP, 512:512 + ns], m[0:NSMP, 0:ns], ALU.mult))
                        acc = past(Aacc[0:NSMP, SEQ:TOK], L)
                        step(tt_(acc, acc, packed(Atmp[0:NSMP, 0:ns], L), ALU.add))
                    tt_(Atmp[:, 0:SEQ // 2].rearrange("p (c n) -> p c n", c=QT),
                        slot(key)[:, 0:SEQ // 2].rearrange("p (c n) -> p c n", c=QT), bc(m, 1, QT),
                        ALU.mult).then_inc(freed(key), 1)
                    evac(dve, key)
                    acc = past(Aacc[:, 0:SEQ], L)
                    step(tt_(acc, acc, packed(Atmp[:, 0:SEQ // 2], L), ALU.add))
                dve.sem_inc(sem("scores_done"), 1)
                if h:
                    mixed_lo(3 + h)
                if h + 1 < HH:
                    keys_decayed(h + 1)
                key = ("osum", h)
                inverse_rms(key, TOK, HK, Atmp)
                key = ("o", h)
                stt(MX[:, 4 + h, :], slot(key)[:, 0:TOK], GV[:, V_HG + h:V_HG + h + 1], RSTD[:, :], ALU.mult,
                    ALU.mult).then_inc(freed(key), 1)
                evac(dve, key)
                evac(dve, ("hg", h))
                tt_(MX[:, 4 + h, :], MX[:, 4 + h, :], hG[:, h, :], ALU.mult).then_inc(sem("hg_out"), 1)
            mixed_lo(3 + HH)
            dve.sem_inc(sem("dve_phase"), 1)

            def residual(name, n_norm):
                norm_of[0] = n_norm
                for m in range(KT):
                    key = (name, m)
                    full(dve, key)
                    tt_(two(X[:, m, :]), two(X[:, m, :]), halves(slot(key)), ALU.add).then_inc(freed(key), 1)
                    evac(dve, key)
                    square(m)
            dve.wait_ge(sem("store_phase"), 2)
            residual("wout", 1)

            for n in range(2):
                evac(dve, ("mT", n))
                x = mnT[:, 4 * n:4 * n + 4, :]
                tt_(mkT[:, 4 * n:4 * n + 4, :], x, x, ALU.mult).then_inc(sem("mem_squares"), 1)
            key = ("msum",)
            r = RSTD[:, 0:MEM]
            inverse_rms(key, MEM, DM, KX[:, 0, 0:MEM])
            for k in range(KT):
                stt(mnT[:, k, :], mnT[:, k, :], GV[:, V_MEM + k:V_MEM + k + 1], r, ALU.mult,
                    ALU.mult).then_inc(sem("mem_raw"), 1)
            for k in range(KT):
                dve.wait_ge(sem("mem_hi"), k + 1)
                ins = tt_(MNL[:, k, :], mnT[:, k, :], MNH[:, k, :].bitcast(F32), ALU.subtract)
            ins.then_inc(sem("mem_normed"), 1)
            normalize_split(1)

            for i in range(QT):
                key = ("cS", i)
                full(dve, key)
                x = slice(4 * (i % 2), 4 * (i % 2) + 4)
                if i >= 2:
                    dve.wait_ge(sem("cross_probs"), i - 1)
                step(v.tensor_reduce(xmx[:, x], slot(key)[:, :].rearrange("p (h n) -> p h n", h=CH), AX, ALU.max))
                ts(xnm[:, x], xmx[:, x], -CSCALE, None, ALU.mult).then_inc(sem("cross_max"), 1)
                evac(dve, key)
                step(v.reciprocal(xden[:, x], xden[:, x]))
                xp = xP[:, i % 2, :].rearrange("p (h n) -> p h n", h=CH)
                tt_(xp, xp, bc(xden[:, x], 2, MEM), ALU.mult).then_inc(sem("cross_probs"), 1)
                if i == 1:
                    dve.wait_ge(sem("cross_cleared"), 1)
                    for n in range(KT):
                        evac(dve, ("wq", n))
                        for b2 in range(2):
                            at = 16 * b2 + 4 * (n // 2)
                            step(cp(qbc[:, n, b2::2, at:at + DS],
                                    QC[:, n, SEQ:TOK].rearrange("p (b t) -> p b t", b=DB)[:, b2::2, :]))
                    dve.sem_inc(sem("cross_diag"), 1)
            dve.wait_ge(hold_full, hold[("cS",)] + 1)
            step(v.tensor_reduce(xmx[:, 0:1], HOLD[:, 0:MEM], AX, ALU.max))
            ts(msc[:, 0:1], xmx[:, 0:1], -CSCALE, None, ALU.mult).then_inc(sem("cross_smp_max"), 1)
            dve.wait_ge(hold_free, hold[("cS",)] + 1)
            step(v.reciprocal(msc[:, 1:2], msc[:, 1:2]))
            ts(yP, yP, msc[:, 1:2], None, ALU.mult).then_inc(sem("cross_smp"), 1)
            dve.wait_ge(sem("cross_smp"), 1)
            for k in range(KT):
                dve.wait_ge(sem("crossed_hi"), k + 1)
                tt_(OPL[:, k, :], MX[:, k, :], OPH[:, k, :].bitcast(F32), ALU.subtract).then_inc(sem("crossed"), 1)
            residual("wo", 2)
            dve.sem_inc(sem("dve_phase"), 1)
            dve.wait_ge(sem("act_phase"), 2)
            dve.wait_ge(sem("store_phase"), 3)
            normalize_split(2)
            for n in range(FT // 2):
                for m in range(2):
                    j = 2 * n + m
                    t = ftmp[:, m, :]
                    dve.wait_ge(sem("gate_exp"), j + 1)
                    step(ts(t, t, 1.0, None, ALU.add))
                    step(v.reciprocal(t, t))
                    key = ("ffg", j)
                    tt_(two(t), two(t), halves(slot(key)), ALU.mult).then_inc(freed(key), 1)
                    evac(dve, key)
                for m in range(2):
                    j = 2 * n + m
                    key = ("ffu", j)
                    full(dve, key)
                    if j:
                        dve.wait_ge(sem("hidden"), j)
                    tt_(two(htmp), two(ftmp[:, m, :]), halves(slot(key)), ALU.mult).then_inc(sem("hidden_raw"), 1)
                    dve.wait_ge(sem("hidden_raw"), j + 1)
                    dve.sem_inc(freed(key), 1)
                    dve.wait_ge(sem("hidden_hi"), j + 1)
                    tt_(HIDL[:, j, :], htmp, HIDH[:, j, :].bitcast(F32), ALU.subtract).then_inc(sem("hidden"), 1)
            residual("ffd", 3)
            normalize(3)

        @block.gpsimd
        def _(pool):
            g = nc.gpsimd
            g.memset(ones[:, :], 1.0).then_inc(sem("ones"), 1)
            gather_list = [k for k in raws if gathered_tile(k)]
            gathered = [0]

            def gather(count):
                for name in gather_list[gathered[0]:gathered[0] + count]:
                    n = raws[name]
                    raw_free(pool, n)
                    if name[0] == "c":
                        src, b = a["cache_cmp_" + "kv"[name[1]]], name[2]
                    else:
                        src, b = a["cache_sel_" + name[0][1]], 4 * name[1] + name[2]
                    g.indirect_dma_start(RAW[:, n % RAWS, :], None, src.rearrange(
                        "l n (r t) g d -> (l n r) (t g d)", r=PROWS), bass.IndirectOffsetOnAxis(
                            PGROW[:, b:b + 1], axis=0)).then_inc(rgather[n % RAWS], 16)
                gathered[0] += count
            pool.wait_ge(psum_full, ring[("xT", KT - 1)] + 1)
            g.memset(qbd.rearrange("p k n -> p (k n)"), 0.0).then_inc(sem("cleared"), 1)
            g.memset(qtok[:, QT, :], 0.0).then_inc(sem("cleared"), 1)
            g.memset(ksw[:, QT, :, :].rearrange("p s d -> p (s d)"), 0.0).then_inc(sem("cleared"), 1)
            pool.wait_ge(sem("pages_in"), 16 * NPAGE)
            pool.wait_ge(sem("cst_in"), 16)
            g.tensor_scalar(PGROW[:, :], PGID[:, :], float(PROWS), cst("page_row"), ALU.mult,
                            ALU.add).then_inc(sem("page_rows"), 1)
            pool.wait_ge(sem("page_rows"), 1)
            gather(RAWS)

            def flat(name):
                return out[name].rearrange("l b t g d -> (l b t) (g d)")

            def store_rows(kind, src, s):
                g.dma_start(flat("p_" + kind).rearrange("(t p) c -> p t c", p=P), src[:, 0:QT]).then_inc(s, 16)
            counts = {"kv_out": 0}

            def kv_store(kind, src):
                store_rows(kind, src, sem("kv_out"))
                counts["kv_out"] += 16
                if kind[:3] != "win":
                    g.dma_start(flat("s_" + kind), src[0:NSMP, QT]).then_inc(sem("kv_out"), 16)
                    counts["kv_out"] += 16
                else:
                    for b in range(DB):
                        at = b * WIN + WIN - DS
                        g.dma_start(flat("s_" + kind)[at:at + DS, :],
                                    src[DS * b:DS * b + DS, QT]).then_inc(sem("kv_out"), 16)
                        counts["kv_out"] += 16
            evac(pool, ("cmp", "p"))
            for n in range(2):
                store_rows("cmp_" + "kv"[n], ckcv[:, :, n * GW:(n + 1) * GW], sem("cmp_rows_out"))
            evac(pool, ("cmp", "s"))
            for n in range(2):
                g.dma_start(flat("s_cmp_" + "kv"[n]), ckcv[0:NSMP, QT, n * GW:(n + 1) * GW]).then_inc(sem("kv_out"), 16)
                counts["kv_out"] += 16
            for s, name in enumerate(("sel", "win")):
                evac(pool, (name, "p"))
                evac(pool, (name, "s"))
                kv_store(name + "_v", vtok[:, :, s, :])
            pool.wait_ge(sem("k_rotated"), 1)
            for s, name in enumerate(("sel", "win")):
                kv_store(name + "_k", ksw[:, :, s, :])
            pool.wait_ge(sem("gates_done"), 1)
            g.dma_start(scr_g, gates[0:NSMP, QT, :]).then_inc(sem("gsmp_out"), 16)
            pool.wait_ge(sem("gsmp_out"), 16)
            for b in range(DB):
                rd, q = b // 4, 32 * (b % 4)
                g.dma_start(gsmp[q:q + 32, rd, :],
                            scr_g[DS * b:DS * b + DS, :].rearrange("t (h n) -> h t n", h=NH)).then_inc(sem("gsmp_in"), 16)
            gather(8 - RAWS)
            pool.wait_ge(sem("kv_out"), counts["kv_out"])
            pool.wait_ge(sem("cmp_rows_out"), 32)
            pool.sem_inc(sem("t_stored"), 1)
            gather(8)
            pool.wait_ge(hold_full, hold[("h", 1, 2)] + 1)
            g.memset(qr0[HD:P], 0.0).then_inc(sem("q_padded"), 1)
            pool.wait_ge(sem("q0_copied"), 1)
            g.memset(qrT[0:HD, :, 0:SEQ], 0.0).then_inc(sem("q_padded"), 1)
            lo = SplitsLo(pool, g, DVE_SPLITS + 1)
            lo.upto(splits[("hi0", 1)])
            gather(12)

            def samples_out(rd):
                pool.wait_ge(sem("smp_o"), rd + 1)
                for b in range(4):
                    t0 = 16 * rd + 4 * b
                    g.dma_start(scr_o[t0:t0 + DS, :].rearrange("t (h d) -> h t d", h=NH),
                                oacc[32 * b:32 * b + 32, 512:576]).then_inc(sem("smp_o_out"), 16)
            samples_out(0)
            gather(4)
            samples_out(1)
            lo.upto(splits[("hi1", 0)])
            pool.wait_ge(sem("smp_o_out"), 16 * DB)
            g.dma_start(otok[0:NSMP, QT, :], scr_o).then_inc(sem("smp_o_in"), 16)
            pool.sem_inc(sem("store_phase"), 1)
            lo.upto(splits[("hg", 1, 1)])
            for h in range(HH):
                pool.wait_ge(sem("decay_sum"), h + 1)
                for L in range(1, len(LEVELS)):
                    x = h * 7 + L
                    n = TOK if LEVELS[L] < DS else SEQ
                    w = 2 * LEVELS[L]
                    if x > 2:
                        pool.wait_ge(sem("level_exp"), x - 2)
                    b3 = hB[:, h, 0:n].rearrange("p (k w) -> p k w", w=w)
                    d3 = LD[:, x % 2, 0:n].rearrange("p (k w) -> p k w", w=w)
                    hw = w // 2
                    ref = b3[:, :, hw - 1:hw].broadcast_to([P, n // w, hw])
                    g.tensor_tensor(d3[:, :, 0:hw], b3[:, :, 0:hw], ref, ALU.subtract).then_inc(sem("level_in"), 1)
                    g.tensor_tensor(d3[:, :, hw:w], ref, b3[:, :, hw:w], ALU.subtract).then_inc(sem("level_in"), 1)
                if h == 0:
                    lo.upto(splits[("wout", 0, 1)])
                pool.wait_ge(sem("states_done"), h + 1)
                g.dma_start(out["p_hgrn"][0, 0, h], Sst[:, QT - 1, :]).then_inc(sem("hg_stored"), 16)
                g.dma_start(out["s_hgrn"][0, :, h].rearrange("b d e -> d b e"),
                            Snew.rearrange("p (b e) -> p b e", b=DB)).then_inc(sem("hg_stored"), 16)
                for n in range(2):
                    for b in (2 * h, 2 * h + 1):
                        rows = (WIN - DS) * GW
                        src = a["cache_win_" + "kv"[n]].rearrange("l b t g d -> (l b) (t g d)")[b, DS * GW:WIN * GW]
                        dst = out["s_win_" + "kv"[n]].rearrange("l b t g d -> (l b) (t g d)")[b, 0:rows]
                        g.dma_start(dst.rearrange("(a n) -> a n", a=16),
                                    src.rearrange("(a n) -> a n", a=16)).then_inc(sem("win_out"), 16)
            pool.wait_ge(sem("hg_stored"), 32 * HH)
            pool.sem_inc(sem("store_phase"), 1)
            lo.upto(splits[("wk", 0, 1)])
            pool.wait_ge(sem("dve_phase"), 2)
            g.memset(qbc.rearrange("p k b n -> p (k b n)"), 0.0).then_inc(sem("cross_cleared"), 1)
            g.memset(yPT.rearrange("p j b n -> p (j b n)"), 0.0).then_inc(sem("cross_cleared"), 1)
            for c, name, src in (("wk", "p_mem_k", mst), ("wv", "p_mem_v", mv)):
                lo.upto(splits[(c, 3, 1)] + 2)
                for n in range(4):
                    evac(pool, (c, n))
                g.dma_start(out[name].rearrange("l b (m p) h d -> p (l b m) (h d)", p=P), src).then_inc(sem("mem_out"), 16)
            lo.upto(splits[("wo", 0, 1)])
            pool.wait_ge(sem("mem_out"), 32)
            pool.sem_inc(sem("store_phase"), 1)
            lo.upto(len(splits) - 1)
            pool.wait_ge(sem("win_out"), 16 * 2 * DB)

        @block.sync
        def _(sp):
            def cols(name, at, n):
                return a[name][0, :, at:at + n].rearrange("(k p) n -> p k n", p=P)

            src = {("cmp",): cols("w_in", C_CK, 256), ("sel",): cols("w_in", C_SK, 256),
                   ("win",): cols("w_in", C_WK, 256), ("gate",): cols("w_in", C_G, 24)}
            for n in range(2):
                src[(f"q{n}",)] = cols("w_in", C_Q + 256 * n, 256)
                src[(f"hi{n}",)] = cols("w_in", C_HI + 256 * n, 256)
                src[("w1", n)] = a["cmp_w1_" + "kv"[n]][0].rearrange("(k p) n -> p k n", p=P)
                for c, at in (("hf", C_HF), ("hq", C_HQ), ("hg", C_HG)):
                    src[(c, n)] = cols("w_in", at + 256 * n, 256)
            for n in range(4):
                for c, name in (("wout", "w_out"), ("wk", "ca_wk"), ("wv", "ca_wv"), ("wq", "ca_wq"), ("wo", "ca_wo")):
                    src[(c, n)] = cols(name, 256 * n, 256)
                for k in range(3):
                    r1 = min(1024 * (k + 1), FFN)
                    src[("ffd", n, k)] = a["ffn_w_down"][0, 1024 * k:r1, 256 * n:256 * n + 256].rearrange(
                        "(k p) n -> p k n", p=P)
            for n in range(FT // 2):
                src[("ffg", n)] = cols("ffn_w_gate", 256 * n, 256)
                src[("ffu", n)] = cols("ffn_w_up", 256 * n, 256)
            order = list(chunks)

            def weights(name):
                n = chunks[name]
                if n >= WRING:
                    before_ = order[n - WRING]
                    if before_ in chunk_last:
                        sp.wait_ge(psum_full, chunk_last[before_] + 1)
                    else:
                        sp.wait_ge(sem("weights_lo"), max(x for name_, x in splits.items() if name_[:-1] == before_) + 1)
                s = src[name]
                kk, w = s.shape[1], s.shape[2]
                dst, loaded, _ = wsl(name)
                sp.dma_start(dst[:, 0:kk * w].rearrange("p (k n) -> p k n", k=kk), s).then_inc(loaded, 16)

            def raw_tile(name):
                n = raws[name]
                slot_, s = RAW[:, n % RAWS, :], rload[n % RAWS]
                kind = name[0]
                if kind == "c" and name[2] == 8:
                    raw_free(sp, n)
                    sp.wait_ge(sem("cmp_rows_out"), 32)
                    sp.dma_start(slot_[0:SEQ // 8, :], out["p_cmp_" + "kv"[name[1]]].rearrange(
                        "l b (p t) g d -> (l b p) (t g d)", t=8)).then_inc(s, 16)
                elif kind in ("wk", "wv"):
                    raw_free(sp, n)
                    b = 4 * name[1] + name[2]
                    sp.dma_start(slot_[:, 0:512], a["cache_win_" + kind[1]][0, b].rearrange(
                        "(p t) g d -> p (t g d)", t=4)).then_inc(s, 16)

            sp.dma_start(XST[:, 0:QT, :], a["x_prompt"][0].rearrange("(t p) n -> p t n", p=P)).then_inc(sem("x_in"), 16)
            sp.dma_start(XST[0:NSMP, QT, :], a["x_sample"].rearrange("b t n -> (b t) n")).then_inc(sem("x_in"), 16)
            sp.dma_start(CST[:, :], a["tables"]).then_inc(sem("cst_in"), 16)
            for name, at, rows in (("norm_mix", V_MIX, 8), ("norm_ca", V_CA, 8), ("norm_mem", V_MEM, 8),
                                   ("norm_ffn", V_FFN, 8), ("nsa_out_norm", V_NSA, 4), ("hg_out_norm", V_HG, 4)):
                sp.dma_start(VECS[at:at + rows, :], a[name][0].rearrange("(k p) -> k p", p=P)).then_inc(sem("vec_in"), 16)
            sp.dma_start(VECS[V_FIN:V_FIN + 8, :], a["final_norm"].rearrange("(k p) -> k p", p=P)).then_inc(sem("vec_in"), 16)
            sp.dma_start(VECS[V_LB:V_LB + 8, :], a["hg_lb_logits"].rearrange("l (k p) -> (l k) p", p=P)).then_inc(
                sem("vec_in"), 16)
            for n in range(2):
                sp.dma_start(VECS[V_PEK + 16 * n:V_PEK + 16 * n + 16, :], a["cmp_pe_" + "kv"[n]][0].rearrange(
                    "(k t) d -> k (t d)", t=2)).then_inc(sem("vec_in"), 16)
                sp.dma_start(w2[:, n, :], a["cmp_w2_" + "kv"[n]][0]).then_inc(sem("w2_in"), 16)
            for c in order[0:2]:
                weights(c)
            for n in range(NPAGE):
                sp.dma_start(PGID[n * PROWS:(n + 1) * PROWS, :],
                             bc(a["page_table"][:, n], 0, PROWS),
                             allow_slow_non_contiguous=True).then_inc(sem("pages_in"), 16)
            for c in order[2:8]:
                weights(c)
            raw_tile(("c", 0, 8))
            weights(("hi0",))
            raw_tile(("c", 1, 8))
            weights(("hi1",))
            weights(("hf", 0))
            for name in raws:
                if name[0] != "c":
                    raw_tile(name)

            def state(h):
                if h >= 2:
                    full(sp, ("o", h - 2))
                    sp.wait_ge(sem("states_done"), h - 1)
                sp.dma_start(S0[:, h % 2, :].rearrange("p (b e) -> p b e", b=DB),
                             a["state_hgrn"][0, :, h].rearrange("b d e -> d b e")).then_inc(sload[h % 2], 16)
            sp.wait_ge(hold_full, hold[("PV", 1)] + 1)
            for e in ("act_phase", "dve_phase", "store_phase"):
                sp.wait_ge(sem(e), 1)
            state(0)
            state(1)
            out_at = chunks[("wout", 0)]
            for c in order[chunks[("hf", 1)]:out_at + 2]:
                weights(c)
            state(2)
            state(3)
            for e in ("dve_phase", "store_phase"):
                sp.wait_ge(sem(e), 2)
            sp.dma_start(mst, a["mem_prompt"][0].rearrange("(m p) n -> p m n", p=P)).then_inc(sem("mem_in"), 16)

            def cross(x):
                if 3 <= x < DB + 3:
                    full(sp, ("cx", x - 3, 1))
                elif x >= DB + 3:
                    sp.wait_ge(sem("cross_values_used"), x - 3 - DB + 1)
                src_ = a["cache_mem_" + ("k" if x < DB else "v")][0, x % DB]
                sp.dma_start(RC[:, x % 3, :], src_.rearrange("(p j) h d -> p (j h d)", j=2)).then_inc(cload[x % 3], 16)
            for x in range(3):
                cross(x)
            cross_at = chunks[("wo", 0)]
            for c in order[out_at + 2:cross_at + 2]:
                weights(c)
            for x in range(3, 2 * DB):
                cross(x)
            for c in order[cross_at + 2:]:
                weights(c)
            for tt in range(QT + 1):
                evac(sp, ("y", tt))
                if tt < QT:
                    dst, n = out["y_prompt"][0, tt * P:(tt + 1) * P, :], P
                else:
                    dst, n = out["y_sample"].rearrange("b t n -> (b t) n"), NSMP
                sp.dma_start(dst, ymid[0:n, tt % 2, :]).then_inc(sem(f"y_out{tt % 2}"), 16)
            sp.wait_ge(sem("y_out0"), 48)
            sp.wait_ge(sem("y_out1"), 32)


_OUTS = [("y_prompt", (1, SEQ, DM)), ("y_sample", (DB, DS, DM))]
_OUTS += [(f"p_{k}_{x}", (1, 1, SEQ, NG, HD)) for k in ("cmp", "sel", "win") for x in "kv"]
_OUTS += [("p_hgrn", (1, 1, HH, HK, HK)), ("p_mem_k", (1, 1, MEM, CH, CD)), ("p_mem_v", (1, 1, MEM, CH, CD))]
_OUTS += [(f"s_{k}_{x}", (1, DB, DS, NG, HD)) for k in ("cmp", "sel") for x in "kv"]
_OUTS += [(f"s_win_{x}", (1, DB, WIN, NG, HD)) for x in "kv"]
_OUTS += [("s_hgrn", (1, DB, HH, HK, HK))]


def kernel(**inputs):
    import concourse.bacc as bacc
    from concourse.bass_utils import run_bass_kernel_spmd

    nc = bacc.Bacc("TRN2", target_bir_lowering=False, num_devices=1)
    arrays, a, out = {}, {}, {}
    cat, tables = constants()
    for name, x in list(inputs.items()) + [("tables", tables)]:
        x = np.ascontiguousarray(x)
        arrays[f"in_{name}"] = x
        a[name] = nc.dram_tensor(f"in_{name}", x.shape, mybir.dt.from_np(x.dtype), kind="ExternalInput").ap()
    for name, shape in _OUTS:
        out[name] = nc.dram_tensor(f"out_{name}", shape, F32, kind="ExternalOutput").ap()
    build(nc, a, out, cat)
    r = run_bass_kernel_spmd(nc, [arrays], core_ids=[0])
    return tuple(r.results[0][f"out_{name}"] for name, _ in _OUTS)
```
